# Optimizing a Trainium2 kernel written in Bass

```python
import jax
import jax.numpy as jnp
from jax import lax
import numpy as np

D_MODEL = 1024
BATCH = 1
SEQ = 1024
DEPTH = 1

CHUNK = 64
NORM_EPS = 1e-6
ROPE_THETA = 500000.0

HEAD_DIM = 64
ATT_HEADS = (D_MODEL // 2) // HEAD_DIM
ATT_KV_HEADS = ATT_HEADS // 4
Q_PER_KV = ATT_HEADS // ATT_KV_HEADS
ATT_ROT_DIM = HEAD_DIM // 4
IDX_HEADS = 8
IDX_DIM = 32
IDX_ROT_DIM = IDX_DIM // 4
TOPK_MAX = 256
Q_BLOCK = 128
ATT_WIDTH = ATT_HEADS * HEAD_DIM

MLSTM_HEAD_DIM = 128
MLSTM_HEADS = (D_MODEL // 2) // MLSTM_HEAD_DIM
MLSTM_WIDTH = MLSTM_HEADS * MLSTM_HEAD_DIM
CONV_WIDTH = 4

MIX_WIDTH = ATT_WIDTH + MLSTM_WIDTH

PROJ_SIZES = (
    ATT_WIDTH,
    ATT_KV_HEADS * HEAD_DIM,
    ATT_KV_HEADS * HEAD_DIM,
    IDX_HEADS * IDX_DIM,
    IDX_DIM,
    IDX_HEADS,
    MLSTM_WIDTH,
    MLSTM_WIDTH,
    MLSTM_WIDTH,
    MLSTM_HEADS,
    MLSTM_HEADS,
    MLSTM_WIDTH,
)
PROJ_WIDTH = sum(PROJ_SIZES)

N_EXPERTS = 32
TOP_K = 4
EXPERT_DIM = D_MODEL
SWIGLU_ALPHA = 1.702
SWIGLU_LIMIT = 7.0
EXPERT_BLOCK = 128

kernel_name = 'hybrid_dsa_mlstm_moe_block'

def rms_norm(x, w):
    xf = x.astype(jnp.float32)
    y = xf * lax.rsqrt(jnp.mean(xf * xf, axis=-1, keepdims=True) + NORM_EPS)
    return (y * w.astype(jnp.float32)).astype(x.dtype)

def partial_rope(x, rot_dim):
    seq = x.shape[1]
    pos = jnp.arange(seq, dtype=jnp.float32)
    inv_freq = ROPE_THETA ** (-jnp.arange(0, rot_dim, 2, dtype=jnp.float32) / rot_dim)
    ang = pos[:, None] * inv_freq[None, :]
    cos = jnp.cos(ang)[None, :, None, :]
    sin = jnp.sin(ang)[None, :, None, :]
    xr = x[..., :rot_dim].astype(jnp.float32)
    x1, x2 = jnp.split(xr, 2, axis=-1)
    rot = jnp.concatenate([x1 * cos - x2 * sin, x2 * cos + x1 * sin], axis=-1)
    return jnp.concatenate([rot.astype(x.dtype), x[..., rot_dim:]], axis=-1)

def dsa_attention(q, k, v, qi, ki, wi):
    bsz, seq = q.shape[0], q.shape[1]
    k_sel = min(TOPK_MAX, seq // 4)
    n_blk = seq // Q_BLOCK
    key_chunk = jnp.arange(seq) // CHUNK
    qg = q.reshape(bsz, seq, ATT_KV_HEADS, Q_PER_KV, HEAD_DIM)
    scale = HEAD_DIM ** -0.5

    def block(i):
        s0 = i * Q_BLOCK
        qb = lax.dynamic_slice_in_dim(qg, s0, Q_BLOCK, axis=1)
        qib = lax.dynamic_slice_in_dim(qi, s0, Q_BLOCK, axis=1)
        wib = lax.dynamic_slice_in_dim(wi, s0, Q_BLOCK, axis=1)
        q_chunk = (s0 + jnp.arange(Q_BLOCK)) // CHUNK
        admissible = key_chunk[None, :] <= q_chunk[:, None]
        idx_score = jnp.einsum('bqh,bqhs->bqs', wib,
                               jax.nn.relu(jnp.einsum('bqhd,bsd->bqhs', qib, ki)))
        idx_score = jnp.where(admissible[None], idx_score.astype(jnp.float32), -jnp.inf)
        _, sel = lax.top_k(idx_score, k_sel)
        valid = key_chunk[sel] <= q_chunk[None, :, None]
        ks = jax.vmap(lambda kb, ib: kb[ib])(k, sel)
        vs = jax.vmap(lambda vb, ib: vb[ib])(v, sel)
        logits = jnp.einsum('bqgrd,bqkgd->bqgrk', qb, ks).astype(jnp.float32) * scale
        logits = jnp.where(valid[:, :, None, None, :], logits, -jnp.inf)
        p = jax.nn.softmax(logits, axis=-1).astype(v.dtype)
        return jnp.einsum('bqgrk,bqkgd->bqgrd', p, vs)

    out = lax.map(block, jnp.arange(n_blk))
    return out.transpose(1, 0, 2, 3, 4, 5).reshape(bsz, seq, ATT_WIDTH)

def causal_depthwise_conv(x, w, b):
    c = x.shape[-1]
    y = lax.conv_general_dilated(x, w.reshape(CONV_WIDTH, 1, c), window_strides=(1,),
                                 padding=[(CONV_WIDTH - 1, 0)],
                                 dimension_numbers=('NWC', 'WIO', 'NWC'),
                                 feature_group_count=c)
    return y + b

def mlstm_chunkwise(q, k, v, i_pre, log_f):
    bsz, nh, seq, dh = q.shape
    nc = seq // CHUNK

    def to_chunks(t):
        t = t.reshape(t.shape[:2] + (nc, CHUNK) + t.shape[3:])
        return jnp.moveaxis(t, 2, 0)

    qc, kc, vc, ic, fc = (to_chunks(t) for t in (q, k * dh ** -0.5, v, i_pre, log_f))
    causal = jnp.tril(jnp.ones((CHUNK, CHUNK), dtype=bool))

    def step(carry, inp):
        c_mat, n_vec, m_prev = carry
        qb, kb, vb, ib, fb = inp
        b = jnp.cumsum(fb, axis=-1)
        d_log = jnp.where(causal, b[..., :, None] - b[..., None, :] + ib[..., None, :], -jnp.inf)
        inter_log = b + m_prev[..., None]
        m_t = jnp.maximum(inter_log, jnp.max(d_log, axis=-1))
        d_w = jnp.exp(d_log - m_t[..., None])
        inter_w = jnp.exp(inter_log - m_t)
        s = jnp.einsum('bhtd,bhsd->bhts', qb, kb) * d_w
        num = (jnp.einsum('bhts,bhse->bhte', s, vb)
               + inter_w[..., None] * jnp.einsum('bhtd,bhde->bhte', qb, c_mat))
        den = jnp.sum(s, axis=-1) + inter_w * jnp.einsum('bhtd,bhd->bht', qb, n_vec)
        h = num / jnp.maximum(jnp.abs(den), jnp.exp(-m_t))[..., None]
        b_last = b[..., -1]
        w_log = b_last[..., None] - b + ib
        m_new = jnp.maximum(b_last + m_prev, jnp.max(w_log, axis=-1))
        decay = jnp.exp(b_last + m_prev - m_new)
        w_s = jnp.exp(w_log - m_new[..., None])
        c_new = decay[..., None, None] * c_mat + jnp.einsum('bhsd,bhse->bhde', kb * w_s[..., None], vb)
        n_new = decay[..., None] * n_vec + jnp.einsum('bhs,bhsd->bhd', w_s, kb)
        return (c_new, n_new, m_new), h

    init = (jnp.zeros((bsz, nh, dh, dh), jnp.float32),
            jnp.zeros((bsz, nh, dh), jnp.float32),
            jnp.zeros((bsz, nh), jnp.float32))
    _, hs = lax.scan(step, init, (qc, kc, vc, ic, fc))
    return jnp.moveaxis(hs, 0, 2).reshape(bsz, nh, seq, dh)

def mlstm_mixer(mq, mk, mv, mi, mf, mo, conv_w, conv_b, igate_b, fgate_b, norm_w):
    bsz, seq = mq.shape[0], mq.shape[1]
    qk = jax.nn.silu(causal_depthwise_conv(jnp.concatenate([mq, mk], axis=-1), conv_w, conv_b))
    q, k = jnp.split(qk, 2, axis=-1)

    def heads(t):
        return t.reshape(bsz, seq, MLSTM_HEADS, MLSTM_HEAD_DIM).transpose(0, 2, 1, 3).astype(jnp.float32)

    i_pre = (mi + igate_b).astype(jnp.float32).transpose(0, 2, 1)
    log_f = jax.nn.log_sigmoid((mf + fgate_b).astype(jnp.float32)).transpose(0, 2, 1)
    h = mlstm_chunkwise(heads(q), heads(k), heads(mv), i_pre, log_f)
    h = h * lax.rsqrt(jnp.mean(h * h, axis=-1, keepdims=True) + NORM_EPS)
    h = h.transpose(0, 2, 1, 3).reshape(bsz, seq, MLSTM_WIDTH) * norm_w.astype(jnp.float32)
    return (h * jax.nn.sigmoid(mo.astype(jnp.float32))).astype(mq.dtype)

def moe_ffn(h, router_w, router_b, w_gu, b_gu, w_dn, b_dn):
    bsz, seq, d = h.shape
    t = bsz * seq
    xf = h.reshape(t, d)
    logits = (xf @ router_w + router_b).astype(jnp.float32)
    top_vals, top_idx = lax.top_k(logits, TOP_K)
    gates = jax.nn.softmax(top_vals, axis=-1).astype(h.dtype)
    a = t * TOP_K
    e_flat = top_idx.reshape(a)
    tok_flat = jnp.repeat(jnp.arange(t), TOP_K)
    g_flat = gates.reshape(a)
    order = jnp.argsort(e_flat)
    e_sorted, tok_sorted, g_sorted = e_flat[order], tok_flat[order], g_flat[order]
    counts = jnp.bincount(e_flat, length=N_EXPERTS)
    start = jnp.cumsum(counts) - counts
    padded = (counts + EXPERT_BLOCK - 1) // EXPERT_BLOCK * EXPERT_BLOCK
    pad_end = jnp.cumsum(padded)
    pad_start = pad_end - padded
    dest = pad_start[e_sorted] + (jnp.arange(a) - start[e_sorted])
    n_rows = -(-a // EXPERT_BLOCK) * EXPERT_BLOCK + N_EXPERTS * EXPERT_BLOCK
    n_blocks = n_rows // EXPERT_BLOCK
    x_buf = jnp.zeros((n_rows, d), h.dtype).at[dest].set(xf[tok_sorted])
    blk_expert = jnp.minimum(
        jnp.searchsorted(pad_end, jnp.arange(n_blocks) * EXPERT_BLOCK, side='right'), N_EXPERTS - 1)

    def expert_block(args):
        xb, e = args
        gu = xb @ w_gu[e] + b_gu[e]
        glu = jnp.minimum(gu[:, :EXPERT_DIM], SWIGLU_LIMIT)
        lin = jnp.clip(gu[:, EXPERT_DIM:], -SWIGLU_LIMIT, SWIGLU_LIMIT)
        act = glu * jax.nn.sigmoid(SWIGLU_ALPHA * glu) * (lin + 1.0)
        return act @ w_dn[e] + b_dn[e]

    y_buf = lax.map(expert_block, (x_buf.reshape(n_blocks, EXPERT_BLOCK, d), blk_expert))
    y = y_buf.reshape(n_rows, d)[dest] * g_sorted[:, None]
    return jax.ops.segment_sum(y, tok_sorted, num_segments=t).reshape(bsz, seq, d)

def setup_inputs(seed: int = 0) -> dict:
    key = jax.random.key(seed)
    ks = jax.random.split(key, 20)

    def nrm(k, shape, scale):
        return jax.random.normal(k, shape, jnp.float32) * scale

    return {
        'x': nrm(ks[0], (BATCH, SEQ, D_MODEL), 1.0),
        'mix_norm_w': 1.0 + nrm(ks[1], (DEPTH, D_MODEL), 0.02),
        'w_in': nrm(ks[2], (DEPTH, D_MODEL, PROJ_WIDTH), D_MODEL ** -0.5),
        'conv_w': nrm(ks[3], (DEPTH, CONV_WIDTH, 2 * MLSTM_WIDTH), CONV_WIDTH ** -0.5),
        'conv_b': nrm(ks[4], (DEPTH, 2 * MLSTM_WIDTH), 0.02),
        'igate_b': nrm(ks[5], (DEPTH, MLSTM_HEADS), 0.1),
        'fgate_b': 3.0 + nrm(ks[6], (DEPTH, MLSTM_HEADS), 0.5),
        'mlstm_norm_w': 1.0 + nrm(ks[7], (DEPTH, MLSTM_WIDTH), 0.02),
        'w_out': nrm(ks[8], (DEPTH, MIX_WIDTH, D_MODEL), MIX_WIDTH ** -0.5),
        'ffn_norm_w': 1.0 + nrm(ks[9], (DEPTH, D_MODEL), 0.02),
        'router_w': nrm(ks[10], (DEPTH, D_MODEL, N_EXPERTS), D_MODEL ** -0.5),
        'router_b': nrm(ks[11], (DEPTH, N_EXPERTS), 0.01),
        'w_gate_up': nrm(ks[12], (DEPTH, N_EXPERTS, D_MODEL, 2 * EXPERT_DIM), D_MODEL ** -0.5),
        'b_gate_up': nrm(ks[13], (DEPTH, N_EXPERTS, 2 * EXPERT_DIM), 0.02),
        'w_down': nrm(ks[14], (DEPTH, N_EXPERTS, EXPERT_DIM, D_MODEL), EXPERT_DIM ** -0.5),
        'b_down': nrm(ks[15], (DEPTH, N_EXPERTS, D_MODEL), 0.02),
        'final_norm_w': 1.0 + nrm(ks[16], (D_MODEL,), 0.02),
    }

def reference(x, mix_norm_w, w_in, conv_w, conv_b, igate_b, fgate_b, mlstm_norm_w, w_out,
              ffn_norm_w, router_w, router_b, w_gate_up, b_gate_up, w_down, b_down, final_norm_w):
    bsz, seq = x.shape[0], x.shape[1]
    split_points = [int(p) for p in np.cumsum(PROJ_SIZES)[:-1]]
    idx_w_scale = (IDX_HEADS ** -0.5) * (IDX_DIM ** -0.5)
    for layer in range(DEPTH):
        h = rms_norm(x, mix_norm_w[layer])
        proj = h @ w_in[layer]
        aq, ak, av, iq, ik, iw, mq, mk, mv, mi, mf, mo = jnp.split(proj, split_points, axis=-1)
        aq = partial_rope(aq.reshape(bsz, seq, ATT_HEADS, HEAD_DIM), ATT_ROT_DIM)
        ak = partial_rope(ak.reshape(bsz, seq, ATT_KV_HEADS, HEAD_DIM), ATT_ROT_DIM)
        av = av.reshape(bsz, seq, ATT_KV_HEADS, HEAD_DIM)
        iq = partial_rope(iq.reshape(bsz, seq, IDX_HEADS, IDX_DIM), IDX_ROT_DIM)
        ik = partial_rope(ik.reshape(bsz, seq, 1, IDX_DIM), IDX_ROT_DIM)[:, :, 0, :]
        att_out = dsa_attention(aq, ak, av, iq, ik, iw * idx_w_scale)
        mem_out = mlstm_mixer(mq, mk, mv, mi, mf, mo, conv_w[layer], conv_b[layer],
                              igate_b[layer], fgate_b[layer], mlstm_norm_w[layer])
        x = x + jnp.concatenate([att_out, mem_out], axis=-1) @ w_out[layer]
        x = x + moe_ffn(rms_norm(x, ffn_norm_w[layer]), router_w[layer], router_b[layer],
                        w_gate_up[layer], b_gate_up[layer], w_down[layer], b_down[layer])
    return rms_norm(x, final_norm_w)


_drawn_inputs = setup_inputs


def setup_inputs(seed=0):
    import zlib

    import numpy as np

    out = dict(_drawn_inputs(seed))
    spreads = {}
    factors = {'igate_b': 8.0, 'b_gate_up': 5.338, 'b_down': 6.181, 'final_norm_w': 2.856}
    for name, (base, spread) in spreads.items():
        noise = np.random.default_rng([zlib.crc32(name.encode()), seed]).standard_normal(out[name].shape)
        drawn = base * np.exp(spread * noise) if base else spread * noise
        out[name] = jnp.asarray(drawn.astype(out[name].dtype))
    for name, factor in factors.items():
        out[name] = (out[name] * factor).astype(out[name].dtype)
    return out
```

```python
from contextlib import ExitStack

import numpy as np

import concourse.bass as bass
from concourse import mybir

F32 = mybir.dt.float32
F32R = mybir.dt.float32r
I32 = mybir.dt.int32
U32 = mybir.dt.uint32
ALU = mybir.AluOpType
ACT = mybir.ActivationFunctionType
AX = mybir.AxisListType

P = 128
T = 1024
D = 1024
NT = T // P
KC = D // P
EPS = 1e-6
CHUNK = 64

HEADS, HD, KVH = 8, 64, 2
IH, ID = 8, 32
TOPK = 256
MH, MD = 4, 128
CONV = 4
E, TOP = 32, 4
FE = 1024
ALPHA, LIMIT = 1.702, 7.0

C_AQ, C_AK, C_AV, C_IQ, C_IK, C_IW = 0, 512, 640, 768, 1024, 1056
C_MQ, C_MK, C_MV, C_MI, C_MF, C_MO = 1064, 1576, 2088, 2600, 2604, 2608

NEG = -1.0e30
GONE = -3.0e38

HALF = 72
ROWS = 2 * HALF
NBMAX = E + (T * TOP - E) // ROWS + 1
TOKW = HALF
assert P * TOKW >= (NBMAX + 1) * ROWS
PIECES = 12
KDVE = 4
CAPT = -(-T // ROWS)

FT_IQ, FT_IK, FT_SMALL, FT_Q, FT_K, FT_V, FT_MQK, FT_MV, FT_MO, NFT = 0, 2, 3, 4, 8, 9, 10, 18, 22, 26


def feature_tiles():
    tiles = [[(0, C_IQ, P)], [(0, C_IQ + P, P)]]
    tiles += [[(ID * r, C_IK, ID) for r in range(4)]]
    tiles += [[(0, C_MI, MH), (32, C_MF, MH), (64, C_IW, IH)]]
    tiles += [[(0, C_AQ + HD * j, HD), (HD, C_AQ + HD * (j + 4), HD)] for j in range(4)]
    tiles += [[(0, C_AK, P)], [(0, C_AV, P)]]
    tiles += [[(0, C_MQ + P * j, P)] for j in range(4)] + [[(0, C_MK + P * j, P)] for j in range(4)]
    tiles += [[(0, C_MV + P * j, P)] for j in range(4)] + [[(0, C_MO + P * j, P)] for j in range(4)]
    return tiles


CONST = {}


def constants():
    parts, at = [], 0

    def put(name, a):
        nonlocal at
        full = np.zeros((P, a.shape[1]), np.float32)
        full[: a.shape[0]] = a
        CONST[name] = (at, a.shape[0], a.shape[1])
        parts.append(full)
        at += a.shape[1]

    i = np.arange(P)
    put("ident", np.eye(P, dtype=np.float32))
    put("ones", np.ones((P, P), np.float32))
    put("before", (i[:, None] < i[None, :]).astype(np.float32))
    put("future", np.where(i[:, None] <= i[None, :], 0.0, NEG).astype(np.float32))
    put("seen", np.zeros((P, P), np.float32))
    put("unseen", np.where(i[None, :] // CHUNK <= i[:, None] // CHUNK, 0.0, NEG).astype(np.float32))

    def swap(period, half):
        m = np.zeros((P, P), np.float32)
        for base in range(0, P, period):
            for a in range(half):
                m[base + a + half, base + a] = -1.0
                m[base + a, base + a + half] = 1.0
        return m

    put("swap_q", swap(HD, HD // 8))
    put("swap_i", swap(ID, ID // 8))
    sel = np.zeros((MH, MH * P), np.float32)
    for h in range(MH):
        sel[h, h * P:(h + 1) * P] = 1.0
    put("pick", sel)
    put("experts", np.tile(np.arange(E, dtype=np.float32), (P, 1)))
    put("row", i[:, None].astype(np.float32))
    put("steps", np.tile(np.arange(CAPT, dtype=np.float32) * ROWS, (P, 1)))
    carry = np.ones((MH, T), np.float32)
    carry[:, ::P] = 0.0
    return np.concatenate(parts, 1), carry


def rope_tables(period, rot):
    pos = np.arange(T, dtype=np.float32)
    freq = (np.float32(500000.0) ** (-np.arange(0, rot, 2, dtype=np.float32) / np.float32(rot))).astype(np.float32)
    ang = pos[:, None] * freq[None, :]
    c, s = np.ones((P, T), np.float32), np.zeros((P, T), np.float32)
    for base in range(0, P, period):
        for a in range(rot):
            c[base + a] = np.cos(ang[:, a % (rot // 2)])
            s[base + a] = np.sin(ang[:, a % (rot // 2)])
    return np.stack([c, s], 1)


def unused_slots():
    q = np.arange(P * TOKW) % ROWS
    return (T * TOP + q).astype(np.int32).reshape(P, TOKW)


CONST_ARRAY, CARRY = constants()
CW = CONST_ARRAY.shape[1]


COLS = 1152
DEST_STEPS = 28


class Steps:

    def __init__(self, eng, sem):
        self.eng, self.sem, self.n = eng, sem, 0

    def __call__(self, ins):
        ins.then_inc(self.sem, 1)
        self.n += 1
        return self.n

    def done(self, back=0):
        if self.n > back:
            self.eng.wait_ge(self.sem, self.n - back)


class Semaphores:

    def __init__(self, sem):
        self.ld_const = sem("ld_const")
        self.ld_x0 = sem("ld_x0")
        self.ld_x1 = sem("ld_x1")
        self.ld_wn = sem("ld_wn")
        self.ld_w0 = sem("ld_w0")
        self.ld_w1 = sem("ld_w1")
        self.ld_gate = sem("ld_gate")
        self.ld_rope = sem("ld_rope")
        self.ld_small = sem("ld_small")
        self.ld_ropeq = sem("ld_ropeq")
        self.a_square = sem("a_square")
        self.a_root = sem("a_root")
        self.a_hthi = sem("a_hthi")
        self.v_rcp = sem("v_rcp")
        self.v_xn = sem("v_xn")
        self.v_htlo = sem("v_htlo")
        self.p_ht = sem("p_ht")
        self.a_whi = sem("a_whi")
        self.g_wlo = sem("g_wlo")
        self.p_ft = sem("p_ft")
        self.a_ev = sem("a_ev")
        self.g_pad = sem("g_pad")
        self.p_ri = sem("p_ri")
        self.v_rm = sem("v_rm")
        self.v_rc = sem("v_rc")
        self.v_ra = sem("v_ra")
        self.a_gate = sem("a_gate")
        self.v_gate = sem("v_gate")
        self.g_stack = sem("g_stack")
        self.p_iwt = sem("p_iwt")
        self.a_iwt = sem("a_iwt")
        self.p_is = sem("p_is")
        self.a_relu = sem("a_relu")
        self.v_score = sem("v_score")
        self.v_topk = sem("v_topk")
        self.v_mask = sem("v_mask")
        self.p_mcol = sem("p_mcol")
        self.v_mcol = sem("v_mcol")
        self.a_mexp = sem("a_mexp")
        self.p_decay = sem("p_decay")
        self.a_decay = sem("a_decay")
        self.p_rq = sem("p_rq")
        self.a_rq = sem("a_rq")
        self.g_rq = sem("g_rq")
        self.p_vt = sem("p_vt")
        self.a_vt = sem("a_vt")
        self.st_mo0 = sem("st_mo0")
        self.st_mo1 = sem("st_mo1")
        self.g_ones = sem("g_ones")
        self.g_conv = sem("g_conv")
        self.a_silu = sem("a_silu")
        self.ld_mo0 = sem("ld_mo0")
        self.ld_mo1 = sem("ld_mo1")
        self.p_m1 = sem("p_m1")
        self.a_m1 = sem("a_m1")
        self.g_m1 = sem("g_m1")
        self.p_m2 = sem("p_m2")
        self.a_m2 = sem("a_m2")
        self.g_m2 = sem("g_m2")
        self.a_sq = sem("a_sq")
        self.g_rms = sem("g_rms")
        self.a_hn = sem("a_hn")
        self.p_m3 = sem("p_m3")
        self.a_m3 = sem("a_m3")
        self.g_mix = sem("g_mix")
        self.p_s = sem("p_s")
        self.v_msk = sem("v_msk")
        self.v_nm = sem("v_nm")
        self.a_exp = sem("a_exp")
        self.p_pt = sem("p_pt")
        self.a_pt = sem("a_pt")
        self.p_pv = sem("p_pv")
        self.v_rs = sem("v_rs")
        self.v_arow = sem("v_arow")
        self.p_at = sem("p_at")
        self.a_at = sem("a_at")
        self.ld_wo0 = sem("ld_wo0")
        self.ld_wo1 = sem("ld_wo1")
        self.a_wohi = sem("a_wohi")
        self.g_wolo = sem("g_wolo")
        self.a_mxhi = sem("a_mxhi")
        self.v_mxlo = sem("v_mxlo")
        self.p_out = sem("p_out")
        self.ld_r0 = sem("ld_r0")
        self.ld_r1 = sem("ld_r1")
        self.v_x2 = sem("v_x2")
        self.st_x0 = sem("st_x0")
        self.st_x1 = sem("st_x1")
        self.a_sq2 = sem("a_sq2")
        self.a_root2 = sem("a_root2")
        self.v_rcp2 = sem("v_rcp2")
        self.v_h2 = sem("v_h2")
        self.st_h0 = sem("st_h0")
        self.st_h1 = sem("st_h1")
        self.p_h2t = sem("p_h2t")
        self.a_h2t = sem("a_h2t")
        self.p_lg = sem("p_lg")
        self.v_lg = sem("v_lg")
        self.ld_rw = sem("ld_rw")
        self.ld_wn2 = sem("ld_wn2")
        self.v_route = sem("v_route")
        self.a_gexp = sem("a_gexp")
        self.p_rank = sem("p_rank")
        self.v_dest = sem("v_dest")
        self.ld_scur = sem("ld_scur")
        self.st_zero = sem("st_zero")
        self.g_tok = sem("g_tok")
        self.st_tok = sem("st_tok")
        self.st_be = sem("st_be")
        self.passed = sem("passed")
        self.ld_idx = sem("ld_idx")
        self.ld_b = sem("ld_b")
        self.ld_g0 = sem("ld_g0")
        self.ld_g1 = sem("ld_g1")
        self.ld_g2 = sem("ld_g2")
        self.e_hi = sem("e_hi")
        self.e_lo = sem("e_lo")
        self.e_lop = sem("e_lop")
        self.p_pc = sem("p_pc")
        self.e_ev = sem("e_ev")
        self.e_mn = sem("e_mn")
        self.e_cl = sem("e_cl")
        self.e_yd = sem("e_yd")
        self.e_t = sem("e_t")
        self.e_sg = sem("e_sg")
        self.e_act = sem("e_act")
        self.e_ah = sem("e_ah")
        self.e_al = sem("e_al")
        self.e_y = sem("e_y")
        self.p_xt = sem("p_xt")
        self.e_xh = sem("e_xh")
        self.e_xl = sem("e_xl")
        self.e_bg = sem("e_bg")
        self.e_bd = sem("e_bd")
        self.p_yt = sem("p_yt")
        self.e_yr = sem("e_yr")
        self.st_y = sem("st_y")
        self.ld_xg = sem("ld_xg")
        self.st_hx = sem("st_hx")
        self.e_gx = sem("e_gx")
        self.e_ix = sem("e_ix")
        self.g_y = sem("g_y")
        self.ld_y0 = sem("ld_y0")
        self.ld_y1 = sem("ld_y1")
        self.ld_x30 = sem("ld_x30")
        self.ld_x31 = sem("ld_x31")
        self.v_sum = sem("v_sum")
        self.a_sq3 = sem("a_sq3")
        self.v_rcp3 = sem("v_rcp3")
        self.v_o = sem("v_o")
        self.st_o0 = sem("st_o0")
        self.st_o1 = sem("st_o1")
        self.ld_wn3 = sem("ld_wn3")


def build(nc, I, out):
    def scratch(name, shape, dt):
        return nc.dram_tensor(name, shape, dt, kind="Internal").ap()

    with ExitStack() as ctx:
        base = nc.sbuf_base
        base += -base % 64
        limit = nc.sbuf_usable_end
        used = {}

        def at(name, offset, shape, dt=F32):
            n = 4 * int(np.prod(shape[1:]))
            assert base + offset + n <= limit, (name, offset, n, limit - base)
            used[name] = (offset, offset + n)
            return nc.alloc_sbuf_tensor_at(name, shape, dt, offset=base + offset)

        def sem(name):
            return ctx.enter_context(nc.semaphore(name))

        KB = 1024
        cst = at("cst", 0, [P, CW])
        small0 = 4 * CW + (-4 * CW) % 64
        cols = at("cols", small0, [P, COLS])
        o = small0 + 4 * COLS
        R0 = o

        def const(name, p0=0, p1=None, c0=0, c1=None):
            a, rows, w = CONST[name]
            return cst[p0:rows if p1 is None else p1, a + c0:a + (w if c1 is None else c1)]

        ident = const("ident")
        seen = cst[:, CONST["seen"][0]:CONST["seen"][0] + 2 * P]
        taken = [0]

        def column(n):
            a = taken[0]
            taken[0] += n
            assert taken[0] <= COLS
            return cols[:, a:a + n]

        ss, rstd, rinv = column(NT), column(NT), column(NT)
        iwc = column(NT * IH).rearrange("p (t h) -> p t h", t=NT)
        igb, fgb = column(1), column(1)
        convw = column(8 * CONV).rearrange("p (f k) -> p f k", f=8)
        convb, mnw = column(8), column(MH)
        top8 = column(16).rearrange("p (k e) -> p k e", k=2)
        mcol = column(NT * 16).rearrange("p (c k h) -> p c k h", c=NT, k=4)
        mexp = column(NT * 12).rearrange("p (c k h) -> p c k h", c=NT, k=3)
        decay = column(MH * NT).rearrange("p (h c) -> p h c", h=MH)
        mx, nmx, rs, rsi = column(2), column(2), column(16), column(HEADS)
        den, hss, hrs = column(NT * MH), column(NT * MH), column(NT * MH)
        den = den.rearrange("p (c h) -> p c h", c=NT)

        H0 = R0
        W0 = H0 + 64 * KB
        Q0 = W0 + 24 * KB
        M0 = Q0 + 24 * KB
        MVB = 4 * NT * MH * (MD + 1)
        V0 = M0 + 4 * 8 * (T + 4)
        S0 = V0 + MVB
        SCW = sum(P * (i + 1) for i in range(2, NT))
        X0 = S0 + 4 * SCW
        G0 = X0 + 12 * KB

        ht_hi = at("ht_hi", H0, [P, KC, T], F32R)
        ht_lo = at("ht_lo", H0 + 32 * KB, [P, KC, T], F32R)
        w_raw = at("w_raw", W0, [P, 2, KC, P])
        w_hi = at("w_hi", W0 + 8 * KB, [P, 2, KC, P], F32R)
        w_lo = at("w_lo", W0 + 16 * KB, [P, 2, KC, P], F32R)
        qt = at("qt", Q0, [P, 4, T])
        kt = at("kt", Q0 + 16 * KB, [P, T])
        vtok = at("vtok", Q0 + 20 * KB, [P, NT, P])
        xt = at("xt", Q0, [P, 2, D])
        xn = at("xn", Q0 + 8 * KB, [P, 2, D])
        wnb = at("wnb", Q0 + 16 * KB, [P, D])
        mqk = at("mqk", M0, [P, 8, T + 4])
        rbuf = at("rbuf", M0, [P, 2, T])
        mvtok = at("mvtok", V0, [P, NT, MH, MD + 1])
        rope_i = at("rope_i", V0, [P, 2, T])
        rtmp = at("rtmp", V0 + 8 * KB, [P, T])
        score = at("score", S0, [P, SCW])
        iqt = at("iqt", X0, [P, 2, T])
        ikt = at("ikt", X0 + 8 * KB, [P, T])
        rope_q = at("rope_q", X0, [P, 2, T])
        qtmp = at("qtmp", X0 + 8 * KB, [P, T])
        row_i = at("row_i", M0 + 24 * KB, [P, T])
        row_f = at("row_f", M0 + 28 * KB, [P, T])
        row_t = at("row_t", G0, [P, T])
        row_b = at("row_b", V0 + 12 * KB, [P, T])
        iwt = at("iwt", M0 + 8 * KB, [P, T])
        vtmp = at("vtmp", X0, [P, 2, T])
        stack = at("stack", M0 + 12 * KB, [P, T])
        mrow = at("mrow", M0 + 16 * KB, [P, T])
        carry = at("carry", M0 + 20 * KB, [P, T])
        negm = row_t

        ctmp = at("ctmp", G0 + 4 * KB, [P, T])
        cmul = at("cmul", X0 + 8 * KB, [P, T])
        mixt = at("mixt", H0, [P, KC, T])
        HW = MH * (MD + 1)
        m_kw = at("m_kw", W0, [P, MH, P])
        m_sc = at("m_sc", W0 + 2 * KB, [P, MH, P])
        m_ex = at("m_ex", W0 + 4 * KB, [P, MH, P])
        m_w = at("m_w", W0 + 6 * KB, [P, MH, P])
        m_h = at("m_h", W0 + 8 * KB, [P, MH, P])
        m_hn = at("m_hn", W0 + 10 * KB, [P, MH, P])
        m_mt = at("m_mt", W0 + 12 * KB, [P, MH, P])
        m_o = at("m_o", W0 + 14 * KB, [P, 2, MH, P])
        m_in = at("m_in", H0 + 32 * KB, [P, MH, MD + 1])
        m_nd = at("m_nd", H0 + 32 * KB + 2080, [P, MH, MD + 1])
        m_up = at("m_up", H0 + 32 * KB + 4160, [P, MH, MD + 1])
        m_n = at("m_n", H0 + 32 * KB + 6240, [P, MH, MD + 1])
        state = at("state", H0 + 32 * KB + 8320, [P, MH, MD + 1])
        a_s = at("a_s", H0 + 44 * KB, [P, 2, T])
        a_p = at("a_p", H0 + 52 * KB, [P, 2, T])
        a_t = at("a_t", W0, [P, 2, KC, P])
        arow = at("arow", W0 + 8 * KB, [P, 2, HEADS * HD])
        wo_hi = at("wo_hi", Q0, [P, KC, D], F32R)
        wo_lo = at("wo_lo", Q0 + 32 * KB, [P, KC, D], F32R)
        wo_raw = at("wo_raw", W0 + 16 * KB, [P, 2, D])
        mx_hi = at("mx_hi", H0 + 32 * KB, [P, 2, KC, P], F32R)
        mx_lo = at("mx_lo", H0 + 40 * KB, [P, 2, KC, P], F32R)
        xr = at("xr", H0 + 48 * KB, [P, 2, D])
        x2 = at("x2", H0 + 56 * KB, [P, 2, D])
        h2 = at("h2", W0, [P, 2, D])
        h2t = at("h2t", W0 + 8 * KB, [P, 2, KC, P])
        wn2 = at("wn2", S0, [P, D])
        rw = at("rw", S0 + 4 * KB, [P, KC, E])
        rb = at("rb", S0 + 5 * KB, [P, E])
        oneh = at("oneh", S0 + 6 * KB, [P, TOP, NT, E])
        prod = at("prod", S0 + 10 * KB, [P, NT, E])
        chosen = at("chosen", S0 + 11 * KB, [P, NT, E])
        place = at("place", S0 + 12 * KB, [P, NT, E])
        stepc = at("stepc", S0 + 13 * KB, [P, E, CAPT])
        F_ = R0
        e_raw = at("e_raw", F_, [P, 3, KC, 512])
        e_whi = at("e_whi", F_ + 48 * KB, [P, 4, KC, 256], F32R)
        e_wlo = at("e_wlo", F_ + 80 * KB, [P, 4, KC, 256], F32R)
        F1 = F_ + 112 * KB
        XB = 4 * KC * ROWS
        e_x = at("e_x", F1, [P, KC, 2, ROWS], F32R)
        e_a = at("e_a", F1 + 2 * XB, [P, KC, 2, ROWS], F32R)
        yt = at("yt", F1 + 4 * XB, [P, KC, ROWS])
        F2 = F1 + 5 * XB
        xg = at("xg", F2, [P, 2, D])
        yr = at("yr", F2 + 8 * KB, [P, 2, D])
        F3 = F2 + 16 * KB
        GB = 4 * 2 * 2 * ROWS
        gl, ul, sg, tt, af = [at(n_, F3 + k_ * GB, [P, 2, 2, ROWS]) for k_, n_ in enumerate(("gl", "ul", "sg", "tt", "af"))]
        F4 = F3 + 5 * GB
        brow = at("brow", F4, [P, P])
        bgu = at("bgu", F4 + 512, [P, 16])
        bdn = at("bdn", F4 + 576, [P, 8])
        idx, gidx, scur, slast = [at(n_, F4 + 640 + 32 * k_, [P, 2], I32) for k_, n_ in enumerate(("idx", "gidx", "scur", "slast"))]
        esum = at("esum", F4 + 768, [P, 2, 2, ROWS])
        yg = at("yg", F_, [P, 2, TOP, D])
        x3 = at("x3", F_ + 32 * KB, [P, 2, D])
        ot = at("ot", F_ + 40 * KB, [P, 2, D])
        wn3 = at("wn3", F_ + 48 * KB, [P, D])

        lg = column(E)
        best = column(NT * 8).rearrange("p (t k) -> p t k", t=NT)
        besti = column(NT * 8).bitcast(U32).rearrange("p (t k) -> p t k", t=NT)
        bestf = column(NT * 8).rearrange("p (t k) -> p t k", t=NT)
        gates = column(NT * TOP).rearrange("p (t k) -> p t k", t=NT)
        gsum = column(NT)
        counts, nblk, bend, bstart = column(E), column(E), column(E), column(E)
        destf = column(NT * TOP).rearrange("p (t k) -> p t k", t=NT)
        desti = column(NT * TOP).bitcast(I32).rearrange("p (t k) -> p t k", t=NT)
        bef, bei, nbi = column(1), column(1).bitcast(I32), column(1).bitcast(I32)
        tokid = column(NT * TOP).bitcast(I32).rearrange("p (t k) -> p t k", t=NT)
        mabs, mden, mrd, mss, mrs_ = column(4), column(4), column(4), column(4), column(4)
        minus1, mhalf = column(4), column(4)

        score_at = {}
        n = 0
        for i in range(2, NT):
            score_at[i] = n
            n += P * (i + 1)

        ps = ctx.enter_context(nc.psum_tensor("ps", [P, 8, 512], F32))

        def pair(b):
            return ps[:, b:b + 2, :].rearrange("p b n -> p (b n)")

        mo_d = scratch("mo_d", (MH, P, T), F32)
        x2_d = scratch("x2_d", (T, D), F32)
        h2_d = scratch("h2_d", (T + ROWS // TOP, D), F32)
        y_d = scratch("y_d", (T * TOP + ROWS, D), F32)
        tok_d = scratch("tok_d", (P * TOKW, 1), I32)
        be_d = scratch("be_d", (P, 1), I32)
        gu_w = I["w_gate_up"].rearrange("o e (c p) n -> (o e) p c n", p=P)
        dn_w = I["w_down"].rearrange("o e (c p) n -> (o e) p c n", p=P)
        gu_b = I["b_gate_up"].rearrange("o e (k n) -> (o e) k n", n=P)
        dn_b = I["b_down"].rearrange("o e (k n) -> (o e) k n", n=P)

        s = Semaphores(sem)

        def gate_on(eng, sem_, value):
            eng.wait_ge(sem_, value)
            eng.sem_inc(s.passed, 1)

        st_x, st_h, ld_r, ld_wo, ld_g = (s.st_x0, s.st_x1), (s.st_h0, s.st_h1), (s.ld_r0, s.ld_r1), (s.ld_wo0, s.ld_wo1), (s.ld_g0, s.ld_g1, s.ld_g2)
        ld_y, ld_x3, st_o = (s.ld_y0, s.ld_y1), (s.ld_x30, s.ld_x31), (s.st_o0, s.st_o1)
        ld_x, ld_w, st_mo = (s.ld_x0, s.ld_x1), (s.ld_w0, s.ld_w1), (s.st_mo0, s.st_mo1)
        fts = feature_tiles()
        bctx = ExitStack()
        block = bctx.enter_context(nc.Block())

        w_in = I["w_in"].rearrange("o (c p) n -> p (o c) n", p=P)
        nw = [0]

        def piece(ring, m):
            return ring[:, m % 4, :, :].rearrange("p k (g n) -> p k g n", g=2)

        def raw_piece(m):
            c, q = m // 2, m % 2
            a = e_raw[:, c % 3, :, :]
            if c < 4:
                return a.rearrange("p k (g n) -> p k g n", g=2)[:, :, :, P * q:P * q + P]
            return a[:, :, 256 * q:256 * q + 256].rearrange("p k (g n) -> p k g n", g=2)

        def sums_of(f):
            return ps[:, 2 * (f % 2):2 * (f % 2) + 2, 0:2 * ROWS].rearrange("p g (s n) -> p g n s", s=2)

        @block.sync
        def _(sp):
            sp.dma_start(cst[:], I["c_const"]).then_inc(s.ld_const, 16)
            sp.dma_start(wnb[:], I["mix_norm_w"][0:1, :].to_broadcast([P, D])).then_inc(s.ld_wn, 16)
            for t in range(NT):
                if t >= 2:
                    sp.wait_ge(s.v_xn, t - 1)
                sp.dma_start(xt[:, t % 2, :], I["x"][0, t * P:(t + 1) * P, :]).then_inc(ld_x[t % 2], 16)
                if t == 1:
                    for f in range(2):
                        for dst, src, w in fts[f]:
                            sp.dma_start(w_raw[:, f % 2, :, dst:dst + w], w_in[:, :, src:src + w]).then_inc(ld_w[f % 2], 16)
            sp.dma_start(igb[0:MH, :], I["igate_b"].rearrange("o h -> h o")).then_inc(s.ld_gate, 16)
            sp.dma_start(fgb[0:MH, :], I["fgate_b"].rearrange("o h -> h o")).then_inc(s.ld_gate, 16)
            sp.dma_start(carry[0:MH, :], I["c_carry"]).then_inc(s.ld_gate, 16)
            sp.dma_start(rope_i[:], I["c_rope_i"]).then_inc(s.ld_rope, 16)
            with nc.allow_non_contiguous_dma(reason="small columns"):
                for f in range(8):
                    for k in range(CONV):
                        sp.dma_start(convw[:, f, k:k + 1], I["conv_w"][0, k, f * P:(f + 1) * P].unsqueeze(1)).then_inc(s.ld_small, 16)
                    sp.dma_start(convb[:, f:f + 1], I["conv_b"][0, f * P:(f + 1) * P].unsqueeze(1)).then_inc(s.ld_small, 16)
                for h in range(MH):
                    sp.dma_start(mnw[:, h:h + 1], I["mlstm_norm_w"][0, h * P:(h + 1) * P].unsqueeze(1)).then_inc(s.ld_small, 16)
            for f in range(2, NFT):
                sp.wait_ge(s.g_wlo, f - 1)
                for dst, src, w in fts[f]:
                    sp.dma_start(w_raw[:, f % 2, :, dst:dst + w], w_in[:, :, src:src + w]).then_inc(ld_w[f % 2], 16)
                if f == 5:
                    sp.wait_ge(s.a_relu, 48)
                    sp.wait_ge(s.p_is, 48)
                    sp.dma_start(rope_q[:], I["c_rope_q"]).then_inc(s.ld_ropeq, 16)
            for j in range(4):
                sp.wait_ge(s.a_ev, FT_MO + j + 1)
                sp.dma_start(mo_d[j], vtmp[:, (FT_MO + j) % 2, :]).then_inc(st_mo[j % 2], 16)
            sp.wait_ge(st_mo[0], 32)
            sp.wait_ge(st_mo[1], 32)
            sp.wait_ge(s.p_ft, NFT)
            for c in range(NT):
                if c >= 2:
                    sp.wait_ge(s.g_mix, c - 1)
                sp.dma_start(m_o[:, c % 2, :, :], mo_d[:, :, c * P:(c + 1) * P].rearrange("h p t -> p h t")).then_inc(
                    (s.ld_mo0, s.ld_mo1)[c % 2], 16)

            sp.wait_ge(s.a_at, NT)
            sp.dma_start(wn2[:], I["ffn_norm_w"][0:1, :].to_broadcast([P, D])).then_inc(s.ld_wn2, 16)
            sp.dma_start(rw[:], I["router_w"].rearrange("o (c p) n -> p (o c) n", p=P)).then_inc(s.ld_rw, 16)
            sp.dma_start(rb[:], I["router_b"][0:1, :].to_broadcast([P, E])).then_inc(s.ld_rw, 16)
            for c in range(KC):
                if c >= 2:
                    sp.wait_ge(s.g_wolo, c - 1)
                sp.dma_start(wo_raw[:, c % 2, :], I["w_out"][0, c * P:(c + 1) * P, :]).then_inc(ld_wo[c % 2], 16)
            for t in range(NT + 1):
                if t < NT:
                    if t >= 2:
                        sp.wait_ge(s.v_x2, t - 1)
                    sp.dma_start(xr[:, t % 2, :], I["x"][0, t * P:(t + 1) * P, :]).then_inc(ld_r[t % 2], 16)
                if t >= 1:
                    rows = slice((t - 1) * P, t * P)
                    sp.wait_ge(s.v_x2, t)
                    sp.dma_start(x2_d[rows, :], x2[:, (t - 1) % 2, :]).then_inc(st_x[(t - 1) % 2], 16)
                    sp.wait_ge(s.v_h2, t)
                    sp.dma_start(h2_d[rows, :], h2[:, (t - 1) % 2, :]).then_inc(st_h[(t - 1) % 2], 16)
                    if t == NT:
                        sp.dma_start(h2_d[T:T + ROWS // TOP, :], h2[0:ROWS // TOP, (t - 1) % 2, :]).then_inc(s.st_hx, 16)
            sp.dma_start(tok_d.rearrange("(p w) o -> p (w o)", w=TOKW), I["c_slots"]).then_inc(s.st_zero, 16)
            sp.wait_ge(s.v_dest, DEST_STEPS)
            sp.dma_start(be_d, bei).then_inc(s.st_be, 16)
            sp.dma_start(scur[0:HALF, :], I["c_slots"][0:2, :].rearrange("a (q h) -> (a q) h", h=2)).then_inc(s.ld_scur, 16)
            sp.wait_ge(s.st_be, 16)
            sp.wait_ge(s.st_y, 32)
            sp.wait_ge(s.st_tok, 16 * (NT * TOP - 2))
            sp.wait_ge(s.st_hx, 16)
            for k in range(2):
                sp.wait_ge(st_x[k], 16 * NT // 2)
                sp.wait_ge(st_h[k], 16 * NT // 2)

            nb = sp.value_load(nbi[0:1, 0:1], min_val=1, max_val=NBMAX)
            sp.dma_start(idx[0:HALF, :], tok_d[0:ROWS, :].rearrange("(p h) o -> p (h o)", p=HALF)).then_inc(s.ld_idx, 16)
            e0 = sp.value_load(be_d[0:1, 0:1], min_val=0, max_val=E - 1)
            sp.dma_start(brow[0:16, :], gu_b[bass.ds(e0, 1), :, :].rearrange("o k n -> (o k) n")).then_inc(s.ld_b, 16)
            sp.dma_start(brow[16:24, :], dn_b[bass.ds(e0, 1), :, :].rearrange("o k n -> (o k) n")).then_inc(s.ld_b, 16)
            with sp.Fori(0, nb) as i:
                e = sp.value_load(be_d[bass.ds(i, 1), 0:1], min_val=0, max_val=E - 1)
                for c in range(6):
                    sp.wait_ge(s.e_lo, i * 12 + (2 * c + 2))
                    sp.wait_ge(s.e_lop, i * 12 + (2 * c + 2))
                    if c < 4:
                        for k in range(2):
                            a_ = FE * k + 256 * c
                            sp.dma_start(e_raw[:, c % 3, :, 256 * k:256 * k + 256],
                                         gu_w[bass.ds(e, 1), :, :, a_:a_ + 256].rearrange("o p c n -> (o p) c n")).then_inc(ld_g[c % 3], 16)
                    else:
                        for k in range(2):
                            a_ = 512 * (c - 4) + 256 * k
                            sp.dma_start(e_raw[:, c % 3, :, 256 * k:256 * k + 256],
                                         dn_w[bass.ds(e, 1), :, :, a_:a_ + 256].rearrange("o p c n -> (o p) c n")).then_inc(ld_g[c % 3], 16)
                    if c == 3:
                        en = sp.value_load(be_d[bass.ds(i + 1, 1), 0:1], min_val=0, max_val=E - 1)
                        sp.wait_ge(s.e_gx, i + 1)
                        sp.wait_ge(s.e_ix, i * 2 + 3)
                        sp.dma_start(idx[0:HALF, :], tok_d[bass.ds((i + 1) * ROWS, ROWS), :].rearrange("(p h) o -> p (h o)", p=HALF)).then_inc(s.ld_idx, 16)
                        sp.wait_ge(s.p_xt, i + 1)
                        sp.dma_start(brow[0:16, :], gu_b[bass.ds(en, 1), :, :].rearrange("o k n -> (o k) n")).then_inc(s.ld_b, 16)
                        sp.dma_start(brow[16:24, :], dn_b[bass.ds(en, 1), :, :].rearrange("o k n -> (o k) n")).then_inc(s.ld_b, 16)

            sp.wait_ge(s.p_pc, nb * 12 + 4)
            sp.wait_ge(s.g_y, 1)
            sp.wait_ge(s.ld_idx, nb * 16 + 16)
            sp.wait_ge(s.ld_b, nb * 32 + 32)
            sp.dma_start(wn3[:], I["final_norm_w"].rearrange("(o n) -> o n", o=1).to_broadcast([P, D])).then_inc(s.ld_wn3, 16)
            for t in range(NT + 1):
                if t < NT:
                    if t >= 2:
                        sp.wait_ge(s.v_o, t - 1)
                    sp.dma_start(yg[:, t % 2, :, :], y_d[t * P * TOP:(t + 1) * P * TOP, :].rearrange("(p k) n -> p k n", k=TOP)).then_inc(ld_y[t % 2], 16)
                    sp.dma_start(x3[:, t % 2, :], x2_d[t * P:(t + 1) * P, :]).then_inc(ld_x3[t % 2], 16)
                if t >= 1:
                    sp.wait_ge(s.v_o, t)
                    sp.dma_start(out[0, (t - 1) * P:t * P, :], ot[:, (t - 1) % 2, :]).then_inc(st_o[(t - 1) % 2], 16)
            sp.wait_ge(st_o[0], 16 * NT // 2)
            sp.wait_ge(st_o[1], 16 * NT // 2)

        loads = [sum(16 * len(fts[g]) for g in range(f % 2, f + 1, 2)) for f in range(NFT)]

        @block.gpsimd
        def _(gp):
            conv = Steps(gp, s.g_conv)

            def convolve(f):
                gp.wait_ge(s.a_ev, FT_MQK + f + 1)
                if f >= 1:
                    gp.wait_ge(s.a_silu, f)
                x = [mqk[:, f, 1 + k:1 + k + T] for k in range(CONV)]
                conv(nc.gpsimd.tensor_scalar(ctmp[:], x[3], convw[:, f, 3:4], convb[:, f:f + 1], ALU.mult, ALU.add))
                for k in range(3):
                    conv(nc.gpsimd.tensor_scalar(cmul[:], x[k], convw[:, f, k:k + 1], 1.0, ALU.mult, ALU.mult))
                    conv.done()
                    conv(nc.gpsimd.tensor_tensor(ctmp[:], ctmp[:], cmul[:], ALU.add))
                    conv.done()

            for f in range(NFT):
                gp.wait_ge(s.a_whi, f + 1)
                if f >= 2:
                    gp.wait_ge(s.p_ft, f - 1)
                nc.gpsimd.tensor_tensor(w_lo[:, f % 2, :, :], w_raw[:, f % 2, :, :],
                                        w_hi[:, f % 2, :, :].bitcast(F32), ALU.subtract).then_inc(s.g_wlo, 1)
                if f == 3:
                    nc.gpsimd.memset(stack[:], 0.0).then_inc(s.g_stack, 1)
                if f == FT_MQK:
                    gp.wait_ge(s.v_score, 6 * 9)
                    gp.wait_ge(s.v_gate, 12)
                    gp.wait_ge(s.p_iwt, 1)
                    gp.wait_ge(s.p_mcol, 1)
                    nc.gpsimd.memset(mqk[:, :, 0:4], 0.0).then_inc(s.g_pad, 1)
                    gp.wait_ge(s.v_ra, 3)
                    nc.gpsimd.memset(mvtok[:, :, :, MD:MD + 1], 1.0).then_inc(s.g_ones, 1)
                if FT_Q + 2 <= f <= FT_K + 2:
                    j = f - 2 - FT_Q
                    ft = qt[:, j, :] if j < 4 else kt[:]
                    gp.wait_ge(s.ld_ropeq, 16)
                    gp.wait_ge(s.a_rq, j + 1)
                    nc.gpsimd.tensor_tensor(qtmp[:], qtmp[:], rope_q[:, 1, :], ALU.mult).then_inc(s.g_rq, 1)
                    nc.gpsimd.tensor_tensor(ft, ft, rope_q[:, 0, :], ALU.mult).then_inc(s.g_rq, 1)
                    gp.wait_ge(s.g_rq, 3 * j + 2)
                    nc.gpsimd.tensor_tensor(ft, ft, qtmp[:], ALU.add).then_inc(s.g_rq, 1)
                if f >= FT_MQK + 2 and f % 2 == 0:
                    if f == FT_MQK + 2:
                        gp.wait_ge(s.g_rq, 15)
                        gp.wait_ge(s.ld_small, 16 * (8 * CONV + 8 + MH))
                    convolve((f - FT_MQK - 2) // 2)

            convolve(7)

            m1, m2, rms = Steps(gp, s.g_m1), Steps(gp, s.g_m2), Steps(gp, s.g_rms)
            gp.wait_ge(s.p_ft, NFT)
            m1(nc.gpsimd.memset(state[:], 0.0))
            m1(nc.gpsimd.memset(minus1, -1.0))
            m1(nc.gpsimd.memset(mhalf, -0.5))
            gp.wait_ge(s.a_mexp, 1)
            m1(nc.gpsimd.tensor_scalar(mexp[:, :, 1, :], mexp[:, :, 1, :], MD ** -0.5, 1.0, ALU.mult, ALU.mult))
            m1.done()
            for c in range(NT):
                gp.wait_ge(s.a_m1, 9 * (c + 1))
                m1(nc.gpsimd.tensor_tensor(m_w[:], m_sc[:], m_ex[:], ALU.mult))
                gp.wait_ge(s.a_m2, 8 * (c + 1) - 2)
                m2(nc.gpsimd.tensor_tensor(m_n[:], m_nd[:], m_in[:], ALU.add))
                gp.wait_ge(s.a_m2, 8 * (c + 1))
                for h in range(MH):
                    m2(nc.gpsimd.tensor_scalar(state[:, h, :], state[:, h, :], decay[:, h, c:c + 1], 1.0, ALU.mult, ALU.mult))
                m2.done()
                m2(nc.gpsimd.tensor_tensor(state[:], state[:], m_up[:], ALU.add))
                gp.wait_ge(s.a_sq, 5 * c + 1)
                for h in range(MH):
                    rms(nc.gpsimd.tensor_scalar(mden[:, h:h + 1], mabs[:, h:h + 1], mexp[:, c, 2, h:h + 1], 1.0, ALU.max, ALU.mult))
                rms.done()
                rms(nc.gpsimd.tensor_tensor(mrd, mden, minus1, ALU.pow))
                rms.done()
                rms(nc.gpsimd.tensor_tensor(m_h[:], m_n[:, :, 0:MD], mrd.unsqueeze(2).to_broadcast([P, MH, MD]), ALU.mult))
                gp.wait_ge(s.a_sq, 5 * c + 5)
                rms(nc.gpsimd.tensor_scalar(mrs_, mss, 1.0 / MD, EPS, ALU.mult, ALU.add))
                rms.done()
                rms(nc.gpsimd.tensor_tensor(mss, mrs_, mhalf, ALU.pow))
                gp.wait_ge(s.a_m3, 4 * (c + 1))
                gp.wait_ge((s.ld_mo0, s.ld_mo1)[c % 2], 16 * (c // 2 + 1))
                nc.gpsimd.tensor_tensor(mixt[:, 4:8, c * P:(c + 1) * P], m_mt[:], m_o[:, c % 2, :, :], ALU.mult).then_inc(s.g_mix, 1)

            for c in range(KC):
                gp.wait_ge(s.a_wohi, c + 1)
                nc.gpsimd.tensor_tensor(wo_lo[:, c, :], wo_raw[:, c % 2, :], wo_hi[:, c, :].bitcast(F32), ALU.subtract).then_inc(s.g_wolo, 1)
            nc.gpsimd.iota(tokid, pattern=[[P * TOP, NT], [1, TOP]], base=0, channel_multiplier=TOP).then_inc(s.g_tok, 1)
            gp.wait_ge(s.g_tok, 1)
            gp.wait_ge(s.st_zero, 16)
            gp.wait_ge(s.v_dest, DEST_STEPS)
            for t in range(NT):
                for k in range(TOP):
                    nc.gpsimd.indirect_dma_start(tok_d[:, :], bass.IndirectOffsetOnAxis(ap=desti[:, t, k:k + 1], axis=0),
                                                 tokid[:, t, k:k + 1], None).then_inc(s.st_y if t == NT - 1 and k >= 2 else s.st_tok, 16)
            for k in range(2):
                gp.wait_ge(st_h[k], 16 * NT // 2)
            gp.wait_ge(s.st_hx, 16)

            def gather():
                for h in range(2):
                    nc.gpsimd.indirect_dma_start(xg[0:HALF, h, :], None, h2_d[:, :],
                                                 bass.IndirectOffsetOnAxis(ap=gidx[0:HALF, h:h + 1], axis=0)).then_inc(s.ld_xg, 16)

            def scatter(rows):
                for h in range(2):
                    nc.gpsimd.indirect_dma_start(y_d[:, :], bass.IndirectOffsetOnAxis(ap=rows[0:HALF, h:h + 1], axis=0),
                                                 yr[0:HALF, h, :], None).then_inc(s.st_y, 16)

            nb = gp.value_load(nbi[0:1, 0:1], min_val=1, max_val=NBMAX)
            gp.wait_ge(s.e_gx, 1)
            gather()
            gp.sem_inc(s.e_lop, 6)
            gp.wait_ge(s.e_lop, 6)
            with gp.Fori(0, nb) as i:
                for m in range(PIECES):
                    gate_on(gp, s.e_hi, i * PIECES + (m + 1))
                    ks = slice(KDVE, KC)
                    nc.gpsimd.tensor_tensor(piece(e_wlo, m)[:, ks], raw_piece(m)[:, ks], piece(e_whi, m)[:, ks].bitcast(F32),
                                            ALU.subtract).then_inc(s.e_lop, 1)
                    if m == 6:
                        gate_on(gp, s.e_gx, i + 2)
                        gate_on(gp, s.p_xt, i + 1)
                        gather()
                    if m == 7:
                        gate_on(gp, s.e_ix, i * 2 + 3)
                        gate_on(gp, s.e_yr, i * 4 + 5)
                        scatter(slast)
            gate_on(gp, s.e_yr, nb * 4 + 5)
            scatter(scur)
            gate_on(gp, s.ld_xg, nb * 32 + 32)
            gate_on(gp, s.st_y, nb * 32 + 64)

            gp.sem_inc(s.g_y, 1)

        @block.scalar
        def _(act):
            act.wait_ge(s.ld_const, 16)

            def ht_hi_of(t):
                act.wait_ge(s.p_ht, t + 1)
                nc.scalar.activation(ht_hi[:, :, t * P:(t + 1) * P],
                                     pair(2 * (t % 2)).rearrange("p (c n) -> p c n", c=KC), ACT.Copy).then_inc(s.a_hthi, 1)

            for t in range(NT):
                act.wait_ge(ld_x[t % 2], 16 * (t // 2 + 1))
                if t >= 2:
                    act.wait_ge(s.p_ht, t - 1)
                nc.scalar.activation(xn[:, t % 2, :], xt[:, t % 2, :], ACT.Square, accum_out=ss[:, t:t + 1]).then_inc(s.a_square, 1)
                act.wait_ge(s.a_square, t + 1)
                nc.scalar.activation(rstd[:, t:t + 1], ss[:, t:t + 1], ACT.Sqrt, bias=EPS, scale=1.0 / D).then_inc(s.a_root, 1)
                if t >= 1:
                    ht_hi_of(t - 1)
            ht_hi_of(NT - 1)

            def hi(f):
                act.wait_ge(ld_w[f % 2], loads[f])
                if f >= 2:
                    act.wait_ge(s.p_ft, f - 1)
                nc.scalar.activation(w_hi[:, f % 2, :, :], w_raw[:, f % 2, :, :], ACT.Copy).then_inc(s.a_whi, 1)

            def evacuate(f):
                act.wait_ge(s.p_ft, f + 1)
                src = pair(4 + 2 * (f % 2))
                if f < FT_IK:
                    nc.scalar.activation(iqt[:, f, :], src, ACT.Copy).then_inc(s.a_ev, 1)
                elif f == FT_IK:
                    nc.scalar.activation(ikt[:], src, ACT.Copy).then_inc(s.a_ev, 1)
                elif f == FT_SMALL:
                    act.wait_ge(s.ld_gate, 48)
                    nc.scalar.activation(row_i[0:MH, :], src[0:MH, :], ACT.Identity, bias=igb[0:MH, :]).then_inc(s.a_gate, 1)
                    nc.scalar.activation(row_f[0:MH, :], src[32:32 + MH, :], ACT.Identity, bias=fgb[0:MH, :]).then_inc(s.a_gate, 1)
                    nc.scalar.activation(iwt[0:IH, :], src[64:64 + IH, :], ACT.Copy, scale=1.0 / 16.0).then_inc(s.a_ev, 1)
                    act.wait_ge(s.a_gate, 2)
                    nc.scalar.activation(row_t[0:MH, :], row_f[0:MH, :], ACT.Abs).then_inc(s.a_gate, 1)
                    act.wait_ge(s.a_gate, 3)
                    nc.scalar.activation(row_t[0:MH, :], row_t[0:MH, :], ACT.Exp, scale=-1.0).then_inc(s.a_gate, 1)
                    act.wait_ge(s.a_gate, 4)
                    nc.scalar.activation(row_t[0:MH, :], row_t[0:MH, :], ACT.Ln, bias=1.0).then_inc(s.a_gate, 1)
                elif f < FT_K:
                    nc.scalar.activation(qt[:, f - FT_Q, :], src, ACT.Copy).then_inc(s.a_ev, 1)
                elif f == FT_K:
                    nc.scalar.activation(kt[:], src, ACT.Copy).then_inc(s.a_ev, 1)
                elif f == FT_V or FT_MV <= f < FT_MO:
                    if f == FT_V:
                        act.wait_ge(s.g_rq, 15)
                    else:
                        act.wait_ge(s.p_vt, 1 if f < FT_MV + 2 else f - FT_MV)
                    nc.scalar.activation(vtmp[:, f % 2, :], src, ACT.Copy).then_inc(s.a_ev, 1)
                elif f < FT_MV:
                    if f == FT_MQK:
                        act.wait_ge(s.g_pad, 1)
                    nc.scalar.activation(mqk[:, f - FT_MQK, 4:4 + T], src, ACT.Copy).then_inc(s.a_ev, 1)
                else:
                    if f < FT_MO + 2:
                        act.wait_ge(s.p_vt, f - FT_MO + 4)
                    else:
                        act.wait_ge(st_mo[f % 2], 16)
                    nc.scalar.activation(vtmp[:, f % 2, :], src, ACT.Sigmoid).then_inc(s.a_ev, 1)

            def silu(f):
                act.wait_ge(s.g_conv, 7 * (f + 1))
                nc.scalar.activation(mqk[:, f, 4:4 + T], ctmp[:], ACT.Silu).then_inc(s.a_silu, 1)

            def at_out(i):
                act.wait_ge(s.p_at, i + 1)
                nc.scalar.activation(mixt[:, 0:4, i * P:(i + 1) * P], ps[:, 7, :].rearrange("p (c n) -> p c n", n=P),
                                     ACT.Copy).then_inc(s.a_at, 1)

            for f in range(NFT + 1):
                if f < NFT:
                    hi(f)
                if f >= 1:
                    evacuate(f - 1)
                if f == FT_SMALL + 1:
                    act.wait_ge(s.p_iwt, 1)
                    nc.scalar.activation(iwc, ps[:, 0, 0:NT * IH].rearrange("p (t h) -> p t h", t=NT), ACT.Copy).then_inc(s.a_iwt, 1)
                    for u in range(6 * IH):
                        i, h = 2 + u // IH, u % IH
                        w = P * (i + 1)
                        act.wait_ge(s.p_is, u + 1)
                        if u >= 2:
                            act.wait_ge(s.v_score, 9 * ((u - 2) // IH) + (u - 2) % IH + 1)
                        nc.scalar.activation(rbuf[:, u % 2, 0:w], pair(2 * (u % 2))[:, 0:w], ACT.Relu).then_inc(s.a_relu, 1)
                    act.wait_ge(s.v_mcol, 1)
                    nc.scalar.activation(mexp, mcol[:, :, 1:4, :], ACT.Exp).then_inc(s.a_mexp, 1)
                    act.wait_ge(s.p_decay, 1)
                    nc.scalar.activation(decay, ps[:, 0, 0:MH * NT].rearrange("p (h c) -> p h c", h=MH), ACT.Exp).then_inc(s.a_decay, 1)
                if FT_Q + 1 <= f <= FT_K + 1:
                    j = f - 1 - FT_Q
                    act.wait_ge(s.p_rq, j + 1)
                    if j >= 1:
                        act.wait_ge(s.g_rq, 3 * j)
                    else:
                        act.wait_ge(s.a_relu, 48)
                        act.wait_ge(s.p_is, 48)
                    nc.scalar.activation(qtmp[:], pair(2 * (j % 2)), ACT.Copy).then_inc(s.a_rq, 1)
                if f == FT_V + 1 or FT_MV + 1 <= f <= FT_MO:
                    j = 0 if f == FT_V + 1 else f - FT_MV
                    act.wait_ge(s.p_vt, j + 1)
                    if j == 1:
                        act.wait_ge(s.g_ones, 1)
                    dst = vtok[:] if j == 0 else mvtok[:, :, j - 1, 0:MD]
                    nc.scalar.activation(dst, pair(2 * ((j + 1) % 2)).rearrange("p (t n) -> p t n", t=NT), ACT.Copy).then_inc(s.a_vt, 1)

                if f >= FT_MQK + 4 and f % 2 == 0:
                    silu((f - FT_MQK - 4) // 2)
            silu(7)

            m1, m2, sq = Steps(act, s.a_m1), Steps(act, s.a_m2), Steps(act, s.a_sq)
            for c in range(NT):
                act.wait_ge(s.p_m1, c + 1)
                if c == 0:
                    act.wait_ge(s.g_m1, 4)
                else:
                    act.wait_ge(s.p_m2, 2 * c)
                    act.wait_ge(s.g_m1, 4 + c)
                for h in range(MH):
                    m1(nc.scalar.activation(m_kw[:, h, :], ps[:, 0, h * P:(h + 1) * P], ACT.Copy, scale=mexp[:, c, 1, h:h + 1]))
                for h in range(MH):
                    m1(nc.scalar.activation(m_ex[:, h, :], ps[:, 2, h * P:(h + 1) * P], ACT.Exp, bias=mcol[:, c, 0, h:h + 1]))
                m1(nc.scalar.activation(m_sc[:], ps[:, 1, :].rearrange("p (h n) -> p h n", h=MH), ACT.Copy, scale=MD ** -0.5))
                act.wait_ge(s.p_m2, 2 * c + 1)
                if c >= 1:
                    act.wait_ge(s.g_m2, 6 * c)
                for h in range(MH):
                    b, o_ = 5 + h // 2, (h % 2) * (MD + 1)
                    m2(nc.scalar.activation(m_in[:, h, :], ps[:, b, o_:o_ + MD + 1], ACT.Copy, scale=mexp[:, c, 0, h:h + 1]))
                for k in range(2):
                    m2(nc.scalar.activation(m_nd[:, 2 * k:2 * k + 2, :], ps[:, 3 + k, 0:2 * (MD + 1)].rearrange("p (h n) -> p h n", h=2), ACT.Copy))
                act.wait_ge(s.p_m2, 2 * c + 2)
                for k in range(2):
                    m2(nc.scalar.activation(m_up[:, 2 * k:2 * k + 2, :], ps[:, (7, 0)[k], 0:2 * (MD + 1)].rearrange("p (h n) -> p h n", h=2), ACT.Copy))
                act.wait_ge(s.g_m2, 6 * c + 1)
                sq(nc.scalar.activation(mabs, m_n[:, :, MD], ACT.Abs))
                act.wait_ge(s.g_rms, 8 * c + 6)
                if c >= 1:
                    act.wait_ge(s.p_m3, c)
                for h in range(MH):
                    sq(nc.scalar.activation(m_hn[:, h, :], m_h[:, h, :], ACT.Square, accum_out=mss[:, h:h + 1]))
                act.wait_ge(s.g_rms, 8 * c + 8)
                sq.done()
                for h in range(MH):
                    nc.scalar.activation(m_hn[:, h, :], m_h[:, h, :], ACT.Copy, scale=mss[:, h:h + 1]).then_inc(s.a_hn, 1)
                act.wait_ge(s.p_m3, c + 1)
                if c >= 1:
                    act.wait_ge(s.g_mix, c)
                for h in range(MH):
                    nc.scalar.activation(m_mt[:, h, :], ps[:, 2, h * P:(h + 1) * P], ACT.Copy, scale=mnw[:, h:h + 1]).then_inc(s.a_m3, 1)

            def exp(u):
                i, h = u // HEADS, u % HEADS
                w = P * (i + 1)
                act.wait_ge(s.v_nm, u + 1)
                if u >= 2:
                    act.wait_ge(s.p_pt, u - 1)
                if h == 0 and i >= 2:
                    act.wait_ge(s.v_rs, i - 1)
                nc.scalar.activation(a_p[:, u % 2, 0:w], a_s[:, u % 2, 0:w], ACT.Exp, scale=HD ** -0.5, bias=nmx[:, u % 2:u % 2 + 1],
                                     accum_out=rs[:, (i % 2) * 8 + h:(i % 2) * 8 + h + 1]).then_inc(s.a_exp, 1)

            def pt_out(u):
                i = u // HEADS
                act.wait_ge(s.p_pt, u + 1)
                if u >= 2:
                    act.wait_ge(s.p_pv, u - 1)
                nc.scalar.activation(a_t[:, u % 2, 0:i + 1, :], pair(4)[:, 0:P * (i + 1)].rearrange("p (c n) -> p c n", n=P),
                                     ACT.Copy).then_inc(s.a_pt, 1)

            act.wait_ge(s.g_mix, NT)
            exp(0)
            for u in range(NT * HEADS):
                if u + 1 < NT * HEADS:
                    exp(u + 1)
                pt_out(u)
                if u % HEADS == 2 and u > HEADS:
                    at_out(u // HEADS - 1)
            at_out(NT - 1)


            def root2(t):
                act.wait_ge(s.v_x2, t + 1)
                if t >= 2:
                    act.wait_ge(st_h[t % 2], 16 * (t // 2))
                    act.wait_ge(s.p_h2t, t - 1)
                nc.scalar.activation(h2[:, t % 2, :], x2[:, t % 2, :], ACT.Square, accum_out=ss[:, t:t + 1]).then_inc(s.a_sq2, 1)
                act.wait_ge(s.a_sq2, t + 1)
                nc.scalar.activation(rstd[:, t:t + 1], ss[:, t:t + 1], ACT.Sqrt, bias=EPS, scale=1.0 / D).then_inc(s.a_root2, 1)

            def h2t_out(t):
                act.wait_ge(s.p_h2t, t + 1)
                if t >= 2:
                    act.wait_ge(s.p_lg, t - 1)
                nc.scalar.activation(h2t[:, t % 2, :, :], pair(4).rearrange("p (c n) -> p c n", c=KC), ACT.Copy).then_inc(s.a_h2t, 1)

            for c in range(KC):
                act.wait_ge(ld_wo[c % 2], 16 * (c // 2 + 1))
                nc.scalar.activation(wo_hi[:, c, :], wo_raw[:, c % 2, :], ACT.Copy).then_inc(s.a_wohi, 1)
            for t in range(NT + 1):
                if t < NT:
                    if t >= 2:
                        act.wait_ge(s.p_out, t - 1)
                    nc.scalar.activation(mx_hi[:, t % 2, :, :], mixt[:, :, t * P:(t + 1) * P], ACT.Copy).then_inc(s.a_mxhi, 1)
                if t >= 1:
                    root2(t - 1)
                    h2t_out(t - 1)
            act.wait_ge(s.v_route, 1)
            nc.scalar.activation(gates, gates, ACT.Exp).then_inc(s.a_gexp, 1)

            act.wait_ge(s.v_dest, DEST_STEPS)
            nb = act.value_load(nbi[0:1, 0:1], min_val=1, max_val=NBMAX)

            def x_hi(n):
                act.wait_ge(s.p_xt, n)
                nc.scalar.activation(e_x[:, 0:6, 0, :].rearrange("p (b k) n -> p b k n", b=2),
                                     ps[:, 4:6, 0:3 * ROWS].rearrange("p b (k n) -> p b k n", k=3), ACT.Copy).then_inc(s.e_xh, 1)
                nc.scalar.activation(e_x[:, 6:8, 0, :], ps[:, 6, 0:2 * ROWS].rearrange("p (k n) -> p k n", k=2), ACT.Copy).then_inc(s.e_xh, 1)

            def y_rows(i, q):
                h, dq = q // 2, q % 2
                act.wait_ge(s.p_yt, i * 4 + (q + 1))
                nc.scalar.activation(yr[0:HALF, h, dq * 512:dq * 512 + 512], ps[0:HALF, 4 + q, :], ACT.Copy).then_inc(s.e_yr, 1)

            def y_bias(i, m):
                act.wait_ge(s.e_yd, i * 4 + (m + 1))
                for d in (2 * m, 2 * m + 1):
                    nc.scalar.activation(yt[:, d, :], yt[:, d, :], ACT.Identity, bias=bdn[:, d:d + 1]).then_inc(s.e_y, 1)

            x_hi(1)
            act.sem_inc(s.e_yr, 1)
            act.wait_ge(s.e_yr, 1)
            with act.Fori(0, nb) as i:
                def split_hi(m):
                    act.wait_ge(ld_g[m // 2 % 3], i * 64 + 32 * (m // 6 + 1))
                    act.wait_ge(s.p_pc, i * PIECES + (m + 1))
                    nc.scalar.activation(piece(e_whi, m), raw_piece(m), ACT.Copy).then_inc(s.e_hi, 1)

                def sigmoid(q):
                    act.wait_ge(s.e_mn, i * 16 + 4 * (q + 1))
                    nc.scalar.activation(sg[:, q % 2], gl[:, q % 2], ACT.Sigmoid, scale=ALPHA).then_inc(s.e_sg, 1)

                def a_hi(q):
                    act.wait_ge(s.e_act, i * 4 + (q + 1))
                    if q == 0:
                        act.wait_ge(s.p_pc, i * PIECES + 4)
                    nc.scalar.activation(e_a[:, 2 * q:2 * q + 2, 0, :], af[:, q % 2], ACT.Copy).then_inc(s.e_ah, 1)

                act.wait_ge(s.e_bd, i + 1)
                for m in range(4):
                    split_hi(m)
                    y_bias(i, m)
                act.wait_ge(s.e_bg, i + 1)
                act.wait_ge(s.e_y, i * 8 + 8)
                nc.scalar.activation(bdn[:], ps[:, 6, 2 * ROWS + 16:2 * ROWS + 24], ACT.Copy).then_inc(s.e_bd, 1)
                for m in range(4, 6):
                    split_hi(m)
                sigmoid(0)
                act.wait_ge(s.st_y, i * 32 + 32)
                for q in range(4):
                    y_rows(i, q)
                for q in range(3):
                    split_hi(2 * q + 6)
                    a_hi(q)
                    if q < 2:
                        split_hi(2 * q + 7)
                    sigmoid(q + 1)
                a_hi(3)
                split_hi(11)
                x_hi(i + 2)
            act.wait_ge(s.e_bd, nb + 1)
            for m in range(4):
                y_bias(nb, m)
            act.wait_ge(s.st_y, nb * 32 + 32)
            for q in range(4):
                y_rows(nb, q)

            for t in range(NT):
                act.wait_ge(s.v_sum, 4 * (t + 1))
                if t >= 2:
                    act.wait_ge(st_o[t % 2], 16 * (t // 2))
                nc.scalar.activation(ot[:, t % 2, :], x3[:, t % 2, :], ACT.Square, accum_out=ss[:, t:t + 1]).then_inc(s.a_sq3, 1)
                act.wait_ge(s.a_sq3, 2 * t + 1)
                nc.scalar.activation(rstd[:, t:t + 1], ss[:, t:t + 1], ACT.Sqrt, bias=EPS, scale=1.0 / D).then_inc(s.a_sq3, 1)

        def product(dst, a_hi, a_lo, b_hi, b_lo, first, last):
            nc.tensor.matmul(dst, a_hi, b_hi, start=first, stop=False)
            nc.tensor.matmul(dst, a_hi, b_lo, start=False, stop=False)
            return nc.tensor.matmul(dst, a_lo, b_hi, start=False, stop=last)

        @block.tensor
        def _(pe):
            pe.wait_ge(s.ld_const, 16)
            for t in range(NT):
                pe.wait_ge(s.v_xn, t + 1)
                if t >= 2:
                    pe.wait_ge(s.v_htlo, t - 1)
                    pe.wait_ge(s.a_hthi, t - 1)
                for c in range(KC):
                    m = nc.tensor.transpose(pair(2 * (t % 2))[:, c * P:(c + 1) * P], xn[:, t % 2, c * P:(c + 1) * P], ident)
                m.then_inc(s.p_ht, 1)

            def project(f):
                pe.wait_ge(s.g_wlo, f + 1)
                if f == 0:
                    pe.wait_ge(s.v_htlo, NT)
                    pe.wait_ge(s.a_hthi, NT)
                if f >= 2:
                    pe.wait_ge(s.a_ev, f - 1)
                for half in range(2):
                    tok = slice(half * 512, half * 512 + 512)
                    for c in range(KC):
                        m = product(ps[:, 4 + 2 * (f % 2) + half, :], w_hi[:, f % 2, c, :], w_lo[:, f % 2, c, :],
                                    ht_hi[:, c, tok], ht_lo[:, c, tok], c == 0, c == KC - 1)
                m.then_inc(s.p_ft, 1)

            for f in range(4):
                project(f)
            for j in range(3):
                pe.wait_ge(s.a_ev, j + 1)
                if j == 2:
                    pe.wait_ge(s.v_rm, 1)
                for half in range(2):
                    m = nc.tensor.matmul(ps[:, 2 * (j % 2) + half, :], const("swap_i"),
                                         (iqt[:, j, :] if j < 2 else ikt[:])[:, half * 512:half * 512 + 512], start=True, stop=True)
                m.then_inc(s.p_ri, 1)
            pe.wait_ge(s.a_ev, 4)
            pe.wait_ge(s.v_rm, 3)
            for t in range(NT):
                m = nc.tensor.transpose(ps[:, 0, t * IH:(t + 1) * IH], iwt[0:IH, t * P:(t + 1) * P], ident[0:IH, 0:IH])
            m.then_inc(s.p_iwt, 1)
            pe.wait_ge(s.a_iwt, 1)
            pe.wait_ge(s.v_ra, 3)
            for u in range(6 * IH):
                i, h = 2 + u // IH, u % IH
                w = P * (i + 1)
                if u >= 2:
                    pe.wait_ge(s.a_relu, u - 1)
                g = slice(ID * (h % 4), ID * (h % 4) + ID)
                for a in range(0, w, 512):
                    b = min(a + 512, w)
                    m = nc.tensor.matmul(pair(2 * (u % 2))[:, a:b], iqt[g, h // 4, i * P:(i + 1) * P], ikt[g, a:b],
                                         start=True, stop=True)
                m.then_inc(s.p_is, 1)
            pe.wait_ge(s.v_gate, 12)
            pe.wait_ge(s.a_relu, 48)
            for c in range(NT):
                m = nc.tensor.transpose(pair(2)[:, c * P:(c + 1) * P], stack[:, c * P:(c + 1) * P], ident)
            m.then_inc(s.p_mcol, 1)
            for h in range(MH):
                m = nc.tensor.matmul(ps[:, 0, h * NT:(h + 1) * NT], const("pick", c0=h * P, c1=(h + 1) * P),
                                     mrow[0:MH, 0:NT], start=True, stop=True)
            m.then_inc(s.p_decay, 1)
            for f in range(4, NFT + 1):
                if f < NFT:
                    project(f)
                if FT_Q + 1 <= f <= FT_K + 1:
                    j = f - 1 - FT_Q
                    pe.wait_ge(s.a_ev, f)
                    if j == 0:
                        pe.wait_ge(s.v_mcol, 1)
                        pe.wait_ge(s.a_decay, 1)
                    if j >= 2:
                        pe.wait_ge(s.a_rq, j - 1)
                    for half in range(2):
                        m = nc.tensor.matmul(ps[:, 2 * (j % 2) + half, :], const("swap_q"),
                                             (qt[:, j, :] if j < 4 else kt[:])[:, half * 512:half * 512 + 512], start=True, stop=True)
                    m.then_inc(s.p_rq, 1)
                if f == FT_V + 1 or FT_MV + 1 <= f <= FT_MO:
                    j = 0 if f == FT_V + 1 else f - FT_MV
                    pe.wait_ge(s.a_ev, f)
                    pe.wait_ge(s.a_rq, 5)
                    if j >= 2:
                        pe.wait_ge(s.a_vt, j - 1)
                    for t in range(NT):
                        m = nc.tensor.transpose(pair(2 * ((j + 1) % 2))[:, t * P:(t + 1) * P],
                                                vtmp[:, (f - 1) % 2, t * P:(t + 1) * P], ident)
                    m.then_inc(s.p_vt, 1)

            pe.wait_ge(s.a_silu, 8)
            pe.wait_ge(s.a_ev, NFT)
            pe.wait_ge(s.a_vt, 5)
            pe.wait_ge(s.g_m1, 4)
            for c in range(NT):
                tok = slice(c * P, (c + 1) * P)
                mt = slice(4 + c * P, 4 + (c + 1) * P)
                if c >= 1:
                    pe.wait_ge(s.a_m2, 8 * c)
                    pe.wait_ge(s.a_m3, 4 * c)
                for h in range(MH):
                    nc.tensor.transpose(ps[:, 0, h * P:(h + 1) * P], mqk[:, 4 + h, mt], ident)
                for h in range(MH):
                    nc.tensor.matmul(ps[:, 1, h * P:(h + 1) * P], mqk[:, 4 + h, mt], mqk[:, h, mt], start=True, stop=True)
                for h in range(MH):
                    nc.tensor.matmul(ps[:, 2, h * P:(h + 1) * P], const("pick", c0=h * P, c1=(h + 1) * P), row_t[0:MH, tok],
                                     start=True, stop=False)
                    m = nc.tensor.matmul(ps[:, 2, h * P:(h + 1) * P], ident, const("future"), start=False, stop=True)
                m.then_inc(s.p_m1, 1)
                pe.wait_ge(s.g_m1, 5 + c)
                for h in range(MH):
                    o_ = (h % 2) * (MD + 1)
                    nc.tensor.matmul(ps[:, 3 + h // 2, o_:o_ + MD + 1], m_w[:, h, :], mvtok[:, c, h, :], start=True, stop=True)
                if c >= 1:
                    pe.wait_ge(s.g_m2, 6 * c)
                for h in range(MH):
                    o_ = (h % 2) * (MD + 1)
                    m = nc.tensor.matmul(ps[:, 5 + h // 2, o_:o_ + MD + 1], mqk[:, h, mt], state[:, h, :], start=True, stop=True)
                m.then_inc(s.p_m2, 1)
                for h in range(MH):
                    o_ = (h % 2) * (MD + 1)
                    m = nc.tensor.matmul(ps[:, (7, 0)[h // 2], o_:o_ + MD + 1], m_kw[:, h, :], mvtok[:, c, h, :], start=True, stop=True)
                m.then_inc(s.p_m2, 1)
                pe.wait_ge(s.a_hn, 4 * (c + 1))
                for h in range(MH):
                    m = nc.tensor.transpose(ps[:, 2, h * P:(h + 1) * P], m_hn[:, h, :], ident)
                m.then_inc(s.p_m3, 1)

            def scores(u):
                i, h = u // HEADS, u % HEADS
                w = P * (i + 1)
                if u >= 2:
                    pe.wait_ge(s.v_msk, u - 1)
                g = slice(HD * (h // 4), HD * (h // 4) + HD)
                for a in range(0, w, 512):
                    b = min(a + 512, w)
                    m = nc.tensor.matmul(pair(2 * (u % 2))[:, a:b], qt[g, h % 4, i * P:(i + 1) * P], kt[g, a:b], start=True, stop=True)
                m.then_inc(s.p_s, 1)

            pe.wait_ge(s.a_m3, 4 * NT)
            pe.wait_ge(s.a_m2, 8 * NT)
            pe.wait_ge(s.g_rq, 15)
            scores(0)
            for u in range(NT * HEADS):
                i, h = u // HEADS, u % HEADS
                if u + 1 < NT * HEADS:
                    scores(u + 1)
                pe.wait_ge(s.a_exp, u + 1)
                if u >= 1:
                    pe.wait_ge(s.a_pt, u)
                for j in range(i + 1):
                    m = nc.tensor.transpose(pair(4)[:, j * P:(j + 1) * P], a_p[:, u % 2, j * P:(j + 1) * P], ident)
                m.then_inc(s.p_pt, 1)
                if h == 1 and i >= 1:
                    pe.wait_ge(s.v_arow, i)
                    if i >= 2:
                        pe.wait_ge(s.a_at, i - 1)
                    for j in range(4):
                        m = nc.tensor.transpose(ps[:, 7, j * P:(j + 1) * P], arow[:, (i - 1) % 2, j * P:(j + 1) * P], ident)
                    m.then_inc(s.p_at, 1)
                pe.wait_ge(s.a_pt, u + 1)
                if h == 0 and i >= 1:
                    pe.wait_ge(s.v_arow, i)
                for j in range(i + 1):
                    m = nc.tensor.matmul(ps[:, 6, h * HD:(h + 1) * HD], a_t[:, u % 2, j, :],
                                         vtok[:, j, HD * (h // 4):HD * (h // 4) + HD], start=(j == 0), stop=(j == i))
                m.then_inc(s.p_pv, 1)
            pe.wait_ge(s.v_arow, NT)
            pe.wait_ge(s.a_at, NT - 1)
            for j in range(4):
                m = nc.tensor.transpose(ps[:, 7, j * P:(j + 1) * P], arow[:, (NT - 1) % 2, j * P:(j + 1) * P], ident)
            m.then_inc(s.p_at, 1)


            pe.wait_ge(s.a_at, NT)
            pe.wait_ge(s.g_wolo, KC)
            def out_proj(t):
                pe.wait_ge(s.v_mxlo, t + 1)
                if t >= 2:
                    pe.wait_ge(s.v_x2, t - 1)
                for half in range(2):
                    for c in range(KC):
                        cs = slice(half * 512, half * 512 + 512)
                        m = product(ps[:, 2 * (t % 2) + half, :], mx_hi[:, t % 2, c, :], mx_lo[:, t % 2, c, :],
                                    wo_hi[:, c, cs], wo_lo[:, c, cs], c == 0, c == KC - 1)
                m.then_inc(s.p_out, 1)

            def router(t):
                pe.wait_ge(s.v_h2, t + 1)
                if t >= 1:
                    pe.wait_ge(s.a_h2t, t)
                for c in range(KC):
                    m = nc.tensor.transpose(pair(4)[:, c * P:(c + 1) * P], h2[:, t % 2, c * P:(c + 1) * P], ident)
                m.then_inc(s.p_h2t, 1)
                pe.wait_ge(s.a_h2t, t + 1)
                if t >= 1:
                    pe.wait_ge(s.v_lg, 3 * t)
                else:
                    pe.wait_ge(s.ld_rw, 32)
                for c in range(KC):
                    m = nc.tensor.matmul(ps[:, 6, 0:E], h2t[:, t % 2, c, :], rw[:, c, :], start=(c == 0), stop=(c == KC - 1))
                m.then_inc(s.p_lg, 1)

            for t in range(NT + 1):
                if t < NT:
                    out_proj(t)
                if t >= 1:
                    router(t - 1)
            pe.wait_ge(s.v_dest, 5)
            for t in range(NT):
                for j in range(t + 1):
                    nc.tensor.matmul(ps[:, 7, t * E:(t + 1) * E], const("before") if j == t else const("ones"), chosen[:, j, :],
                                     start=(j == 0), stop=(j == t))
            for j in range(NT):
                m = nc.tensor.matmul(ps[:, 0, 0:E], const("ones"), chosen[:, j, :], start=(j == 0), stop=(j == NT - 1))
            m.then_inc(s.p_rank, 1)

            pe.wait_ge(s.v_dest, DEST_STEPS)
            nb = pe.value_load(nbi[0:1, 0:1], min_val=1, max_val=NBMAX)

            def x_transposes():
                for k in range(KC):
                    for h in range(2):
                        o_ = (k % 3) * ROWS + h * HALF
                        nc.tensor.transpose(ps[:, 4 + k // 3, o_:o_ + HALF], xg[0:HALF, h, k * P:(k + 1) * P], ident[0:HALF, 0:HALF])
                return nc.tensor.transpose(ps[:, 6, 2 * ROWS:2 * ROWS + 24], brow[0:24, :], ident[0:24, 0:24])

            def y_transposes():
                for q in range(4):
                    h, dq = q // 2, (q % 2) * 4
                    for d in range(4):
                        m = nc.tensor.transpose(ps[0:HALF, 4 + q, d * P:(d + 1) * P], yt[:, dq + d, h * HALF:(h + 1) * HALF], ident)
                    m.then_inc(s.p_yt, 1)

            pe.wait_ge(s.ld_xg, 32)
            pe.wait_ge(s.ld_b, 32)
            x_transposes().then_inc(s.p_xt, 1)
            pe.sem_inc(s.p_pc, 4)
            pe.wait_ge(s.p_pc, 4)
            with pe.Fori(0, nb) as i:
                def split_product(dst, m, g, k, moving, first, last):
                    nc.tensor.matmul(dst[:, 0:2 * ROWS], piece(e_whi, m)[:, k, g, :], moving[:, k, :, :].rearrange("p s n -> p (s n)"),
                                     start=first, stop=False, skip_group_check=True)
                    return nc.tensor.matmul(dst[:, 0:ROWS], piece(e_wlo, m)[:, k, g, :], moving[:, k, 0, :], start=False, stop=last,
                                            skip_group_check=True)

                def split(m):
                    pe.wait_ge(s.e_lo, i * PIECES + (m + 7))
                    pe.wait_ge(s.e_lop, i * PIECES + (m + 7))

                for f in range(8):
                    split(f)
                    if f == 0:
                        pe.wait_ge(s.e_xl, i * 2 + 2)
                    if f < 2:
                        pe.wait_ge(s.e_yd, i * 4 + (f + 3))
                    else:
                        pe.wait_ge(s.e_ev, i * 8 + (f - 1))
                    for g in range(2):
                        for k in range(KC):
                            m_ = split_product(ps[:, 2 * (f % 2) + g, :], f, g, k, e_x, k == 0, k == KC - 1)
                    m_.then_inc(s.p_pc, 1)
                    if f == 1:
                        pe.wait_ge(s.e_bd, i + 2)
                        pe.wait_ge(s.e_yr, i * 4 + 1)
                        y_transposes()
                pe.wait_ge(s.ld_xg, i * 32 + 64)
                pe.wait_ge(s.ld_b, i * 32 + 64)
                pe.wait_ge(s.e_yr, i * 4 + 5)
                x_transposes().then_inc(s.p_xt, 1)
                for j in range(4):
                    split(8 + j)
                    if j < 2:
                        pe.wait_ge(s.e_ev, i * 8 + (j + 7))
                    else:
                        pe.wait_ge(s.e_yd, i * 4 + (j + 3))
                    for part, ks in enumerate((range(0, 6), range(6, 8))):
                        if j == 0:
                            pe.wait_ge(s.e_al, i * 4 + (4 + part))
                        for g in range(2):
                            for k in ks:
                                m_ = split_product(ps[:, 2 * (j % 2) + g, :], 8 + j, g, k, e_a, k == 0, k == KC - 1)
                    m_.then_inc(s.p_pc, 1)
            pe.wait_ge(s.e_y, nb * 8 + 8)
            pe.wait_ge(s.e_bg, nb + 1)
            pe.wait_ge(s.e_yr, nb * 4 + 1)
            y_transposes()

        @block.vector
        def _(dve):
            dve.wait_ge(s.ld_const, 16)
            dve.wait_ge(s.ld_wn, 16)

            def ht_lo_of(t):
                dve.wait_ge(s.a_hthi, t + 1)
                lo = ht_lo[:, :, t * P:(t + 1) * P]
                nc.vector.tensor_tensor(lo, pair(2 * (t % 2)).rearrange("p (c n) -> p c n", c=KC),
                                        ht_hi[:, :, t * P:(t + 1) * P].bitcast(F32), ALU.subtract).then_inc(s.v_htlo, 1)

            for t in range(NT):
                dve.wait_ge(s.a_root, t + 1)
                nc.vector.reciprocal(rinv[:, t:t + 1], rstd[:, t:t + 1]).then_inc(s.v_rcp, 1)
                dve.wait_ge(s.v_rcp, t + 1)
                nc.vector.scalar_tensor_tensor(out=xn[:, t % 2, :], in0=xt[:, t % 2, :], scalar=rinv[:, t:t + 1],
                                               in1=wnb[:], op0=ALU.mult, op1=ALU.mult).then_inc(s.v_xn, 1)
                if t >= 1:
                    ht_lo_of(t - 1)
            ht_lo_of(NT - 1)

            dve.wait_ge(s.ld_rope, 16)
            for j in range(3):
                ft = iqt[:, j, :] if j < 2 else ikt[:]
                dve.wait_ge(s.p_ri, j + 1)
                if j >= 1:
                    dve.wait_ge(s.v_ra, j)
                nc.vector.tensor_tensor(rtmp[:], pair(2 * (j % 2)), rope_i[:, 1, :], ALU.mult).then_inc(s.v_rm, 1)
                nc.vector.tensor_tensor(ft, ft, rope_i[:, 0, :], ALU.mult).then_inc(s.v_rc, 1)
                dve.wait_ge(s.v_rm, j + 1)
                dve.wait_ge(s.v_rc, j + 1)
                nc.vector.tensor_tensor(ft, ft, rtmp[:], ALU.add).then_inc(s.v_ra, 1)

            gate = Steps(dve, s.v_gate)
            heads = slice(0, MH)

            def chunks(a):
                return a.rearrange("p (c n) -> p c n", c=NT)

            dve.wait_ge(s.a_gate, 5)
            dve.wait_ge(s.ld_gate, 48)
            dve.wait_ge(s.g_stack, 1)
            gate(nc.vector.scalar_tensor_tensor(out=row_f[heads, :], in0=row_f[heads, :], scalar=0.0,
                                                in1=row_t[heads, :], op0=ALU.min, op1=ALU.subtract))
            gate.done()
            gate(nc.vector.tensor_tensor_scan(row_b[heads, :], carry[heads, :], row_f[heads, :], 0.0, ALU.mult, ALU.add))
            gate(nc.vector.tensor_tensor_scan(mrow[heads, :], row_f[heads, :], row_i[heads, :], 0.0, ALU.add, ALU.max))
            gate.done()
            gate(nc.vector.tensor_tensor(stack[0:MH, :], row_i[heads, :], row_b[heads, :], ALU.subtract))
            gate(nc.vector.tensor_tensor(row_t[heads, :], row_b[heads, :], mrow[heads, :], ALU.subtract))
            gate(nc.vector.tensor_scalar(stack[96:96 + MH, :], mrow[heads, :], -1.0, None, ALU.mult))
            gate.done()
            gate(nc.vector.memset(row_b[heads, 0:1], 0.0))
            gate.done()
            gate(nc.vector.tensor_copy(row_b[heads, 1:NT], chunks(mrow[heads, :])[:, 0:NT - 1, P - 1]))
            gate.done()
            gate(nc.vector.tensor_tensor(chunks(stack[32:32 + MH, :]), chunks(row_t[heads, :]),
                                         row_b[heads, 0:NT].unsqueeze(2).to_broadcast([MH, NT, P]), ALU.add))
            gate(nc.vector.tensor_tensor(chunks(stack[64:64 + MH, :]), chunks(stack[0:MH, :]),
                                         chunks(row_t[heads, :])[:, :, P - 1:P].to_broadcast([MH, NT, P]), ALU.add))
            gate(nc.vector.tensor_tensor(mrow[heads, 0:NT], row_b[heads, 0:NT], chunks(row_t[heads, :])[:, :, P - 1], ALU.add))
            gate(nc.vector.memset(top8, 0.0))
            assert gate.n == 12

            dve.wait_ge(s.a_iwt, 1)
            for i in range(2, NT):
                sc = score[:, score_at[i]:score_at[i] + P * (i + 1)]
                for h in range(IH):
                    u = (i - 2) * IH + h
                    dve.wait_ge(s.a_relu, u + 1)
                    r = rbuf[:, u % 2, 0:P * (i + 1)]
                    if h == 0:
                        nc.vector.tensor_scalar(sc, r, iwc[:, i, 0:1], None, ALU.mult).then_inc(s.v_score, 1)
                    else:
                        dve.wait_ge(s.v_score, 9 * (i - 2) + h)
                        nc.vector.scalar_tensor_tensor(out=sc, in0=r, scalar=iwc[:, i, h:h + 1], in1=sc,
                                                       op0=ALU.mult, op1=ALU.add).then_inc(s.v_score, 1)
                dve.wait_ge(s.v_score, 9 * (i - 2) + 8)
                nc.vector.tensor_tensor(sc[:, i * P:(i + 1) * P], sc[:, i * P:(i + 1) * P], const("unseen"),
                                        ALU.add).then_inc(s.v_score, 1)
            dve.wait_ge(s.p_mcol, 1)
            nc.vector.tensor_copy(mcol, pair(2).rearrange("p (c k n) -> p c k n", c=NT, k=4)[:, :, :, 0:MH]).then_inc(s.v_mcol, 1)

            dve.wait_ge(s.v_score, 54)
            n = 0
            for i in range(2, NT, 2):
                sc = [score[:, score_at[j]:score_at[j] + P * (j + 1)] for j in (i, i + 1)]
                for it in range(TOPK // 8):
                    for k in range(2):
                        if n:
                            dve.wait_ge(s.v_topk, n - 1)
                        nc.vector.max(top8[:, k, :], sc[k]).then_inc(s.v_topk, 1)
                        n += 1
                    for k in range(2):
                        dve.wait_ge(s.v_topk, n - 1)
                        nc.vector.match_replace(sc[k], top8[:, k, :], sc[k], GONE).then_inc(s.v_topk, 1)
                        n += 1
                for k in range(2):
                    dve.wait_ge(s.v_topk, n - 1 + k)
                    nc.vector.tensor_scalar(sc[k], sc[k], GONE / 2, NEG, ALU.is_gt, ALU.mult).then_inc(s.v_mask, 1)
            def normalize(i):
                dve.wait_ge(s.a_exp, HEADS * (i + 1))
                if i >= 1:
                    dve.wait_ge(s.v_arow, i)
                nc.vector.reciprocal(rsi, rs[:, (i % 2) * 8:(i % 2) * 8 + 8]).then_inc(s.v_rs, 1)
                dve.wait_ge(s.v_rs, i + 1)
                dve.wait_ge(s.p_pv, HEADS * (i + 1))
                if i >= 2:
                    dve.wait_ge(s.p_at, i - 1)
                nc.vector.tensor_tensor(arow[:, i % 2, :].rearrange("p (h n) -> p h n", h=HEADS),
                                        ps[:, 6, :].rearrange("p (h n) -> p h n", h=HEADS),
                                        rsi.unsqueeze(2).to_broadcast([P, HEADS, HD]), ALU.mult).then_inc(s.v_arow, 1)

            for u in range(NT * HEADS):
                i, h = u // HEADS, u % HEADS
                w = P * (i + 1)
                dve.wait_ge(s.p_s, u + 1)
                if u >= 2:
                    dve.wait_ge(s.a_exp, u - 1)
                src, dst = pair(2 * (u % 2))[:, 0:w], a_s[:, u % 2, 0:w]
                if i >= 2:
                    dve.wait_ge(s.v_mask, i - 1)
                    nc.vector.tensor_tensor_reduce(dst, src, score[:, score_at[i]:score_at[i] + w], 1.0, GONE,
                                                   ALU.add, ALU.max, mx[:, u % 2:u % 2 + 1]).then_inc(s.v_msk, 1)
                else:
                    nc.vector.tensor_tensor_reduce(dst, src, seen[:, P - P * i:2 * P], 1.0, GONE,
                                                   ALU.add, ALU.max, mx[:, u % 2:u % 2 + 1]).then_inc(s.v_msk, 1)
                dve.wait_ge(s.v_msk, u + 1)
                nc.vector.tensor_scalar(nmx[:, u % 2:u % 2 + 1], mx[:, u % 2:u % 2 + 1], -HD ** -0.5, None, ALU.mult).then_inc(s.v_nm, 1)
                if h == 1 and i >= 1:
                    normalize(i - 1)
            normalize(NT - 1)

            def x2_of(t):
                dve.wait_ge(s.p_out, t + 1)
                dve.wait_ge(ld_r[t % 2], 16 * (t // 2 + 1))
                if t >= 2:
                    dve.wait_ge(st_x[t % 2], 16 * (t // 2))
                    dve.wait_ge(s.v_h2, t - 1)
                nc.vector.tensor_tensor(x2[:, t % 2, :], pair(2 * (t % 2)), xr[:, t % 2, :], ALU.add).then_inc(s.v_x2, 1)

            def h2_of(t):
                dve.wait_ge(s.a_root2, t + 1)
                nc.vector.reciprocal(rinv[:, t:t + 1], rstd[:, t:t + 1]).then_inc(s.v_rcp2, 1)
                dve.wait_ge(s.v_rcp2, t + 1)
                nc.vector.scalar_tensor_tensor(out=h2[:, t % 2, :], in0=x2[:, t % 2, :], scalar=rinv[:, t:t + 1],
                                               in1=wn2[:], op0=ALU.mult, op1=ALU.mult).then_inc(s.v_h2, 1)

            def route(t):
                dve.wait_ge(s.p_lg, t + 1)
                nc.vector.tensor_tensor(lg, ps[:, 6, 0:E], rb[:], ALU.add).then_inc(s.v_lg, 1)
                dve.wait_ge(s.v_lg, 3 * t + 1)
                nc.vector.max(best[:, t, :], lg).then_inc(s.v_lg, 1)
                dve.wait_ge(s.v_lg, 3 * t + 2)
                nc.vector.max_index(besti[:, t, :], best[:, t, :], lg).then_inc(s.v_lg, 1)
                dve.wait_ge(s.v_lg, 3 * t + 3)

            dve.wait_ge(s.ld_wn2, 16)
            dve.wait_ge(s.ld_rw, 32)
            for t in range(NT + 1):
                if t < NT:
                    dve.wait_ge(s.a_mxhi, t + 1)
                    nc.vector.tensor_tensor(mx_lo[:, t % 2, :, :], mixt[:, :, t * P:(t + 1) * P], mx_hi[:, t % 2, :, :].bitcast(F32),
                                            ALU.subtract).then_inc(s.v_mxlo, 1)
                if t >= 1:
                    x2_of(t - 1)
                    h2_of(t - 1)
                    route(t - 1)
            r = Steps(dve, s.v_route)
            r(nc.vector.tensor_tensor(gates, best[:, :, 0:TOP], best[:, :, 0:1].to_broadcast([P, NT, TOP]), ALU.subtract))
            r(nc.vector.tensor_copy(bestf, besti))
            r.done()
            for k in range(TOP):
                m_ = nc.vector.tensor_tensor(oneh[:, k], const("experts").unsqueeze(1).to_broadcast([P, NT, E]),
                                             bestf[:, :, k:k + 1].to_broadcast([P, NT, E]), ALU.is_equal)
                if k == TOP - 1:
                    r(m_)
                else:
                    m_.then_inc(s.v_dest, 1)
            d = Steps(dve, s.v_dest)
            d.n = TOP - 1
            r.done()
            r(nc.vector.tensor_tensor(chosen[:], oneh[:, 0], oneh[:, 1], ALU.add))
            d(nc.vector.tensor_tensor(prod[:], oneh[:, 2], oneh[:, 3], ALU.add))
            r.done()
            d.done()
            d(nc.vector.tensor_tensor(chosen[:], chosen[:], prod[:], ALU.add))
            d.done()
            dve.wait_ge(s.a_gexp, 1)
            d(nc.vector.tensor_reduce(gsum, gates, AX.X, ALU.add))
            d.done()
            d(nc.vector.reciprocal(gsum, gsum))
            d.done()
            d(nc.vector.tensor_tensor(gates, gates, gsum.unsqueeze(2).to_broadcast([P, NT, TOP]), ALU.mult))
            dve.wait_ge(s.p_rank, 1)
            d(nc.vector.tensor_copy(counts, ps[:, 0, 0:E]))
            d.done()
            d(nc.vector.tensor_tensor(stepc[:], counts.unsqueeze(2).to_broadcast([P, E, CAPT]),
                                      const("steps").unsqueeze(1).to_broadcast([P, E, CAPT]), ALU.is_gt))
            d.done()
            d(nc.vector.tensor_reduce(nblk, stepc[:], AX.X, ALU.add))
            d.done()
            d(nc.vector.tensor_tensor_scan(bend, const("ones", c1=E), nblk, 0.0, ALU.mult, ALU.add))
            d.done()
            d(nc.vector.tensor_tensor(bstart, bend, nblk, ALU.subtract))
            d(nc.vector.tensor_scalar(counts, bend, const("row"), None, ALU.is_le))
            d(nc.vector.tensor_copy(nbi, bend[:, E - 1:E]))
            d.done()
            d(nc.vector.tensor_reduce(bef, counts, AX.X, ALU.add))
            d(nc.vector.tensor_scalar(bstart, bstart, float(ROWS), None, ALU.mult))
            d.done()
            d(nc.vector.tensor_scalar(bei, bef, float(E - 1), None, ALU.min))
            d(nc.vector.tensor_tensor(place[:], ps[:, 7, 0:NT * E].rearrange("p (t e) -> p t e", t=NT),
                                      bstart.unsqueeze(1).to_broadcast([P, NT, E]), ALU.add))
            for k in range(TOP):
                d.done()
                d(nc.vector.tensor_tensor(prod[:], oneh[:, k], place[:], ALU.mult))
                d.done()
                d(nc.vector.tensor_reduce(destf[:, :, k], prod[:], AX.X, ALU.add))
            d.done()
            d(nc.vector.tensor_copy(desti, destf))
            assert d.n == DEST_STEPS, d.n
            d.done()

            nb = dve.value_load(nbi[0:1, 0:1], min_val=1, max_val=NBMAX)

            def x_lo(n):
                dve.wait_ge(s.e_xh, 2 * n)
                nc.vector.tensor_tensor(e_x[:, 0:6, 1, :].rearrange("p (b k) n -> p b k n", b=2),
                                        ps[:, 4:6, 0:3 * ROWS].rearrange("p b (k n) -> p b k n", k=3),
                                        e_x[:, 0:6, 0, :].rearrange("p (b k) n -> p b k n", b=2).bitcast(F32), ALU.subtract).then_inc(s.e_xl, 1)
                nc.vector.tensor_tensor(e_x[:, 6:8, 1, :], ps[:, 6, 0:2 * ROWS].rearrange("p (k n) -> p k n", k=2),
                                        e_x[:, 6:8, 0, :].bitcast(F32), ALU.subtract).then_inc(s.e_xl, 1)
                nc.vector.tensor_copy(bgu[:], ps[:, 6, 2 * ROWS:2 * ROWS + 16]).then_inc(s.e_bg, 1)

            def gather_rows(n):
                dve.wait_ge(s.ld_idx, n * 16)
                nc.vector.tensor_scalar(gidx[0:HALF, :], idx[0:HALF, :], TOP.bit_length() - 1, None, ALU.logical_shift_right).then_inc(s.e_gx, 1)

            def y_sums(i, m):
                dve.wait_ge(s.p_pc, i * PIECES + (m + 1))
                nc.vector.tensor_reduce(yt[:, 2 * m:2 * m + 2, :], sums_of(m), AX.X, ALU.add).then_inc(s.e_yd, 1)

            dve.wait_ge(s.ld_scur, 16)
            nc.vector.memset(bdn[:], 0.0).then_inc(s.e_bd, 1)
            dve.sem_inc(s.e_lo, 6)
            dve.sem_inc(s.e_al, 1)
            dve.sem_inc(s.e_ix, 1)
            dve.wait_ge(s.e_lo, 6)
            dve.wait_ge(s.e_al, 1)
            dve.wait_ge(s.e_ix, 1)
            gather_rows(1)
            x_lo(1)
            with dve.Fori(0, nb) as i:
                def split_lo(m):
                    dve.wait_ge(s.e_hi, i * PIECES + (m + 1))
                    ks = slice(0, KDVE)
                    nc.vector.tensor_tensor(piece(e_wlo, m)[:, ks], raw_piece(m)[:, ks], piece(e_whi, m)[:, ks].bitcast(F32),
                                            ALU.subtract).then_inc(s.e_lo, 1)

                def evacuate_gu(f):
                    dve.wait_ge(s.p_pc, i * PIECES + (f + 5))
                    nc.vector.tensor_reduce(esum[:, f % 2], sums_of(f), AX.X, ALU.add).then_inc(s.e_ev, 1)
                    dve.wait_ge(s.e_ev, i * 8 + (f + 1))
                    for g, dst in enumerate((gl, ul)):
                        nc.vector.tensor_scalar(dst[:, f // 2 % 2, f % 2, :], esum[:, f % 2, g, :], bgu[:, 8 * g + f:8 * g + f + 1],
                                                LIMIT, ALU.add, ALU.min).then_inc(s.e_mn, 1)

                def act_of(q):
                    dve.wait_ge(s.e_mn, i * 16 + 4 * (q + 1))
                    nc.vector.tensor_scalar(ul[:, q % 2], ul[:, q % 2], -LIMIT, 1.0, ALU.max, ALU.add).then_inc(s.e_cl, 1)
                    dve.wait_ge(s.e_cl, i * 4 + (q + 1))
                    nc.vector.tensor_tensor(tt[:, q % 2], ul[:, q % 2], gl[:, q % 2], ALU.mult).then_inc(s.e_t, 1)
                    dve.wait_ge(s.e_t, i * 4 + (q + 1))
                    dve.wait_ge(s.e_sg, i * 4 + (q + 1))
                    dve.wait_ge(s.e_al, i * 4 + max(q, 1))
                    nc.vector.tensor_tensor(af[:, q % 2], tt[:, q % 2], sg[:, q % 2], ALU.mult).then_inc(s.e_act, 1)

                def a_lo(q):
                    dve.wait_ge(s.e_ah, i * 4 + (q + 1))
                    nc.vector.tensor_tensor(e_a[:, 2 * q:2 * q + 2, 1, :], af[:, q % 2], e_a[:, 2 * q:2 * q + 2, 0, :].bitcast(F32),
                                            ALU.subtract).then_inc(s.e_al, 1)

                for m in range(4):
                    y_sums(i, m)
                    split_lo(m)
                dve.wait_ge(s.st_y, i * 32 + 32)
                dve.wait_ge(s.e_ix, i * 2 + 1)
                nc.vector.tensor_copy(slast[0:HALF, :], scur[0:HALF, :]).then_inc(s.e_ix, 1)
                dve.wait_ge(s.ld_idx, i * 16 + 16)
                dve.wait_ge(s.e_ix, i * 2 + 2)
                nc.vector.tensor_copy(scur[0:HALF, :], idx[0:HALF, :]).then_inc(s.e_ix, 1)
                dve.wait_ge(s.e_bg, i + 1)
                for q in range(4):
                    evacuate_gu(2 * q)
                    if q:
                        a_lo(q - 1)
                    split_lo(2 * q + 4)
                    evacuate_gu(2 * q + 1)
                    if q < 3:
                        split_lo(2 * q + 5)
                    act_of(q)
                    if q == 0:
                        dve.wait_ge(s.ld_xg, i * 32 + 32)
                        gather_rows(i + 2)
                a_lo(3)
                split_lo(11)
                x_lo(i + 2)
            for m in range(4):
                y_sums(nb, m)

            dve.wait_ge(s.ld_wn3, 16)
            for t in range(NT):
                dve.wait_ge(ld_y[t % 2], 16 * (t // 2 + 1))
                dve.wait_ge(ld_x3[t % 2], 16 * (t // 2 + 1))
                for k in range(TOP):
                    if k:
                        dve.wait_ge(s.v_sum, 4 * t + k)
                    nc.vector.scalar_tensor_tensor(out=x3[:, t % 2, :], in0=yg[:, t % 2, k, :], scalar=gates[:, t, k:k + 1],
                                                   in1=x3[:, t % 2, :], op0=ALU.mult, op1=ALU.add).then_inc(s.v_sum, 1)
                dve.wait_ge(s.a_sq3, 2 * t + 2)
                nc.vector.reciprocal(rinv[:, t:t + 1], rstd[:, t:t + 1]).then_inc(s.v_rcp3, 1)
                dve.wait_ge(s.v_rcp3, t + 1)
                nc.vector.scalar_tensor_tensor(out=ot[:, t % 2, :], in0=x3[:, t % 2, :], scalar=rinv[:, t:t + 1],
                                               in1=wn3[:], op0=ALU.mult, op1=ALU.mult).then_inc(s.v_o, 1)
        bctx.close()


_INS = ['x', 'mix_norm_w', 'w_in', 'conv_w', 'conv_b', 'igate_b', 'fgate_b', 'mlstm_norm_w', 'w_out', 'ffn_norm_w',
        'router_w', 'router_b', 'w_gate_up', 'b_gate_up', 'w_down', 'b_down', 'final_norm_w']


def kernel(**inputs):
    import numpy as _np
    import concourse.bacc as _bacc
    from concourse import mybir as _mybir
    from concourse.bass_utils import run_bass_kernel_spmd as _run

    nc = _bacc.Bacc("TRN2", target_bir_lowering=False, num_devices=1)
    held = {name: _np.ascontiguousarray(inputs[name]) for name in _INS}
    held["c_const"], held["c_carry"], held["c_slots"] = CONST_ARRAY, CARRY, unused_slots()
    held["c_rope_q"], held["c_rope_i"] = rope_tables(HD, HD // 4), rope_tables(ID, ID // 4)
    arrays = {f"in_{name}_dram": a for name, a in held.items()}
    I = {name: nc.dram_tensor(f"in_{name}_dram", a.shape, _mybir.dt.from_np(a.dtype), kind="ExternalInput").ap()
         for name, a in held.items()}
    out = nc.dram_tensor("out_0_dram", (1, T, D), F32, kind="ExternalOutput").ap()
    build(nc, I, out)
    r = _run(nc, [arrays], core_ids=[0])
    return r.results[0]["out_0_dram"]
```

```python
from contextlib import ExitStack

import numpy as np

import concourse.bass as bass
from concourse import mybir

F32 = mybir.dt.float32
F32R = mybir.dt.float32r
I32 = mybir.dt.int32
U32 = mybir.dt.uint32
ALU = mybir.AluOpType
ACT = mybir.ActivationFunctionType
AX = mybir.AxisListType

P = 128
T = 1024
D = 1024
NT = T // P
KC = D // P
EPS = 1e-6
CHUNK = 64

HEADS, HD, KVH = 8, 64, 2
IH, ID = 8, 32
TOPK = 256
MH, MD = 4, 128
CONV = 4
E, TOP = 32, 4
FE = 1024
ALPHA, LIMIT = 1.702, 7.0

C_AQ, C_AK, C_AV, C_IQ, C_IK, C_IW = 0, 512, 640, 768, 1024, 1056
C_MQ, C_MK, C_MV, C_MI, C_MF, C_MO = 1064, 1576, 2088, 2600, 2604, 2608

NEG = -1.0e30
GONE = -3.0e38

HALF = 72
ROWS = 2 * HALF
NBMAX = E + (T * TOP - E) // ROWS + 1
TOKW = HALF
assert P * TOKW >= (NBMAX + 1) * ROWS
PIECES = 12
KDVE = 4
CAPT = -(-T // ROWS)

FT_IQ, FT_IK, FT_SMALL, FT_Q, FT_K, FT_V, FT_MQK, FT_MV, FT_MO, NFT = 0, 2, 3, 4, 8, 9, 10, 18, 22, 26


def feature_tiles():
    tiles = [[(0, C_IQ, P)], [(0, C_IQ + P, P)]]
    tiles += [[(ID * r, C_IK, ID) for r in range(4)]]
    tiles += [[(0, C_MI, MH), (32, C_MF, MH), (64, C_IW, IH)]]
    tiles += [[(0, C_AQ + HD * j, HD), (HD, C_AQ + HD * (j + 4), HD)] for j in range(4)]
    tiles += [[(0, C_AK, P)], [(0, C_AV, P)]]
    tiles += [[(0, C_MQ + P * j, P)] for j in range(4)] + [[(0, C_MK + P * j, P)] for j in range(4)]
    tiles += [[(0, C_MV + P * j, P)] for j in range(4)] + [[(0, C_MO + P * j, P)] for j in range(4)]
    return tiles


CONST = {}


def constants():
    parts, at = [], 0

    def put(name, a):
        nonlocal at
        full = np.zeros((P, a.shape[1]), np.float32)
        full[: a.shape[0]] = a
        CONST[name] = (at, a.shape[0], a.shape[1])
        parts.append(full)
        at += a.shape[1]

    i = np.arange(P)
    put("ident", np.eye(P, dtype=np.float32))
    put("ones", np.ones((P, P), np.float32))
    put("before", (i[:, None] < i[None, :]).astype(np.float32))
    put("future", np.where(i[:, None] <= i[None, :], 0.0, NEG).astype(np.float32))
    put("seen", np.zeros((P, P), np.float32))
    put("unseen", np.where(i[None, :] // CHUNK <= i[:, None] // CHUNK, 0.0, NEG).astype(np.float32))

    def swap(period, half):
        m = np.zeros((P, P), np.float32)
        for base in range(0, P, period):
            for a in range(half):
                m[base + a + half, base + a] = -1.0
                m[base + a, base + a + half] = 1.0
        return m

    put("swap_q", swap(HD, HD // 8))
    put("swap_i", swap(ID, ID // 8))
    sel = np.zeros((MH, MH * P), np.float32)
    for h in range(MH):
        sel[h, h * P:(h + 1) * P] = 1.0
    put("pick", sel)
    put("experts", np.tile(np.arange(E, dtype=np.float32), (P, 1)))
    put("row", i[:, None].astype(np.float32))
    put("steps", np.tile(np.arange(CAPT, dtype=np.float32) * ROWS, (P, 1)))
    carry = np.ones((MH, T), np.float32)
    carry[:, ::P] = 0.0
    return np.concatenate(parts, 1), carry


def rope_tables(period, rot):
    pos = np.arange(T, dtype=np.float32)
    freq = (np.float32(500000.0) ** (-np.arange(0, rot, 2, dtype=np.float32) / np.float32(rot))).astype(np.float32)
    ang = pos[:, None] * freq[None, :]
    c, s = np.ones((P, T), np.float32), np.zeros((P, T), np.float32)
    for base in range(0, P, period):
        for a in range(rot):
            c[base + a] = np.cos(ang[:, a % (rot // 2)])
            s[base + a] = np.sin(ang[:, a % (rot // 2)])
    return np.stack([c, s], 1)


def unused_slots():
    q = np.arange(P * TOKW) % ROWS
    return (T * TOP + q).astype(np.int32).reshape(P, TOKW)


CONST_ARRAY, CARRY = constants()
CW = CONST_ARRAY.shape[1]


COLS = 1152
DEST_STEPS = 28


class Steps:

    def __init__(self, eng, sem):
        self.eng, self.sem, self.n = eng, sem, 0

    def __call__(self, ins):
        ins.then_inc(self.sem, 1)
        self.n += 1
        return self.n

    def done(self, back=0):
        if self.n > back:
            self.eng.wait_ge(self.sem, self.n - back)


class Semaphores:

    def __init__(self, sem):
        self.ld_const = sem("ld_const")
        self.ld_x0 = sem("ld_x0")
        self.ld_x1 = sem("ld_x1")
        self.ld_wn = sem("ld_wn")
        self.ld_w0 = sem("ld_w0")
        self.ld_w1 = sem("ld_w1")
        self.ld_gate = sem("ld_gate")
        self.ld_rope = sem("ld_rope")
        self.ld_small = sem("ld_small")
        self.a_square = sem("a_square")
        self.a_root = sem("a_root")
        self.a_hthi = sem("a_hthi")
        self.v_rcp = sem("v_rcp")
        self.v_xn = sem("v_xn")
        self.v_htlo = sem("v_htlo")
        self.p_ht = sem("p_ht")
        self.a_whi = sem("a_whi")
        self.g_wlo = sem("g_wlo")
        self.p_ft = sem("p_ft")
        self.a_ev = sem("a_ev")
        self.g_pad = sem("g_pad")
        self.p_ri = sem("p_ri")
        self.v_rm = sem("v_rm")
        self.v_rc = sem("v_rc")
        self.v_ra = sem("v_ra")
        self.a_iqhi = sem("a_iqhi")
        self.g_iqz = sem("g_iqz")
        self.v_iqlo = sem("v_iqlo")
        self.a_gate = sem("a_gate")
        self.v_gate = sem("v_gate")
        self.g_stack = sem("g_stack")
        self.p_iwt = sem("p_iwt")
        self.a_iwt = sem("a_iwt")
        self.p_is = sem("p_is")
        self.a_relu = sem("a_relu")
        self.v_score = sem("v_score")
        self.v_topk = sem("v_topk")
        self.v_mask = sem("v_mask")
        self.p_mcol = sem("p_mcol")
        self.v_mcol = sem("v_mcol")
        self.a_mexp = sem("a_mexp")
        self.p_decay = sem("p_decay")
        self.a_decay = sem("a_decay")
        self.p_rq = sem("p_rq")
        self.a_rq = sem("a_rq")
        self.g_rq = sem("g_rq")
        self.p_vt = sem("p_vt")
        self.a_vt = sem("a_vt")
        self.st_mo0 = sem("st_mo0")
        self.st_mo1 = sem("st_mo1")
        self.g_ones = sem("g_ones")
        self.g_conv = sem("g_conv")
        self.a_silu = sem("a_silu")
        self.ld_mo0 = sem("ld_mo0")
        self.ld_mo1 = sem("ld_mo1")
        self.g_m1 = sem("g_m1")
        self.p_s1 = sem("p_s1")
        self.a_s1 = sem("a_s1")
        self.g_w = sem("g_w")
        self.p_nd = sem("p_nd")
        self.a_nd = sem("a_nd")
        self.p_in = sem("p_in")
        self.a_in = sem("a_in")
        self.g_n = sem("g_n")
        self.p_up = sem("p_up")
        self.a_up = sem("a_up")
        self.g_st = sem("g_st")
        self.a_abs = sem("a_abs")
        self.g_h = sem("g_h")
        self.a_sq = sem("a_sq")
        self.g_rs = sem("g_rs")
        self.a_mt = sem("a_mt")
        self.a_hn = sem("a_hn")
        self.p_m3 = sem("p_m3")
        self.g_mix = sem("g_mix")
        self.p_s = sem("p_s")
        self.v_msk = sem("v_msk")
        self.v_nm = sem("v_nm")
        self.a_exp = sem("a_exp")
        self.p_pt = sem("p_pt")
        self.a_pt = sem("a_pt")
        self.p_pv = sem("p_pv")
        self.v_rs = sem("v_rs")
        self.v_arow = sem("v_arow")
        self.p_at = sem("p_at")
        self.a_at = sem("a_at")
        self.a_qkhi = sem("a_qkhi")
        self.g_qz = sem("g_qz")
        self.v_qklo = sem("v_qklo")
        self.a_wohi = sem("a_wohi")
        self.g_wolo = sem("g_wolo")
        self.a_mxhi = sem("a_mxhi")
        self.v_mxlo = sem("v_mxlo")
        self.p_out = sem("p_out")
        self.v_x2 = sem("v_x2")
        self.st_x0 = sem("st_x0")
        self.st_x1 = sem("st_x1")
        self.v_h2 = sem("v_h2")
        self.st_h0 = sem("st_h0")
        self.st_h1 = sem("st_h1")
        self.p_h2t = sem("p_h2t")
        self.a_h2t = sem("a_h2t")
        self.p_lg = sem("p_lg")
        self.v_lg = sem("v_lg")
        self.ld_rw = sem("ld_rw")
        self.v_route = sem("v_route")
        self.a_gexp = sem("a_gexp")
        self.p_rank = sem("p_rank")
        self.v_dest = sem("v_dest")
        self.ld_scur = sem("ld_scur")
        self.st_zero = sem("st_zero")
        self.g_tok = sem("g_tok")
        self.st_tok = sem("st_tok")
        self.st_be = sem("st_be")
        self.passed = sem("passed")
        self.ld_idx = sem("ld_idx")
        self.ld_b = sem("ld_b")
        self.ld_g0 = sem("ld_g0")
        self.ld_g1 = sem("ld_g1")
        self.ld_g2 = sem("ld_g2")
        self.e_hi = sem("e_hi")
        self.e_lo = sem("e_lo")
        self.e_lop = sem("e_lop")
        self.p_pc = sem("p_pc")
        self.e_ev = sem("e_ev")
        self.e_mn = sem("e_mn")
        self.e_cl = sem("e_cl")
        self.e_yd = sem("e_yd")
        self.e_t = sem("e_t")
        self.e_sg = sem("e_sg")
        self.e_act = sem("e_act")
        self.e_ah = sem("e_ah")
        self.e_al = sem("e_al")
        self.e_y = sem("e_y")
        self.p_xt = sem("p_xt")
        self.e_xh = sem("e_xh")
        self.e_xl = sem("e_xl")
        self.e_bg = sem("e_bg")
        self.e_bd = sem("e_bd")
        self.p_yt = sem("p_yt")
        self.e_yr = sem("e_yr")
        self.st_y = sem("st_y")
        self.ld_xg = sem("ld_xg")
        self.st_hx = sem("st_hx")
        self.e_gx = sem("e_gx")
        self.e_ix = sem("e_ix")
        self.g_y = sem("g_y")
        self.ld_y0 = sem("ld_y0")
        self.ld_y1 = sem("ld_y1")
        self.v_sum = sem("v_sum")
        self.a_sq3 = sem("a_sq3")
        self.v_o = sem("v_o")
        self.st_o0 = sem("st_o0")
        self.st_o1 = sem("st_o1")


def build(nc, I, out):
    def scratch(name, shape, dt):
        return nc.dram_tensor(name, shape, dt, kind="Internal").ap()

    with ExitStack() as ctx:
        base = nc.sbuf_base
        base += -base % 64
        limit = nc.sbuf_usable_end
        used = {}

        def at(name, offset, shape, dt=F32):
            n = 4 * int(np.prod(shape[1:]))
            assert base + offset + n <= limit, (name, offset, n, limit - base)
            used[name] = (offset, offset + n)
            return nc.alloc_sbuf_tensor_at(name, shape, dt, offset=base + offset)

        def sem(name):
            return ctx.enter_context(nc.semaphore(name))

        KB = 1024
        cst = at("cst", 0, [P, CW])
        small0 = 4 * CW + (-4 * CW) % 64
        cols = at("cols", small0, [P, COLS])
        o = small0 + 4 * COLS
        R0 = o

        def const(name, p0=0, p1=None, c0=0, c1=None):
            a, rows, w = CONST[name]
            return cst[p0:rows if p1 is None else p1, a + c0:a + (w if c1 is None else c1)]

        ident = const("ident")
        seen = cst[:, CONST["seen"][0]:CONST["seen"][0] + 2 * P]
        taken = [0]

        def column(n):
            a = taken[0]
            taken[0] += n
            assert taken[0] <= COLS
            return cols[:, a:a + n]

        ss, rstd, rinv = column(NT), column(NT), column(NT)
        iwc = column(NT * IH).rearrange("p (t h) -> p t h", t=NT)
        igb, fgb = column(1), column(1)
        convw = column(8 * CONV).rearrange("p (f k) -> p f k", f=8)
        convb, mnw = column(8), column(MH)
        top8 = column(16).rearrange("p (k e) -> p k e", k=2)
        mcol = column(NT * 16).rearrange("p (c k h) -> p c k h", c=NT, k=4)
        mexp = column(NT * 12).rearrange("p (c k h) -> p c k h", c=NT, k=3)
        decay = column(MH * NT).rearrange("p (h c) -> p h c", h=MH)
        mx, nmx, rs, rsi = column(2), column(2), column(16), column(HEADS)
        den, hss, hrs = column(NT * MH), column(NT * MH), column(NT * MH)
        den = den.rearrange("p (c h) -> p c h", c=NT)

        H0 = R0
        W0 = H0 + 64 * KB
        Q0 = W0 + 24 * KB
        M0 = Q0 + 24 * KB
        MVB = 4 * NT * MH * (MD + 1)
        V0 = M0 + 4 * 8 * (T + 4)
        S0 = V0 + MVB
        SCW = sum(P * (i + 1) for i in range(2, NT))
        X0 = S0 + 4 * SCW
        G0 = X0 + 12 * KB

        ht_hi = at("ht_hi", H0, [P, KC, T], F32R)
        ht_lo = at("ht_lo", H0 + 32 * KB, [P, KC, T], F32R)
        w_raw = at("w_raw", W0, [P, 2, KC, P])
        w_hi = at("w_hi", W0 + 8 * KB, [P, 2, KC, P], F32R)
        w_lo = at("w_lo", W0 + 16 * KB, [P, 2, KC, P], F32R)
        qt = at("qt", Q0, [P, 4, T])
        kt = at("kt", Q0 + 16 * KB, [P, T])
        vtok = at("vtok", Q0 + 20 * KB, [P, NT, P])
        xt = at("xt", Q0, [P, 2, D])
        xn = at("xn", Q0 + 8 * KB, [P, 2, D])
        wnb = at("wnb", Q0 + 16 * KB, [P, D])
        mqk = at("mqk", M0, [P, 8, T + 4])
        rbuf = at("rbuf", M0, [P, 2, T])
        mvtok = at("mvtok", V0, [P, NT, MH, MD + 1])
        rope_i = at("rope_i", V0, [P, 2, T])
        rtmp = at("rtmp", V0 + 8 * KB, [P, T])
        score = at("score", S0, [P, SCW])
        iqt = at("iqt", X0, [P, 2, T])
        ikt = at("ikt", X0 + 8 * KB, [P, T])
        iq_hi = at("iq_hi", Q0, [P, 2, IH, P], F32R)
        iq_lo = at("iq_lo", Q0 + 8 * KB, [P, 2, IH, P], F32R)
        ik_hi = at("ik_hi", Q0 + 16 * KB, [P, T], F32R)
        ik_lo = at("ik_lo", Q0 + 20 * KB, [P, T], F32R)
        rope_q = at("rope_q", X0, [P, 2, T])
        qtmp = at("qtmp", X0 + 8 * KB, [P, T])
        row_i = at("row_i", M0 + 24 * KB, [P, T])
        row_f = at("row_f", M0 + 28 * KB, [P, T])
        row_t = at("row_t", G0, [P, T])
        row_b = at("row_b", V0 + 12 * KB, [P, T])
        iwt = at("iwt", M0 + 8 * KB, [P, T])
        vtmp = at("vtmp", X0, [P, 2, T])
        stack = at("stack", M0 + 12 * KB, [P, T])
        mrow = at("mrow", M0 + 16 * KB, [P, T])
        carry = at("carry", M0 + 20 * KB, [P, T])
        negm = row_t

        cmul = at("cmul", X0 + 8 * KB, [P, T])
        ctmp = at("ctmp", G0 + 4 * KB, [P, T])
        mixt = at("mixt", H0, [P, KC, T])
        HW = MH * (MD + 1)
        m_kw = at("m_kw", W0 + 18 * KB, [P, 2, MH, P])
        m_sc = at("m_sc", W0 + 2 * KB, [P, MH, P])
        m_ex = at("m_ex", W0 + 4 * KB, [P, MH, P])
        m_w = at("m_w", W0 + 6 * KB, [P, MH, P])
        m_h = at("m_h", W0 + 8 * KB, [P, MH, P])
        m_hn = at("m_hn", W0 + 10 * KB, [P, MH, P])
        m_mt = at("m_mt", W0 + 12 * KB, [P, MH, P])
        m_o = at("m_o", W0 + 14 * KB, [P, 2, MH, P])
        m_in = at("m_in", H0 + 32 * KB, [P, MH, MD + 1])
        m_nd = at("m_nd", H0 + 32 * KB + 2080, [P, MH, MD + 1])
        m_up = at("m_up", H0 + 32 * KB + 4160, [P, MH, MD + 1])
        m_n = at("m_n", H0 + 32 * KB + 6240, [P, MH, MD + 1])
        state = at("state", H0 + 32 * KB + 8320, [P, MH, MD + 1])
        a_s = at("a_s", H0 + 44 * KB, [P, 2, T])
        a_p = at("a_p", H0 + 52 * KB, [P, 2, T])
        a_t = at("a_t", W0, [P, 2, KC, P])
        q_hi = at("q_hi", M0, [P, 2, HEADS, P], F32R)
        q_lo = at("q_lo", M0 + 8 * KB, [P, 2, HEADS, P], F32R)
        k_hi = at("k_hi", V0, [P, T], F32R)
        k_lo = at("k_lo", V0 + 4 * KB, [P, T], F32R)
        arow = at("arow", W0 + 8 * KB, [P, 2, HEADS * HD])
        wo_hi = at("wo_hi", Q0, [P, KC, D], F32R)
        wo_lo = at("wo_lo", Q0 + 32 * KB, [P, KC, D], F32R)
        wo_raw = at("wo_raw", W0 + 16 * KB, [P, 2, D])
        mx_hi = at("mx_hi", H0 + 32 * KB, [P, 2, KC, P], F32R)
        mx_lo = at("mx_lo", H0 + 40 * KB, [P, 2, KC, P], F32R)
        xr = at("xr", H0 + 48 * KB, [P, 2, D])
        x2 = at("x2", H0 + 56 * KB, [P, 2, D])
        h2 = at("h2", W0, [P, 2, D])
        h2t = at("h2t", W0 + 8 * KB, [P, 2, KC, P])
        wn2 = at("wn2", S0, [P, D])
        rw = at("rw", S0 + 4 * KB, [P, KC, E])
        rb = at("rb", S0 + 5 * KB, [P, E])
        oneh = at("oneh", S0 + 6 * KB, [P, TOP, NT, E])
        prod = at("prod", S0 + 10 * KB, [P, NT, E])
        chosen = at("chosen", S0 + 11 * KB, [P, NT, E])
        place = at("place", S0 + 12 * KB, [P, NT, E])
        stepc = at("stepc", S0 + 13 * KB, [P, E, CAPT])
        F_ = R0
        e_raw = at("e_raw", F_, [P, 3, KC, 512])
        e_whi = at("e_whi", F_ + 48 * KB, [P, 4, KC, 256], F32R)
        e_wlo = at("e_wlo", F_ + 80 * KB, [P, 4, KC, 256], F32R)
        F1 = F_ + 112 * KB
        XB = 4 * KC * ROWS
        e_x = at("e_x", F1, [P, KC, 2, ROWS], F32R)
        e_a = at("e_a", F1 + 2 * XB, [P, KC, 2, ROWS], F32R)
        yt = at("yt", F1 + 4 * XB, [P, KC, ROWS])
        F2 = F1 + 5 * XB
        xg = at("xg", F2, [P, 2, D])
        yr = at("yr", F2 + 8 * KB, [P, 2, D])
        F3 = F2 + 16 * KB
        GB = 4 * 2 * 2 * ROWS
        gl, ul, sg, tt, af = [at(n_, F3 + k_ * GB, [P, 2, 2, ROWS]) for k_, n_ in enumerate(("gl", "ul", "sg", "tt", "af"))]
        F4 = F3 + 5 * GB
        brow = at("brow", F4, [P, P])
        bgu = at("bgu", F4 + 512, [P, 16])
        bdn = at("bdn", F4 + 576, [P, 8])
        idx, gidx, scur, slast = [at(n_, F4 + 640 + 32 * k_, [P, 2], I32) for k_, n_ in enumerate(("idx", "gidx", "scur", "slast"))]
        esum = at("esum", F4 + 768, [P, 2, 2, ROWS])
        yg = at("yg", F_, [P, 2, TOP, D])
        x3 = at("x3", F_ + 32 * KB, [P, 2, D])
        ot = at("ot", F_ + 40 * KB, [P, 2, D])
        wn3 = at("wn3", F_ + 48 * KB, [P, D])

        lg = column(E)
        best = column(NT * 8).rearrange("p (t k) -> p t k", t=NT)
        besti = column(NT * 8).bitcast(U32).rearrange("p (t k) -> p t k", t=NT)
        bestf = column(NT * 8).rearrange("p (t k) -> p t k", t=NT)
        gates = column(NT * TOP).rearrange("p (t k) -> p t k", t=NT)
        gsum = column(NT)
        counts, nblk, bend, bstart = column(E), column(E), column(E), column(E)
        destf = column(NT * TOP).rearrange("p (t k) -> p t k", t=NT)
        desti = column(NT * TOP).bitcast(I32).rearrange("p (t k) -> p t k", t=NT)
        bef, bei, nbi = column(1), column(1).bitcast(I32), column(1).bitcast(I32)
        tokid = column(NT * TOP).bitcast(I32).rearrange("p (t k) -> p t k", t=NT)
        mabs, mden, mrd, mss, mrs_ = column(4), column(4), column(4), column(4), column(4)
        minus1, mhalf = column(4), column(4)

        score_at = {}
        n = 0
        for i in range(2, NT):
            score_at[i] = n
            n += P * (i + 1)

        ps = ctx.enter_context(nc.psum_tensor("ps", [P, 8, 512], F32))

        def pair(b):
            return ps[:, b:b + 2, :].rearrange("p b n -> p (b n)")

        mo_d = scratch("mo_d", (MH, P, T), F32)
        x2_d = scratch("x2_d", (T, D), F32)
        h2_d = scratch("h2_d", (T + ROWS // TOP, D), F32)
        y_d = scratch("y_d", (T * TOP + ROWS, D), F32)
        tok_d = scratch("tok_d", (P * TOKW, 1), I32)
        be_d = scratch("be_d", (P, 1), I32)
        gu_w = I["w_gate_up"].rearrange("o e (c p) n -> (o e) p c n", p=P)
        dn_w = I["w_down"].rearrange("o e (c p) n -> (o e) p c n", p=P)
        gu_b = I["b_gate_up"].rearrange("o e (k n) -> (o e) k n", n=P)
        dn_b = I["b_down"].rearrange("o e (k n) -> (o e) k n", n=P)

        s = Semaphores(sem)

        def gate_on(eng, sem_, value):
            eng.wait_ge(sem_, value)
            eng.sem_inc(s.passed, 1)

        st_x, st_h, ld_wo, ld_g = (s.st_x0, s.st_x1), (s.st_h0, s.st_h1), (s.ld_w0, s.ld_w1), (s.ld_g0, s.ld_g1, s.ld_g2)
        ld_y, st_o = (s.ld_y0, s.ld_y1), (s.st_o0, s.st_o1)
        ld_x, ld_w, st_mo = (s.ld_x0, s.ld_x1), (s.ld_w0, s.ld_w1), (s.st_mo0, s.st_mo1)
        fts = feature_tiles()
        bctx = ExitStack()
        block = bctx.enter_context(nc.Block())

        w_in = I["w_in"].rearrange("o (c p) n -> p (o c) n", p=P)
        nw = [0]

        def piece(ring, m):
            return ring[:, m % 4, :, :].rearrange("p k (g n) -> p k g n", g=2)

        def raw_piece(m):
            c, q = m // 2, m % 2
            a = e_raw[:, c % 3, :, :]
            if c < 4:
                return a.rearrange("p k (g n) -> p k g n", g=2)[:, :, :, P * q:P * q + P]
            return a[:, :, 256 * q:256 * q + 256].rearrange("p k (g n) -> p k g n", g=2)

        def sums_of(f):
            return ps[:, 2 * (f % 2):2 * (f % 2) + 2, 0:2 * ROWS].rearrange("p g (s n) -> p g n s", s=2)

        @block.sync
        def _(sp):
            sp.dma_start(cst[:], I["c_const"]).then_inc(s.ld_const, 16)
            sp.dma_start(wnb[:], I["mix_norm_w"][0:1, :].to_broadcast([P, D])).then_inc(s.ld_wn, 16)
            for t in range(NT):
                if t >= 2:
                    sp.wait_ge(s.v_xn, t - 1)
                sp.dma_start(xt[:, t % 2, :], I["x"][0, t * P:(t + 1) * P, :]).then_inc(ld_x[t % 2], 16)
                if t == 1:
                    for f in range(2):
                        for dst, src, w in fts[f]:
                            sp.dma_start(w_raw[:, f % 2, :, dst:dst + w], w_in[:, :, src:src + w]).then_inc(ld_w[f % 2], 16)
            sp.dma_start(igb[0:MH, :], I["igate_b"].rearrange("o h -> h o")).then_inc(s.ld_gate, 16)
            sp.dma_start(fgb[0:MH, :], I["fgate_b"].rearrange("o h -> h o")).then_inc(s.ld_gate, 16)
            sp.dma_start(carry[0:MH, :], I["c_carry"]).then_inc(s.ld_gate, 16)
            sp.dma_start(rope_i[:], I["c_rope_i"]).then_inc(s.ld_rope, 16)
            with nc.allow_non_contiguous_dma(reason="small columns"):
                for f in range(8):
                    for k in range(CONV):
                        sp.dma_start(convw[:, f, k:k + 1], I["conv_w"][0, k, f * P:(f + 1) * P].unsqueeze(1)).then_inc(s.ld_small, 16)
                    sp.dma_start(convb[:, f:f + 1], I["conv_b"][0, f * P:(f + 1) * P].unsqueeze(1)).then_inc(s.ld_small, 16)
                for h in range(MH):
                    sp.dma_start(mnw[:, h:h + 1], I["mlstm_norm_w"][0, h * P:(h + 1) * P].unsqueeze(1)).then_inc(s.ld_small, 16)
            for f in range(2, NFT):
                sp.wait_ge(s.g_wlo, f - 1)
                for dst, src, w in fts[f]:
                    sp.dma_start(w_raw[:, f % 2, :, dst:dst + w], w_in[:, :, src:src + w]).then_inc(ld_w[f % 2], 16)
                if f == 5:
                    sp.wait_ge(s.a_relu, 48)
                    sp.wait_ge(s.p_is, 48)
                    sp.dma_start(rope_q[:], I["c_rope_q"]).then_inc(s.ld_rope, 16)
            for j in range(4):
                sp.wait_ge(s.a_ev, FT_MO + j + 1)
                sp.dma_start(mo_d[j], vtmp[:, (FT_MO + j) % 2, :]).then_inc(st_mo[j % 2], 16)
            sp.wait_ge(st_mo[0], 32)
            sp.wait_ge(st_mo[1], 32)
            sp.wait_ge(s.p_ft, NFT)
            for c in range(NT):
                if c >= 2:
                    sp.wait_ge(s.g_mix, c - 1)
                sp.dma_start(m_o[:, c % 2, :, :], mo_d[:, :, c * P:(c + 1) * P].rearrange("h p t -> p h t")).then_inc(
                    (s.ld_mo0, s.ld_mo1)[c % 2], 16)

            sp.wait_ge(s.a_at, NT)
            sp.dma_start(wn2[:], I["ffn_norm_w"][0:1, :].to_broadcast([P, D])).then_inc(s.ld_wn, 16)
            sp.dma_start(rw[:], I["router_w"].rearrange("o (c p) n -> p (o c) n", p=P)).then_inc(s.ld_rw, 16)
            sp.dma_start(rb[:], I["router_b"][0:1, :].to_broadcast([P, E])).then_inc(s.ld_rw, 16)
            for c in range(KC):
                if c >= 2:
                    sp.wait_ge(s.g_wolo, c - 1)
                sp.dma_start(wo_raw[:, c % 2, :], I["w_out"][0, c * P:(c + 1) * P, :]).then_inc(ld_wo[c % 2], 16)
            for t in range(NT + 1):
                if t < NT:
                    if t >= 2:
                        sp.wait_ge(s.v_x2, t - 1)
                    sp.dma_start(xr[:, t % 2, :], I["x"][0, t * P:(t + 1) * P, :]).then_inc(ld_x[t % 2], 16)
                if t >= 1:
                    rows = slice((t - 1) * P, t * P)
                    sp.wait_ge(s.v_x2, t)
                    sp.dma_start(x2_d[rows, :], x2[:, (t - 1) % 2, :]).then_inc(st_x[(t - 1) % 2], 16)
                    sp.wait_ge(s.v_h2, t)
                    sp.dma_start(h2_d[rows, :], h2[:, (t - 1) % 2, :]).then_inc(st_h[(t - 1) % 2], 16)
                    if t == NT:
                        sp.dma_start(h2_d[T:T + ROWS // TOP, :], h2[0:ROWS // TOP, (t - 1) % 2, :]).then_inc(s.st_hx, 16)
            sp.dma_start(tok_d.rearrange("(p w) o -> p (w o)", w=TOKW), I["c_slots"]).then_inc(s.st_zero, 16)
            sp.wait_ge(s.v_dest, DEST_STEPS)
            sp.dma_start(be_d, bei).then_inc(s.st_be, 16)
            sp.dma_start(scur[0:HALF, :], I["c_slots"][0:2, :].rearrange("a (q h) -> (a q) h", h=2)).then_inc(s.ld_scur, 16)
            sp.wait_ge(s.st_be, 16)
            sp.wait_ge(s.st_y, 32)
            sp.wait_ge(s.st_tok, 16 * (NT * TOP - 2))
            sp.wait_ge(s.st_hx, 16)
            for k in range(2):
                sp.wait_ge(st_x[k], 16 * NT // 2)
                sp.wait_ge(st_h[k], 16 * NT // 2)

            nb = sp.value_load(nbi[0:1, 0:1], min_val=1, max_val=NBMAX)
            sp.dma_start(idx[0:HALF, :], tok_d[0:ROWS, :].rearrange("(p h) o -> p (h o)", p=HALF)).then_inc(s.ld_idx, 16)
            e0 = sp.value_load(be_d[0:1, 0:1], min_val=0, max_val=E - 1)
            sp.dma_start(brow[0:16, :], gu_b[bass.ds(e0, 1), :, :].rearrange("o k n -> (o k) n")).then_inc(s.ld_b, 16)
            sp.dma_start(brow[16:24, :], dn_b[bass.ds(e0, 1), :, :].rearrange("o k n -> (o k) n")).then_inc(s.ld_b, 16)
            with sp.Fori(0, nb) as i:
                e = sp.value_load(be_d[bass.ds(i, 1), 0:1], min_val=0, max_val=E - 1)
                for c in range(6):
                    sp.wait_ge(s.e_lo, i * 12 + (2 * c + 2))
                    sp.wait_ge(s.e_lop, i * 12 + (2 * c + 2))
                    if c < 4:
                        for k in range(2):
                            a_ = FE * k + 256 * c
                            sp.dma_start(e_raw[:, c % 3, :, 256 * k:256 * k + 256],
                                         gu_w[bass.ds(e, 1), :, :, a_:a_ + 256].rearrange("o p c n -> (o p) c n")).then_inc(ld_g[c % 3], 16)
                    else:
                        for k in range(2):
                            a_ = 512 * (c - 4) + 256 * k
                            sp.dma_start(e_raw[:, c % 3, :, 256 * k:256 * k + 256],
                                         dn_w[bass.ds(e, 1), :, :, a_:a_ + 256].rearrange("o p c n -> (o p) c n")).then_inc(ld_g[c % 3], 16)
                    if c == 3:
                        en = sp.value_load(be_d[bass.ds(i + 1, 1), 0:1], min_val=0, max_val=E - 1)
                        sp.wait_ge(s.e_gx, i + 1)
                        sp.wait_ge(s.e_ix, i * 2 + 3)
                        sp.dma_start(idx[0:HALF, :], tok_d[bass.ds((i + 1) * ROWS, ROWS), :].rearrange("(p h) o -> p (h o)", p=HALF)).then_inc(s.ld_idx, 16)
                        sp.wait_ge(s.p_xt, i + 1)
                        sp.dma_start(brow[0:16, :], gu_b[bass.ds(en, 1), :, :].rearrange("o k n -> (o k) n")).then_inc(s.ld_b, 16)
                        sp.dma_start(brow[16:24, :], dn_b[bass.ds(en, 1), :, :].rearrange("o k n -> (o k) n")).then_inc(s.ld_b, 16)

            sp.wait_ge(s.p_pc, nb * 12 + 4)
            sp.wait_ge(s.g_y, 1)
            sp.wait_ge(s.ld_idx, nb * 16 + 16)
            sp.wait_ge(s.ld_b, nb * 32 + 32)
            sp.dma_start(wn3[:], I["final_norm_w"].rearrange("(o n) -> o n", o=1).to_broadcast([P, D])).then_inc(s.ld_wn, 16)
            for t in range(NT + 1):
                if t < NT:
                    if t >= 2:
                        sp.wait_ge(s.v_o, t - 1)
                    sp.dma_start(yg[:, t % 2, :, :], y_d[t * P * TOP:(t + 1) * P * TOP, :].rearrange("(p k) n -> p k n", k=TOP)).then_inc(ld_y[t % 2], 16)
                    sp.dma_start(x3[:, t % 2, :], x2_d[t * P:(t + 1) * P, :]).then_inc(ld_x[t % 2], 16)
                if t >= 1:
                    sp.wait_ge(s.v_o, t)
                    sp.dma_start(out[0, (t - 1) * P:t * P, :], ot[:, (t - 1) % 2, :]).then_inc(st_o[(t - 1) % 2], 16)
            sp.wait_ge(st_o[0], 16 * NT // 2)
            sp.wait_ge(st_o[1], 16 * NT // 2)

        loads = [sum(16 * len(fts[g]) for g in range(f % 2, f + 1, 2)) for f in range(NFT)]

        @block.gpsimd
        def _(gp):
            conv = Steps(gp, s.g_conv)

            def convolve(f, taps):
                x = [mqk[:, f, 1 + k:1 + k + T] for k in range(CONV)]
                for k in taps:
                    if k == 3:
                        gp.wait_ge(s.a_ev, FT_MQK + f + 1)
                        if f >= 1:
                            gp.wait_ge(s.a_silu, f)
                        conv(nc.gpsimd.tensor_scalar(ctmp[:], x[3], convw[:, f, 3:4], convb[:, f:f + 1], ALU.mult, ALU.add))
                        continue
                    conv(nc.gpsimd.tensor_scalar(cmul[:], x[k], convw[:, f, k:k + 1], 1.0, ALU.mult, ALU.mult))
                    conv.done()
                    conv(nc.gpsimd.tensor_tensor(ctmp[:], ctmp[:], cmul[:], ALU.add))
                    conv.done()

            for f in range(NFT):
                gp.wait_ge(s.a_whi, f + 1)
                if f >= 2:
                    gp.wait_ge(s.p_ft, f - 1)
                nc.gpsimd.tensor_tensor(w_lo[:, f % 2, :, :], w_raw[:, f % 2, :, :],
                                        w_hi[:, f % 2, :, :].bitcast(F32), ALU.subtract).then_inc(s.g_wlo, 1)
                if f == 0:
                    gp.wait_ge(s.p_ht, NT)
                    nc.gpsimd.memset(iq_hi[:].bitcast(F32), 0.0)
                    nc.gpsimd.memset(iq_lo[:].bitcast(F32), 0.0).then_inc(s.g_iqz, 1)
                if f == 3:
                    nc.gpsimd.memset(stack[:], 0.0).then_inc(s.g_stack, 1)
                if f == FT_MQK:
                    gp.wait_ge(s.v_score, 6 * 9)
                    gp.wait_ge(s.v_gate, 12)
                    gp.wait_ge(s.p_iwt, 1)
                    gp.wait_ge(s.p_mcol, 1)
                    nc.gpsimd.memset(mqk[:, :, 0:4], 0.0).then_inc(s.g_pad, 1)
                    gp.wait_ge(s.v_ra, 3)
                    nc.gpsimd.memset(mvtok[:, :, :, MD:MD + 1], 1.0).then_inc(s.g_ones, 1)
                if FT_Q + 2 <= f <= FT_K + 2:
                    j = f - 2 - FT_Q
                    ft = qt[:, j, :] if j < 4 else kt[:]
                    gp.wait_ge(s.ld_rope, 32)
                    gp.wait_ge(s.a_rq, j + 1)
                    nc.gpsimd.tensor_tensor(qtmp[:], qtmp[:], rope_q[:, 1, :], ALU.mult).then_inc(s.g_rq, 1)
                    nc.gpsimd.tensor_tensor(ft, ft, rope_q[:, 0, :], ALU.mult).then_inc(s.g_rq, 1)
                    gp.wait_ge(s.g_rq, 3 * j + 2)
                    nc.gpsimd.tensor_tensor(ft, ft, qtmp[:], ALU.add).then_inc(s.g_rq, 1)
                if f == FT_MQK + 2:
                    gp.wait_ge(s.g_rq, 15)
                    gp.wait_ge(s.ld_small, 16 * (8 * CONV + 8 + MH))
                if f >= FT_MQK + 2:
                    convolve((f - FT_MQK - 2) // 2, (3, 0) if f % 2 == 0 else (1, 2))
            convolve(7, (3, 0, 1, 2))

            m1 = Steps(gp, s.g_m1)
            gp.wait_ge(s.p_ft, NFT)
            m1(nc.gpsimd.memset(minus1, -1.0))
            m1(nc.gpsimd.memset(mhalf, -0.5))
            gp.wait_ge(s.a_mexp, 1)
            m1(nc.gpsimd.tensor_scalar(mexp[:, :, 1, :], mexp[:, :, 1, :], MD ** -0.5, 1.0, ALU.mult, ALU.mult))
            nc.gpsimd.memset(state[:], 0.0).then_inc(s.g_st, 1)
            m1.done()

            def m_weights(c):
                gp.wait_ge(s.a_s1, c + 1)
                if c >= 1:
                    gp.wait_ge(s.p_nd, c)
                nc.gpsimd.tensor_tensor(m_w[:], m_sc[:], m_ex[:], ALU.mult).then_inc(s.g_w, 1)

            def m_quotient(c):
                gp.wait_ge(s.a_abs, c + 1)
                for h in range(MH):
                    m1(nc.gpsimd.tensor_scalar(mden[:, h:h + 1], mabs[:, h:h + 1], mexp[:, c, 2, h:h + 1], 1.0, ALU.max, ALU.mult))
                m1.done()
                m1(nc.gpsimd.tensor_tensor(mrd, mden, minus1, ALU.pow))
                m1.done()
                if c >= 1:
                    gp.wait_ge(s.a_hn, c)
                nc.gpsimd.tensor_tensor(m_h[:], m_n[:, :, 0:MD], mrd.unsqueeze(2).to_broadcast([P, MH, MD]), ALU.mult).then_inc(s.g_h, 1)

            def m_root(c):
                gp.wait_ge(s.a_sq, c + 1)
                m1(nc.gpsimd.tensor_scalar(mrs_, mss, 1.0 / MD, EPS, ALU.mult, ALU.add))
                m1.done()
                nc.gpsimd.tensor_tensor(mss, mrs_, mhalf, ALU.pow).then_inc(s.g_rs, 1)

            def m_sum(c):
                gp.wait_ge(s.a_in, c + 1)
                if c >= 1:
                    gp.wait_ge(s.g_h, c)
                nc.gpsimd.tensor_tensor(m_n[:], m_nd[:], m_in[:], ALU.add).then_inc(s.g_n, 1)

            def m_state(c):
                gp.wait_ge(s.a_up, c + 1)
                gp.wait_ge(s.p_in, c + 1)
                gp.wait_ge(s.g_st, c + 1)
                for h in range(MH):
                    m1(nc.gpsimd.tensor_scalar(state[:, h, :], state[:, h, :], decay[:, h, c:c + 1], 1.0, ALU.mult, ALU.mult))
                m1.done()
                nc.gpsimd.tensor_tensor(state[:], state[:], m_up[:], ALU.add).then_inc(s.g_st, 1)

            def m_mix(c):
                gp.wait_ge(s.a_mt, c + 1)
                gp.wait_ge((s.ld_mo0, s.ld_mo1)[c % 2], 16 * (c // 2 + 1))
                nc.gpsimd.tensor_tensor(mixt[:, 4:8, c * P:(c + 1) * P], m_mt[:], m_o[:, c % 2, :, :], ALU.mult).then_inc(s.g_mix, 1)

            m_weights(0)
            for c in range(NT + 2):
                if 1 <= c <= NT:
                    m_quotient(c - 1)
                if c + 1 < NT:
                    m_weights(c + 1)
                if 1 <= c <= NT:
                    m_root(c - 1)
                if c < NT:
                    m_sum(c)
                    m_state(c)
                if c >= 2:
                    m_mix(c - 2)

            gp.wait_ge(s.p_in, NT)
            nc.gpsimd.memset(q_hi[:].bitcast(F32), 0.0)
            nc.gpsimd.memset(q_lo[:].bitcast(F32), 0.0).then_inc(s.g_qz, 1)

            for c in range(KC):
                gp.wait_ge(s.a_wohi, c + 1)
                nc.gpsimd.tensor_tensor(wo_lo[:, c, :], wo_raw[:, c % 2, :], wo_hi[:, c, :].bitcast(F32), ALU.subtract).then_inc(s.g_wolo, 1)
            nc.gpsimd.iota(tokid, pattern=[[P * TOP, NT], [1, TOP]], base=0, channel_multiplier=TOP).then_inc(s.g_tok, 1)
            gp.wait_ge(s.g_tok, 1)
            gp.wait_ge(s.st_zero, 16)
            gp.wait_ge(s.v_dest, DEST_STEPS)
            for t in range(NT):
                for k in range(TOP):
                    nc.gpsimd.indirect_dma_start(tok_d[:, :], bass.IndirectOffsetOnAxis(ap=desti[:, t, k:k + 1], axis=0),
                                                 tokid[:, t, k:k + 1], None).then_inc(s.st_y if t == NT - 1 and k >= 2 else s.st_tok, 16)
            for k in range(2):
                gp.wait_ge(st_h[k], 16 * NT // 2)
            gp.wait_ge(s.st_hx, 16)

            def gather():
                for h in range(2):
                    nc.gpsimd.indirect_dma_start(xg[0:HALF, h, :], None, h2_d[:, :],
                                                 bass.IndirectOffsetOnAxis(ap=gidx[0:HALF, h:h + 1], axis=0)).then_inc(s.ld_xg, 16)

            def scatter(rows):
                for h in range(2):
                    nc.gpsimd.indirect_dma_start(y_d[:, :], bass.IndirectOffsetOnAxis(ap=rows[0:HALF, h:h + 1], axis=0),
                                                 yr[0:HALF, h, :], None).then_inc(s.st_y, 16)

            nb = gp.value_load(nbi[0:1, 0:1], min_val=1, max_val=NBMAX)
            gp.wait_ge(s.e_gx, 1)
            gather()
            gp.sem_inc(s.e_lop, 6)
            gp.wait_ge(s.e_lop, 6)
            with gp.Fori(0, nb) as i:
                for m in range(PIECES):
                    gate_on(gp, s.e_hi, i * PIECES + (m + 1))
                    ks = slice(KDVE, KC)
                    nc.gpsimd.tensor_tensor(piece(e_wlo, m)[:, ks], raw_piece(m)[:, ks], piece(e_whi, m)[:, ks].bitcast(F32),
                                            ALU.subtract).then_inc(s.e_lop, 1)
                    if m == 6:
                        gate_on(gp, s.e_gx, i + 2)
                        gate_on(gp, s.p_xt, i + 1)
                        gather()
                    if m == 7:
                        gate_on(gp, s.e_ix, i * 2 + 3)
                        gate_on(gp, s.e_yr, i * 4 + 5)
                        scatter(slast)
            gate_on(gp, s.e_yr, nb * 4 + 5)
            scatter(scur)
            gate_on(gp, s.ld_xg, nb * 32 + 32)
            gate_on(gp, s.st_y, nb * 32 + 64)

            gp.sem_inc(s.g_y, 1)

        @block.scalar
        def _(act):
            act.wait_ge(s.ld_const, 16)

            def ht_hi_of(t):
                act.wait_ge(s.p_ht, t + 1)
                nc.scalar.activation(ht_hi[:, :, t * P:(t + 1) * P],
                                     pair(2 * (t % 2)).rearrange("p (c n) -> p c n", c=KC), ACT.Copy).then_inc(s.a_hthi, 1)

            for t in range(NT):
                act.wait_ge(ld_x[t % 2], 16 * (t // 2 + 1))
                if t >= 2:
                    act.wait_ge(s.p_ht, t - 1)
                nc.scalar.activation(xn[:, t % 2, :], xt[:, t % 2, :], ACT.Square, accum_out=ss[:, t:t + 1]).then_inc(s.a_square, 1)
                act.wait_ge(s.a_square, t + 1)
                nc.scalar.activation(rstd[:, t:t + 1], ss[:, t:t + 1], ACT.Sqrt, bias=EPS, scale=1.0 / D).then_inc(s.a_root, 1)
                if t >= 1:
                    ht_hi_of(t - 1)
            ht_hi_of(NT - 1)

            def hi(f):
                act.wait_ge(ld_w[f % 2], loads[f])
                if f >= 2:
                    act.wait_ge(s.p_ft, f - 1)
                nc.scalar.activation(w_hi[:, f % 2, :, :], w_raw[:, f % 2, :, :], ACT.Copy).then_inc(s.a_whi, 1)

            def evacuate(f):
                act.wait_ge(s.p_ft, f + 1)
                src = pair(4 + 2 * (f % 2))
                if f < FT_IK:
                    nc.scalar.activation(iqt[:, f, :], src, ACT.Copy).then_inc(s.a_ev, 1)
                elif f == FT_IK:
                    nc.scalar.activation(ikt[:], src, ACT.Copy).then_inc(s.a_ev, 1)
                elif f == FT_SMALL:
                    act.wait_ge(s.ld_gate, 48)
                    nc.scalar.activation(row_i[0:MH, :], src[0:MH, :], ACT.Identity, bias=igb[0:MH, :]).then_inc(s.a_gate, 1)
                    nc.scalar.activation(row_f[0:MH, :], src[32:32 + MH, :], ACT.Identity, bias=fgb[0:MH, :]).then_inc(s.a_gate, 1)
                    nc.scalar.activation(iwt[0:IH, :], src[64:64 + IH, :], ACT.Copy, scale=1.0 / 16.0).then_inc(s.a_ev, 1)
                    act.wait_ge(s.a_gate, 2)
                    nc.scalar.activation(row_t[0:MH, :], row_f[0:MH, :], ACT.Abs).then_inc(s.a_gate, 1)
                    act.wait_ge(s.a_gate, 3)
                    nc.scalar.activation(row_t[0:MH, :], row_t[0:MH, :], ACT.Exp, scale=-1.0).then_inc(s.a_gate, 1)
                    act.wait_ge(s.a_gate, 4)
                    nc.scalar.activation(row_t[0:MH, :], row_t[0:MH, :], ACT.Ln, bias=1.0).then_inc(s.a_gate, 1)
                elif f < FT_K:
                    nc.scalar.activation(qt[:, f - FT_Q, :], src, ACT.Copy).then_inc(s.a_ev, 1)
                elif f == FT_K:
                    nc.scalar.activation(kt[:], src, ACT.Copy).then_inc(s.a_ev, 1)
                elif f == FT_V or FT_MV <= f < FT_MO:
                    if f == FT_V:
                        act.wait_ge(s.g_rq, 15)
                    else:
                        act.wait_ge(s.p_vt, 1 if f < FT_MV + 2 else f - FT_MV)
                    nc.scalar.activation(vtmp[:, f % 2, :], src, ACT.Copy).then_inc(s.a_ev, 1)
                elif f < FT_MV:
                    if f == FT_MQK:
                        act.wait_ge(s.g_pad, 1)
                    nc.scalar.activation(mqk[:, f - FT_MQK, 4:4 + T], src, ACT.Copy).then_inc(s.a_ev, 1)
                else:
                    if f < FT_MO + 2:
                        act.wait_ge(s.p_vt, f - FT_MO + 4)
                    else:
                        act.wait_ge(st_mo[f % 2], 16)
                    nc.scalar.activation(vtmp[:, f % 2, :], src, ACT.Sigmoid).then_inc(s.a_ev, 1)

            def silu(f):
                act.wait_ge(s.g_conv, 7 * (f + 1))
                nc.scalar.activation(mqk[:, f, 4:4 + T], ctmp[:], ACT.Silu).then_inc(s.a_silu, 1)

            def at_out(i):
                act.wait_ge(s.p_at, i + 1)
                nc.scalar.activation(mixt[:, 0:4, i * P:(i + 1) * P], ps[:, 7, :].rearrange("p (c n) -> p c n", n=P),
                                     ACT.Copy).then_inc(s.a_at, 1)

            for f in range(NFT + 2):
                if f < NFT:
                    hi(f)
                if FT_Q + 2 <= f <= FT_K + 2:
                    j = f - 2 - FT_Q
                    act.wait_ge(s.p_rq, j + 1)
                    if j >= 1:
                        act.wait_ge(s.g_rq, 3 * j)
                    else:
                        act.wait_ge(s.a_relu, 48)
                        act.wait_ge(s.p_is, 48)
                    nc.scalar.activation(qtmp[:], pair(2 * (j % 2)), ACT.Copy).then_inc(s.a_rq, 1)
                if 1 <= f <= NFT:
                    evacuate(f - 1)
                if f == FT_SMALL + 1:
                    act.wait_ge(s.v_ra, 3)
                    nc.scalar.activation(ik_hi[:], ikt[:], ACT.Copy).then_inc(s.a_iqhi, 1)

                    def iq_hi_of(i):
                        if i == 2:
                            act.wait_ge(s.g_iqz, 1)
                        if i >= 4:
                            act.wait_ge(s.p_is, IH * (i - 3))
                        for g in range(4):
                            rows = slice(ID * g, ID * g + ID)
                            nc.scalar.activation(iq_hi[rows, i % 2, g::4, :], iqt[rows, :, i * P:(i + 1) * P], ACT.Copy).then_inc(s.a_iqhi, 1)

                    iq_hi_of(2)
                    act.wait_ge(s.p_iwt, 1)
                    nc.scalar.activation(iwc, ps[:, 0, 0:NT * IH].rearrange("p (t h) -> p t h", t=NT), ACT.Copy).then_inc(s.a_iwt, 1)
                    for u in range(6 * IH):
                        i, h = 2 + u // IH, u % IH
                        w = P * (i + 1)
                        if h == 2 and i + 1 < NT:
                            iq_hi_of(i + 1)
                        act.wait_ge(s.p_is, u + 1)
                        if u >= 2:
                            act.wait_ge(s.v_score, 9 * ((u - 2) // IH) + (u - 2) % IH + 1)
                        nc.scalar.activation(rbuf[:, u % 2, 0:w], pair(2 * (u % 2))[:, 0:w], ACT.Relu).then_inc(s.a_relu, 1)
                    act.wait_ge(s.v_mcol, 1)
                    nc.scalar.activation(mexp, mcol[:, :, 1:4, :], ACT.Exp).then_inc(s.a_mexp, 1)
                    act.wait_ge(s.p_decay, 1)
                    nc.scalar.activation(decay, ps[:, 0, 0:MH * NT].rearrange("p (h c) -> p h c", h=MH), ACT.Exp).then_inc(s.a_decay, 1)
                if f == FT_V + 2 or FT_MV + 2 <= f <= FT_MO + 1:
                    j = 0 if f == FT_V + 2 else f - 1 - FT_MV
                    act.wait_ge(s.p_vt, j + 1)
                    if j == 1:
                        act.wait_ge(s.g_ones, 1)
                    dst = vtok[:] if j == 0 else mvtok[:, :, j - 1, 0:MD]
                    nc.scalar.activation(dst, pair(2 * ((j + 1) % 2)).rearrange("p (t n) -> p t n", t=NT), ACT.Copy).then_inc(s.a_vt, 1)

                if f >= FT_MQK + 4 and f % 2 == 0:
                    silu((f - FT_MQK - 4) // 2)
            silu(7)

            def m_chunk(c):
                act.wait_ge(s.p_s1, c + 1)
                if c == 0:
                    act.wait_ge(s.g_m1, 3)
                else:
                    act.wait_ge(s.g_w, c)
                if c >= 2:
                    act.wait_ge(s.p_up, c - 1)
                for h in range(MH):
                    nc.scalar.activation(m_kw[:, c % 2, h, :], ps[:, 0, h * P:(h + 1) * P], ACT.Copy, scale=mexp[:, c, 1, h:h + 1])
                for h in range(MH):
                    nc.scalar.activation(m_ex[:, h, :], ps[:, 2, h * P:(h + 1) * P], ACT.Exp, bias=mcol[:, c, 0, h:h + 1])
                nc.scalar.activation(m_sc[:], ps[:, 1, :].rearrange("p (h n) -> p h n", h=MH), ACT.Copy, scale=MD ** -0.5).then_inc(s.a_s1, 1)

            def m_out(dst, bank, signal):
                for k in range(2):
                    m = nc.scalar.activation(dst[:, 2 * k:2 * k + 2, :], ps[:, bank + k, 0:2 * (MD + 1)].rearrange("p (h n) -> p h n", h=2), ACT.Copy)
                m.then_inc(signal, 1)

            m_chunk(0)
            for c in range(NT + 2):
                if c < NT:
                    act.wait_ge(s.p_nd, c + 1)
                    if c >= 1:
                        act.wait_ge(s.g_n, c)
                    m_out(m_nd, 3, s.a_nd)
                if 1 <= c <= NT:
                    act.wait_ge(s.g_n, c)
                    nc.scalar.activation(mabs, m_n[:, :, MD], ACT.Abs).then_inc(s.a_abs, 1)
                if c >= 2:
                    act.wait_ge(s.p_m3, c - 1)
                    if c >= 3:
                        act.wait_ge(s.g_mix, c - 2)
                    for h in range(MH):
                        m = nc.scalar.activation(m_mt[:, h, :], ps[:, 7, h * P:(h + 1) * P], ACT.Copy, scale=mnw[:, h:h + 1])
                    m.then_inc(s.a_mt, 1)
                if c + 1 < NT:
                    m_chunk(c + 1)
                if 1 <= c <= NT:
                    act.wait_ge(s.g_h, c)
                    if c >= 2:
                        act.wait_ge(s.p_m3, c - 1)
                    for h in range(MH):
                        m = nc.scalar.activation(m_hn[:, h, :], m_h[:, h, :], ACT.Square, accum_out=mss[:, h:h + 1])
                    m.then_inc(s.a_sq, 1)
                if c < NT:
                    act.wait_ge(s.p_in, c + 1)
                    if c >= 1:
                        act.wait_ge(s.g_n, c)
                    for h in range(MH):
                        b, o_ = 5 + h // 2, (h % 2) * (MD + 1)
                        m = nc.scalar.activation(m_in[:, h, :], ps[:, b, o_:o_ + MD + 1], ACT.Copy, scale=mexp[:, c, 0, h:h + 1])
                    m.then_inc(s.a_in, 1)
                    act.wait_ge(s.p_up, c + 1)
                    act.wait_ge(s.g_st, c + 1)
                    m_out(m_up, 3, s.a_up)
                if 1 <= c <= NT:
                    act.wait_ge(s.g_rs, c)
                    for h in range(MH):
                        m = nc.scalar.activation(m_hn[:, h, :], m_h[:, h, :], ACT.Copy, scale=mss[:, h:h + 1])
                    m.then_inc(s.a_hn, 1)

            def exp(u):
                i, h = u // HEADS, u % HEADS
                w = P * (i + 1)
                act.wait_ge(s.v_nm, u + 1)
                if u >= 2:
                    act.wait_ge(s.p_pt, u - 1)
                if h == 0 and i >= 2:
                    act.wait_ge(s.v_rs, i - 1)
                nc.scalar.activation(a_p[:, u % 2, 0:w], a_s[:, u % 2, 0:w], ACT.Exp, scale=HD ** -0.5, bias=nmx[:, u % 2:u % 2 + 1],
                                     accum_out=rs[:, (i % 2) * 8 + h:(i % 2) * 8 + h + 1]).then_inc(s.a_exp, 1)

            def pt_out(u):
                i = u // HEADS
                act.wait_ge(s.p_pt, u + 1)
                if u >= 2:
                    act.wait_ge(s.p_pv, u - 1)
                nc.scalar.activation(a_t[:, u % 2, 0:i + 1, :], pair(4)[:, 0:P * (i + 1)].rearrange("p (c n) -> p c n", n=P),
                                     ACT.Copy).then_inc(s.a_pt, 1)

            act.wait_ge(s.g_mix, NT)
            act.wait_ge(s.g_rq, 15)
            nc.scalar.activation(k_hi[:], kt[:], ACT.Copy).then_inc(s.a_qkhi, 1)

            def q_hi_of(i):
                if i == 0:
                    act.wait_ge(s.g_qz, 1)
                if i >= 2:
                    act.wait_ge(s.p_s, HEADS * (i - 1))
                for g in range(KVH):
                    rows = slice(HD * g, HD * g + HD)
                    nc.scalar.activation(q_hi[rows, i % 2, 4 * g:4 * g + 4, :], qt[rows, :, i * P:(i + 1) * P], ACT.Copy).then_inc(s.a_qkhi, 1)

            q_hi_of(0)
            exp(0)
            for u in range(NT * HEADS):
                if u + 1 < NT * HEADS:
                    exp(u + 1)
                pt_out(u)
                if u % HEADS == 4 and u // HEADS + 1 < NT:
                    q_hi_of(u // HEADS + 1)
                if u % HEADS == 3 and u > HEADS:
                    at_out(u // HEADS - 1)
            at_out(NT - 1)


            def root2(t):
                act.wait_ge(s.v_x2, t + 1)
                if t >= 2:
                    act.wait_ge(st_h[t % 2], 16 * (t // 2))
                    act.wait_ge(s.p_h2t, t - 1)
                nc.scalar.activation(h2[:, t % 2, :], x2[:, t % 2, :], ACT.Square, accum_out=ss[:, t:t + 1]).then_inc(s.a_square, 1)
                act.wait_ge(s.a_square, NT + t + 1)
                nc.scalar.activation(rstd[:, t:t + 1], ss[:, t:t + 1], ACT.Sqrt, bias=EPS, scale=1.0 / D).then_inc(s.a_root, 1)

            def h2t_out(t):
                act.wait_ge(s.p_h2t, t + 1)
                if t >= 2:
                    act.wait_ge(s.p_lg, t - 1)
                nc.scalar.activation(h2t[:, t % 2, :, :], pair(4).rearrange("p (c n) -> p c n", c=KC), ACT.Copy).then_inc(s.a_h2t, 1)

            for c in range(KC):
                act.wait_ge(ld_wo[c % 2], loads[NFT - 2 + c % 2] + 16 * (c // 2 + 1))
                nc.scalar.activation(wo_hi[:, c, :], wo_raw[:, c % 2, :], ACT.Copy).then_inc(s.a_wohi, 1)
            for t in range(NT + 1):
                if t < NT:
                    if t >= 2:
                        act.wait_ge(s.p_out, t - 1)
                    nc.scalar.activation(mx_hi[:, t % 2, :, :], mixt[:, :, t * P:(t + 1) * P], ACT.Copy).then_inc(s.a_mxhi, 1)
                if t >= 1:
                    root2(t - 1)
                    h2t_out(t - 1)
            act.wait_ge(s.v_route, 1)
            nc.scalar.activation(gates, gates, ACT.Exp).then_inc(s.a_gexp, 1)

            act.wait_ge(s.v_dest, DEST_STEPS)
            nb = act.value_load(nbi[0:1, 0:1], min_val=1, max_val=NBMAX)

            def x_hi(n):
                act.wait_ge(s.p_xt, n)
                nc.scalar.activation(e_x[:, 0:6, 0, :].rearrange("p (b k) n -> p b k n", b=2),
                                     ps[:, 4:6, 0:3 * ROWS].rearrange("p b (k n) -> p b k n", k=3), ACT.Copy).then_inc(s.e_xh, 1)
                nc.scalar.activation(e_x[:, 6:8, 0, :], ps[:, 6, 0:2 * ROWS].rearrange("p (k n) -> p k n", k=2), ACT.Copy).then_inc(s.e_xh, 1)

            def y_rows(i, q):
                h, dq = q // 2, q % 2
                act.wait_ge(s.p_yt, i * 4 + (q + 1))
                nc.scalar.activation(yr[0:HALF, h, dq * 512:dq * 512 + 512], ps[0:HALF, 4 + q, :], ACT.Copy).then_inc(s.e_yr, 1)

            def y_bias(i, m):
                act.wait_ge(s.e_yd, i * 4 + (m + 1))
                for d in (2 * m, 2 * m + 1):
                    nc.scalar.activation(yt[:, d, :], yt[:, d, :], ACT.Identity, bias=bdn[:, d:d + 1]).then_inc(s.e_y, 1)

            x_hi(1)
            act.sem_inc(s.e_yr, 1)
            act.wait_ge(s.e_yr, 1)
            with act.Fori(0, nb) as i:
                def split_hi(m):
                    act.wait_ge(ld_g[m // 2 % 3], i * 64 + 32 * (m // 6 + 1))
                    act.wait_ge(s.p_pc, i * PIECES + (m + 1))
                    nc.scalar.activation(piece(e_whi, m), raw_piece(m), ACT.Copy).then_inc(s.e_hi, 1)

                def sigmoid(q):
                    act.wait_ge(s.e_mn, i * 16 + 4 * (q + 1))
                    nc.scalar.activation(sg[:, q % 2], gl[:, q % 2], ACT.Sigmoid, scale=ALPHA).then_inc(s.e_sg, 1)

                def a_hi(q):
                    act.wait_ge(s.e_act, i * 4 + (q + 1))
                    if q == 0:
                        act.wait_ge(s.p_pc, i * PIECES + 4)
                    nc.scalar.activation(e_a[:, 2 * q:2 * q + 2, 0, :], af[:, q % 2], ACT.Copy).then_inc(s.e_ah, 1)

                act.wait_ge(s.e_bd, i + 1)
                for m in range(4):
                    split_hi(m)
                    y_bias(i, m)
                act.wait_ge(s.e_bg, i + 1)
                act.wait_ge(s.e_y, i * 8 + 8)
                nc.scalar.activation(bdn[:], ps[:, 6, 2 * ROWS + 16:2 * ROWS + 24], ACT.Copy).then_inc(s.e_bd, 1)
                for m in range(4, 6):
                    split_hi(m)
                sigmoid(0)
                act.wait_ge(s.st_y, i * 32 + 32)
                for q in range(4):
                    y_rows(i, q)
                for q in range(3):
                    split_hi(2 * q + 6)
                    a_hi(q)
                    if q < 2:
                        split_hi(2 * q + 7)
                    sigmoid(q + 1)
                a_hi(3)
                split_hi(11)
                x_hi(i + 2)
            act.wait_ge(s.e_bd, nb + 1)
            for m in range(4):
                y_bias(nb, m)
            act.wait_ge(s.st_y, nb * 32 + 32)
            for q in range(4):
                y_rows(nb, q)

            for t in range(NT):
                act.wait_ge(s.v_sum, 4 * (t + 1))
                if t >= 2:
                    act.wait_ge(st_o[t % 2], 16 * (t // 2))
                nc.scalar.activation(ot[:, t % 2, :], x3[:, t % 2, :], ACT.Square, accum_out=ss[:, t:t + 1]).then_inc(s.a_sq3, 1)
                act.wait_ge(s.a_sq3, 2 * t + 1)
                nc.scalar.activation(rstd[:, t:t + 1], ss[:, t:t + 1], ACT.Sqrt, bias=EPS, scale=1.0 / D).then_inc(s.a_sq3, 1)

        def product(dst, a_hi, a_lo, b_hi, b_lo, first, last):
            nc.tensor.matmul(dst, a_hi, b_hi, start=first, stop=False)
            nc.tensor.matmul(dst, a_hi, b_lo, start=False, stop=False)
            return nc.tensor.matmul(dst, a_lo, b_hi, start=False, stop=last)

        @block.tensor
        def _(pe):
            pe.wait_ge(s.ld_const, 16)
            for t in range(NT):
                pe.wait_ge(s.v_xn, t + 1)
                if t >= 2:
                    pe.wait_ge(s.v_htlo, t - 1)
                    pe.wait_ge(s.a_hthi, t - 1)
                for c in range(KC):
                    m = nc.tensor.transpose(pair(2 * (t % 2))[:, c * P:(c + 1) * P], xn[:, t % 2, c * P:(c + 1) * P], ident)
                m.then_inc(s.p_ht, 1)

            def project(f):
                pe.wait_ge(s.g_wlo, f + 1)
                if f == 0:
                    pe.wait_ge(s.v_htlo, NT)
                    pe.wait_ge(s.a_hthi, NT)
                if f >= 2:
                    pe.wait_ge(s.a_ev, f - 1)
                for half in range(2):
                    tok = slice(half * 512, half * 512 + 512)
                    for c in range(KC):
                        m = product(ps[:, 4 + 2 * (f % 2) + half, :], w_hi[:, f % 2, c, :], w_lo[:, f % 2, c, :],
                                    ht_hi[:, c, tok], ht_lo[:, c, tok], c == 0, c == KC - 1)
                m.then_inc(s.p_ft, 1)

            for f in range(4):
                project(f)
            for j in range(3):
                pe.wait_ge(s.a_ev, j + 1)
                if j == 2:
                    pe.wait_ge(s.v_rm, 1)
                for half in range(2):
                    m = nc.tensor.matmul(ps[:, 2 * (j % 2) + half, :], const("swap_i"),
                                         (iqt[:, j, :] if j < 2 else ikt[:])[:, half * 512:half * 512 + 512], start=True, stop=True)
                m.then_inc(s.p_ri, 1)
            pe.wait_ge(s.a_ev, 4)
            pe.wait_ge(s.v_rm, 3)
            for t in range(NT):
                m = nc.tensor.transpose(ps[:, 0, t * IH:(t + 1) * IH], iwt[0:IH, t * P:(t + 1) * P], ident[0:IH, 0:IH])
            m.then_inc(s.p_iwt, 1)
            pe.wait_ge(s.a_iwt, 1)
            pe.wait_ge(s.v_iqlo, 1)
            for u in range(6 * IH):
                i, h = 2 + u // IH, u % IH
                w = P * (i + 1)
                if u >= 2:
                    pe.wait_ge(s.a_relu, u - 1)
                if h == 0:
                    pe.wait_ge(s.v_iqlo, 4 * (i - 1) + 1)
                for a in range(0, w, 512):
                    b = min(a + 512, w)
                    m = product(pair(2 * (u % 2))[:, a:b], iq_hi[:, i % 2, h, :], iq_lo[:, i % 2, h, :], ik_hi[:, a:b], ik_lo[:, a:b],
                                True, True)
                m.then_inc(s.p_is, 1)
            pe.wait_ge(s.v_gate, 12)
            pe.wait_ge(s.a_relu, 48)
            for c in range(NT):
                m = nc.tensor.transpose(pair(2)[:, c * P:(c + 1) * P], stack[:, c * P:(c + 1) * P], ident)
            m.then_inc(s.p_mcol, 1)
            for h in range(MH):
                m = nc.tensor.matmul(ps[:, 0, h * NT:(h + 1) * NT], const("pick", c0=h * P, c1=(h + 1) * P),
                                     mrow[0:MH, 0:NT], start=True, stop=True)
            m.then_inc(s.p_decay, 1)
            for f in range(4, NFT + 1):
                if f < NFT:
                    project(f)
                if FT_Q + 1 <= f <= FT_K + 1:
                    j = f - 1 - FT_Q
                    pe.wait_ge(s.a_ev, f)
                    if j == 0:
                        pe.wait_ge(s.v_mcol, 1)
                        pe.wait_ge(s.a_decay, 1)
                    if j >= 2:
                        pe.wait_ge(s.a_rq, j - 1)
                    for half in range(2):
                        m = nc.tensor.matmul(ps[:, 2 * (j % 2) + half, :], const("swap_q"),
                                             (qt[:, j, :] if j < 4 else kt[:])[:, half * 512:half * 512 + 512], start=True, stop=True)
                    m.then_inc(s.p_rq, 1)
                if f == FT_V + 1 or FT_MV + 1 <= f <= FT_MO:
                    j = 0 if f == FT_V + 1 else f - FT_MV
                    pe.wait_ge(s.a_ev, f)
                    pe.wait_ge(s.a_rq, 5)
                    if j >= 2:
                        pe.wait_ge(s.a_vt, j - 1)
                    for t in range(NT):
                        m = nc.tensor.transpose(pair(2 * ((j + 1) % 2))[:, t * P:(t + 1) * P],
                                                vtmp[:, (f - 1) % 2, t * P:(t + 1) * P], ident)
                    m.then_inc(s.p_vt, 1)

            pe.wait_ge(s.a_silu, 8)
            pe.wait_ge(s.a_ev, NFT)
            pe.wait_ge(s.a_vt, 5)

            def pair_of_heads(h, bank):
                o_ = (h % 2) * (MD + 1)
                return ps[:, bank + h // 2, o_:o_ + MD + 1]

            def m_chunk(c):
                tok, mt = slice(c * P, (c + 1) * P), slice(4 + c * P, 4 + (c + 1) * P)
                if c >= 1:
                    pe.wait_ge(s.a_s1, c)
                for h in range(MH):
                    nc.tensor.transpose(ps[:, 0, h * P:(h + 1) * P], mqk[:, 4 + h, mt], ident)
                for h in range(MH):
                    nc.tensor.matmul(ps[:, 1, h * P:(h + 1) * P], mqk[:, 4 + h, mt], mqk[:, h, mt], start=True, stop=True)
                for h in range(MH):
                    nc.tensor.matmul(ps[:, 2, h * P:(h + 1) * P], const("pick", c0=h * P, c1=(h + 1) * P), row_t[0:MH, tok],
                                     start=True, stop=False)
                    m = nc.tensor.matmul(ps[:, 2, h * P:(h + 1) * P], ident, const("future"), start=False, stop=True)
                m.then_inc(s.p_s1, 1)

            m_chunk(0)
            for c in range(NT + 2):
                if c < NT:
                    mt = slice(4 + c * P, 4 + (c + 1) * P)
                    pe.wait_ge(s.g_w, c + 1)
                    if c >= 1:
                        pe.wait_ge(s.a_up, c)
                    for h in range(MH):
                        m = nc.tensor.matmul(pair_of_heads(h, 3), m_w[:, h, :], mvtok[:, c, h, :], start=True, stop=True)
                    m.then_inc(s.p_nd, 1)
                if c >= 2:
                    pe.wait_ge(s.a_hn, c - 1)
                    if c >= 3:
                        pe.wait_ge(s.a_mt, c - 2)
                    for h in range(MH):
                        m = nc.tensor.transpose(ps[:, 7, h * P:(h + 1) * P], m_hn[:, h, :], ident)
                    m.then_inc(s.p_m3, 1)
                if c + 1 < NT:
                    m_chunk(c + 1)
                if c < NT:
                    pe.wait_ge(s.g_st, c + 1)
                    if c >= 1:
                        pe.wait_ge(s.a_in, c)
                    for h in range(MH):
                        m = nc.tensor.matmul(pair_of_heads(h, 5), mqk[:, h, mt], state[:, h, :], start=True, stop=True)
                    m.then_inc(s.p_in, 1)
                    pe.wait_ge(s.a_nd, c + 1)
                    for h in range(MH):
                        m = nc.tensor.matmul(pair_of_heads(h, 3), m_kw[:, c % 2, h, :], mvtok[:, c, h, :], start=True, stop=True)
                    m.then_inc(s.p_up, 1)

            def scores(u):
                i, h = u // HEADS, u % HEADS
                w = P * (i + 1)
                if u >= 2:
                    pe.wait_ge(s.v_msk, u - 1)
                if h == 0:
                    pe.wait_ge(s.v_qklo, 2 * (i + 1) + 1)
                for a in range(0, w, 512):
                    b = min(a + 512, w)
                    m = product(pair(2 * (u % 2))[:, a:b], q_hi[:, i % 2, h, :], q_lo[:, i % 2, h, :], k_hi[:, a:b], k_lo[:, a:b],
                                True, True)
                m.then_inc(s.p_s, 1)

            def transposes(u):
                pe.wait_ge(s.a_exp, u + 1)
                if u >= 1:
                    pe.wait_ge(s.a_pt, u)
                for j in range(u // HEADS + 1):
                    m = nc.tensor.transpose(pair(4)[:, j * P:(j + 1) * P], a_p[:, u % 2, j * P:(j + 1) * P], ident)
                m.then_inc(s.p_pt, 1)

            def values(u):
                i, h = u // HEADS, u % HEADS
                pe.wait_ge(s.a_pt, u + 1)
                if h == 0 and i >= 1:
                    pe.wait_ge(s.v_arow, i)
                for j in range(i + 1):
                    m = nc.tensor.matmul(ps[:, 6, h * HD:(h + 1) * HD], a_t[:, u % 2, j, :],
                                         vtok[:, j, HD * (h // 4):HD * (h // 4) + HD], start=(j == 0), stop=(j == i))
                m.then_inc(s.p_pv, 1)

            def rows_out(i):
                pe.wait_ge(s.v_arow, i + 1)
                if i >= 1:
                    pe.wait_ge(s.a_at, i)
                for j in range(4):
                    m = nc.tensor.transpose(ps[:, 7, j * P:(j + 1) * P], arow[:, i % 2, j * P:(j + 1) * P], ident)
                m.then_inc(s.p_at, 1)

            pe.wait_ge(s.a_mt, NT)
            scores(0)
            scores(1)
            for u in range(NT * HEADS + 1):
                if u < NT * HEADS:
                    transposes(u)
                if u >= 1:
                    values(u - 1)
                if u + 2 < NT * HEADS:
                    scores(u + 2)
                if u % HEADS == 3 and u > HEADS:
                    rows_out(u // HEADS - 1)
            rows_out(NT - 1)

            pe.wait_ge(s.a_at, NT)
            pe.wait_ge(s.g_wolo, KC)
            def out_proj(t):
                pe.wait_ge(s.v_mxlo, t + 1)
                if t >= 2:
                    pe.wait_ge(s.v_x2, t - 1)
                for half in range(2):
                    for c in range(KC):
                        cs = slice(half * 512, half * 512 + 512)
                        m = product(ps[:, 2 * (t % 2) + half, :], mx_hi[:, t % 2, c, :], mx_lo[:, t % 2, c, :],
                                    wo_hi[:, c, cs], wo_lo[:, c, cs], c == 0, c == KC - 1)
                m.then_inc(s.p_out, 1)

            def router(t):
                pe.wait_ge(s.v_h2, t + 1)
                if t >= 1:
                    pe.wait_ge(s.a_h2t, t)
                for c in range(KC):
                    m = nc.tensor.transpose(pair(4)[:, c * P:(c + 1) * P], h2[:, t % 2, c * P:(c + 1) * P], ident)
                m.then_inc(s.p_h2t, 1)
                pe.wait_ge(s.a_h2t, t + 1)
                if t >= 1:
                    pe.wait_ge(s.v_lg, 3 * t)
                else:
                    pe.wait_ge(s.ld_rw, 32)
                for c in range(KC):
                    m = nc.tensor.matmul(ps[:, 6, 0:E], h2t[:, t % 2, c, :], rw[:, c, :], start=(c == 0), stop=(c == KC - 1))
                m.then_inc(s.p_lg, 1)

            for t in range(NT + 1):
                if t < NT:
                    out_proj(t)
                if t >= 1:
                    router(t - 1)
            pe.wait_ge(s.v_dest, 5)
            for t in range(NT):
                for j in range(t + 1):
                    nc.tensor.matmul(ps[:, 7, t * E:(t + 1) * E], const("before") if j == t else const("ones"), chosen[:, j, :],
                                     start=(j == 0), stop=(j == t))
            for j in range(NT):
                m = nc.tensor.matmul(ps[:, 0, 0:E], const("ones"), chosen[:, j, :], start=(j == 0), stop=(j == NT - 1))
            m.then_inc(s.p_rank, 1)

            pe.wait_ge(s.v_dest, DEST_STEPS)
            nb = pe.value_load(nbi[0:1, 0:1], min_val=1, max_val=NBMAX)

            def x_transposes():
                for k in range(KC):
                    for h in range(2):
                        o_ = (k % 3) * ROWS + h * HALF
                        nc.tensor.transpose(ps[:, 4 + k // 3, o_:o_ + HALF], xg[0:HALF, h, k * P:(k + 1) * P], ident[0:HALF, 0:HALF])
                return nc.tensor.transpose(ps[:, 6, 2 * ROWS:2 * ROWS + 24], brow[0:24, :], ident[0:24, 0:24])

            def y_transposes():
                for q in range(4):
                    h, dq = q // 2, (q % 2) * 4
                    for d in range(4):
                        m = nc.tensor.transpose(ps[0:HALF, 4 + q, d * P:(d + 1) * P], yt[:, dq + d, h * HALF:(h + 1) * HALF], ident)
                    m.then_inc(s.p_yt, 1)

            pe.wait_ge(s.ld_xg, 32)
            pe.wait_ge(s.ld_b, 32)
            x_transposes().then_inc(s.p_xt, 1)
            pe.sem_inc(s.p_pc, 4)
            pe.wait_ge(s.p_pc, 4)
            with pe.Fori(0, nb) as i:
                def split_product(dst, m, g, k, moving, first, last):
                    nc.tensor.matmul(dst[:, 0:2 * ROWS], piece(e_whi, m)[:, k, g, :], moving[:, k, :, :].rearrange("p s n -> p (s n)"),
                                     start=first, stop=False, skip_group_check=True)
                    return nc.tensor.matmul(dst[:, 0:ROWS], piece(e_wlo, m)[:, k, g, :], moving[:, k, 0, :], start=False, stop=last,
                                            skip_group_check=True)

                def split(m):
                    pe.wait_ge(s.e_lo, i * PIECES + (m + 7))
                    pe.wait_ge(s.e_lop, i * PIECES + (m + 7))

                for f in range(8):
                    split(f)
                    if f == 0:
                        pe.wait_ge(s.e_xl, i * 2 + 2)
                    if f < 2:
                        pe.wait_ge(s.e_yd, i * 4 + (f + 3))
                    else:
                        pe.wait_ge(s.e_ev, i * 8 + (f - 1))
                    for g in range(2):
                        for k in range(KC):
                            m_ = split_product(ps[:, 2 * (f % 2) + g, :], f, g, k, e_x, k == 0, k == KC - 1)
                    m_.then_inc(s.p_pc, 1)
                    if f == 1:
                        pe.wait_ge(s.e_bd, i + 2)
                        pe.wait_ge(s.e_yr, i * 4 + 1)
                        y_transposes()
                pe.wait_ge(s.ld_xg, i * 32 + 64)
                pe.wait_ge(s.ld_b, i * 32 + 64)
                pe.wait_ge(s.e_yr, i * 4 + 5)
                x_transposes().then_inc(s.p_xt, 1)
                for j in range(4):
                    split(8 + j)
                    if j < 2:
                        pe.wait_ge(s.e_ev, i * 8 + (j + 7))
                    else:
                        pe.wait_ge(s.e_yd, i * 4 + (j + 3))
                    for part, ks in enumerate((range(0, 6), range(6, 8))):
                        if j == 0:
                            pe.wait_ge(s.e_al, i * 4 + (4 + part))
                        for g in range(2):
                            for k in ks:
                                m_ = split_product(ps[:, 2 * (j % 2) + g, :], 8 + j, g, k, e_a, k == 0, k == KC - 1)
                    m_.then_inc(s.p_pc, 1)
            pe.wait_ge(s.e_y, nb * 8 + 8)
            pe.wait_ge(s.e_bg, nb + 1)
            pe.wait_ge(s.e_yr, nb * 4 + 1)
            y_transposes()

        @block.vector
        def _(dve):
            dve.wait_ge(s.ld_const, 16)
            dve.wait_ge(s.ld_wn, 16)

            def ht_lo_of(t):
                dve.wait_ge(s.a_hthi, t + 1)
                lo = ht_lo[:, :, t * P:(t + 1) * P]
                nc.vector.tensor_tensor(lo, pair(2 * (t % 2)).rearrange("p (c n) -> p c n", c=KC),
                                        ht_hi[:, :, t * P:(t + 1) * P].bitcast(F32), ALU.subtract).then_inc(s.v_htlo, 1)

            for t in range(NT):
                dve.wait_ge(s.a_root, t + 1)
                nc.vector.reciprocal(rinv[:, t:t + 1], rstd[:, t:t + 1]).then_inc(s.v_rcp, 1)
                dve.wait_ge(s.v_rcp, t + 1)
                nc.vector.scalar_tensor_tensor(out=xn[:, t % 2, :], in0=xt[:, t % 2, :], scalar=rinv[:, t:t + 1],
                                               in1=wnb[:], op0=ALU.mult, op1=ALU.mult).then_inc(s.v_xn, 1)
                if t >= 1:
                    ht_lo_of(t - 1)
            ht_lo_of(NT - 1)

            dve.wait_ge(s.ld_rope, 16)
            for j in range(3):
                ft = iqt[:, j, :] if j < 2 else ikt[:]
                dve.wait_ge(s.p_ri, j + 1)
                if j >= 1:
                    dve.wait_ge(s.v_ra, j)
                nc.vector.tensor_tensor(rtmp[:], pair(2 * (j % 2)), rope_i[:, 1, :], ALU.mult).then_inc(s.v_rm, 1)
                nc.vector.tensor_tensor(ft, ft, rope_i[:, 0, :], ALU.mult).then_inc(s.v_rc, 1)
                dve.wait_ge(s.v_rm, j + 1)
                dve.wait_ge(s.v_rc, j + 1)
                nc.vector.tensor_tensor(ft, ft, rtmp[:], ALU.add).then_inc(s.v_ra, 1)

            dve.wait_ge(s.a_iqhi, 1)
            nc.vector.tensor_tensor(ik_lo[:], ikt[:], ik_hi[:].bitcast(F32), ALU.subtract).then_inc(s.v_iqlo, 1)

            def iq_lo_of(i):
                for g in range(4):
                    rows = slice(ID * g, ID * g + ID)
                    dve.wait_ge(s.a_iqhi, 4 * (i - 2) + g + 2)
                    nc.vector.tensor_tensor(iq_lo[rows, i % 2, g::4, :], iqt[rows, :, i * P:(i + 1) * P],
                                            iq_hi[rows, i % 2, g::4, :].bitcast(F32), ALU.subtract).then_inc(s.v_iqlo, 1)

            iq_lo_of(2)
            gate = Steps(dve, s.v_gate)
            heads = slice(0, MH)

            def chunks(a):
                return a.rearrange("p (c n) -> p c n", c=NT)

            dve.wait_ge(s.a_gate, 5)
            dve.wait_ge(s.ld_gate, 48)
            dve.wait_ge(s.g_stack, 1)
            gate(nc.vector.scalar_tensor_tensor(out=row_f[heads, :], in0=row_f[heads, :], scalar=0.0,
                                                in1=row_t[heads, :], op0=ALU.min, op1=ALU.subtract))
            gate.done()
            gate(nc.vector.tensor_tensor_scan(row_b[heads, :], carry[heads, :], row_f[heads, :], 0.0, ALU.mult, ALU.add))
            gate(nc.vector.tensor_tensor_scan(mrow[heads, :], row_f[heads, :], row_i[heads, :], 0.0, ALU.add, ALU.max))
            gate.done()
            gate(nc.vector.tensor_tensor(stack[0:MH, :], row_i[heads, :], row_b[heads, :], ALU.subtract))
            gate(nc.vector.tensor_tensor(row_t[heads, :], row_b[heads, :], mrow[heads, :], ALU.subtract))
            gate(nc.vector.tensor_scalar(stack[96:96 + MH, :], mrow[heads, :], -1.0, None, ALU.mult))
            gate.done()
            gate(nc.vector.memset(row_b[heads, 0:1], 0.0))
            gate.done()
            gate(nc.vector.tensor_copy(row_b[heads, 1:NT], chunks(mrow[heads, :])[:, 0:NT - 1, P - 1]))
            gate.done()
            gate(nc.vector.tensor_tensor(chunks(stack[32:32 + MH, :]), chunks(row_t[heads, :]),
                                         row_b[heads, 0:NT].unsqueeze(2).to_broadcast([MH, NT, P]), ALU.add))
            gate(nc.vector.tensor_tensor(chunks(stack[64:64 + MH, :]), chunks(stack[0:MH, :]),
                                         chunks(row_t[heads, :])[:, :, P - 1:P].to_broadcast([MH, NT, P]), ALU.add))
            gate(nc.vector.tensor_tensor(mrow[heads, 0:NT], row_b[heads, 0:NT], chunks(row_t[heads, :])[:, :, P - 1], ALU.add))
            gate(nc.vector.memset(top8, 0.0))
            assert gate.n == 12

            dve.wait_ge(s.a_iwt, 1)
            for i in range(2, NT):
                sc = score[:, score_at[i]:score_at[i] + P * (i + 1)]
                for h in range(IH):
                    u = (i - 2) * IH + h
                    if h == 4 and i + 1 < NT:
                        iq_lo_of(i + 1)
                    dve.wait_ge(s.a_relu, u + 1)
                    r = rbuf[:, u % 2, 0:P * (i + 1)]
                    if h == 0:
                        nc.vector.tensor_scalar(sc, r, iwc[:, i, 0:1], None, ALU.mult).then_inc(s.v_score, 1)
                    else:
                        dve.wait_ge(s.v_score, 9 * (i - 2) + h)
                        nc.vector.scalar_tensor_tensor(out=sc, in0=r, scalar=iwc[:, i, h:h + 1], in1=sc,
                                                       op0=ALU.mult, op1=ALU.add).then_inc(s.v_score, 1)
                dve.wait_ge(s.v_score, 9 * (i - 2) + 8)
                nc.vector.tensor_tensor(sc[:, i * P:(i + 1) * P], sc[:, i * P:(i + 1) * P], const("unseen"),
                                        ALU.add).then_inc(s.v_score, 1)
            dve.wait_ge(s.p_mcol, 1)
            nc.vector.tensor_copy(mcol, pair(2).rearrange("p (c k n) -> p c k n", c=NT, k=4)[:, :, :, 0:MH]).then_inc(s.v_mcol, 1)

            dve.wait_ge(s.v_score, 54)
            n = 0
            for i in range(2, NT, 2):
                sc = [score[:, score_at[j]:score_at[j] + P * (j + 1)] for j in (i, i + 1)]
                for it in range(TOPK // 8):
                    for k in range(2):
                        if n:
                            dve.wait_ge(s.v_topk, n - 1)
                        nc.vector.max(top8[:, k, :], sc[k]).then_inc(s.v_topk, 1)
                        n += 1
                    for k in range(2):
                        dve.wait_ge(s.v_topk, n - 1)
                        nc.vector.match_replace(sc[k], top8[:, k, :], sc[k], GONE).then_inc(s.v_topk, 1)
                        n += 1
                for k in range(2):
                    dve.wait_ge(s.v_topk, n - 1 + k)
                    nc.vector.tensor_scalar(sc[k], sc[k], GONE / 2, NEG, ALU.is_gt, ALU.mult).then_inc(s.v_mask, 1)
            def normalize(i):
                dve.wait_ge(s.a_exp, HEADS * (i + 1))
                if i >= 1:
                    dve.wait_ge(s.v_arow, i)
                nc.vector.reciprocal(rsi, rs[:, (i % 2) * 8:(i % 2) * 8 + 8]).then_inc(s.v_rs, 1)
                dve.wait_ge(s.v_rs, i + 1)
                dve.wait_ge(s.p_pv, HEADS * (i + 1))
                if i >= 2:
                    dve.wait_ge(s.p_at, i - 1)
                nc.vector.tensor_tensor(arow[:, i % 2, :].rearrange("p (h n) -> p h n", h=HEADS),
                                        ps[:, 6, :].rearrange("p (h n) -> p h n", h=HEADS),
                                        rsi.unsqueeze(2).to_broadcast([P, HEADS, HD]), ALU.mult).then_inc(s.v_arow, 1)

            dve.wait_ge(s.a_qkhi, 1)
            nc.vector.tensor_tensor(k_lo[:], kt[:], k_hi[:].bitcast(F32), ALU.subtract).then_inc(s.v_qklo, 1)

            def q_lo_of(i):
                for g in range(KVH):
                    rows = slice(HD * g, HD * g + HD)
                    dve.wait_ge(s.a_qkhi, 2 * i + g + 2)
                    nc.vector.tensor_tensor(q_lo[rows, i % 2, 4 * g:4 * g + 4, :], qt[rows, :, i * P:(i + 1) * P],
                                            q_hi[rows, i % 2, 4 * g:4 * g + 4, :].bitcast(F32), ALU.subtract).then_inc(s.v_qklo, 1)

            q_lo_of(0)

            for u in range(NT * HEADS):
                i, h = u // HEADS, u % HEADS
                w = P * (i + 1)
                dve.wait_ge(s.p_s, u + 1)
                if u >= 2:
                    dve.wait_ge(s.a_exp, u - 1)
                src, dst = pair(2 * (u % 2))[:, 0:w], a_s[:, u % 2, 0:w]
                if i >= 2:
                    dve.wait_ge(s.v_mask, i - 1)
                    nc.vector.tensor_tensor_reduce(dst, src, score[:, score_at[i]:score_at[i] + w], 1.0, GONE,
                                                   ALU.add, ALU.max, mx[:, u % 2:u % 2 + 1]).then_inc(s.v_msk, 1)
                else:
                    nc.vector.tensor_tensor_reduce(dst, src, seen[:, P - P * i:2 * P], 1.0, GONE,
                                                   ALU.add, ALU.max, mx[:, u % 2:u % 2 + 1]).then_inc(s.v_msk, 1)
                dve.wait_ge(s.v_msk, u + 1)
                nc.vector.tensor_scalar(nmx[:, u % 2:u % 2 + 1], mx[:, u % 2:u % 2 + 1], -HD ** -0.5, None, ALU.mult).then_inc(s.v_nm, 1)
                if h == 2 and i >= 1:
                    normalize(i - 1)
                if h == 6 and i + 1 < NT:
                    q_lo_of(i + 1)
            normalize(NT - 1)

            def x2_of(t):
                dve.wait_ge(s.p_out, t + 1)
                dve.wait_ge(ld_x[t % 2], 16 * (NT // 2 + t // 2 + 1))
                if t >= 2:
                    dve.wait_ge(st_x[t % 2], 16 * (t // 2))
                    dve.wait_ge(s.v_h2, t - 1)
                nc.vector.tensor_tensor(x2[:, t % 2, :], pair(2 * (t % 2)), xr[:, t % 2, :], ALU.add).then_inc(s.v_x2, 1)

            def h2_of(t):
                dve.wait_ge(s.a_root, NT + t + 1)
                nc.vector.reciprocal(rinv[:, t:t + 1], rstd[:, t:t + 1]).then_inc(s.v_rcp, 1)
                dve.wait_ge(s.v_rcp, NT + t + 1)
                nc.vector.scalar_tensor_tensor(out=h2[:, t % 2, :], in0=x2[:, t % 2, :], scalar=rinv[:, t:t + 1],
                                               in1=wn2[:], op0=ALU.mult, op1=ALU.mult).then_inc(s.v_h2, 1)

            def route(t):
                dve.wait_ge(s.p_lg, t + 1)
                nc.vector.tensor_tensor(lg, ps[:, 6, 0:E], rb[:], ALU.add).then_inc(s.v_lg, 1)
                dve.wait_ge(s.v_lg, 3 * t + 1)
                nc.vector.max(best[:, t, :], lg).then_inc(s.v_lg, 1)
                dve.wait_ge(s.v_lg, 3 * t + 2)
                nc.vector.max_index(besti[:, t, :], best[:, t, :], lg).then_inc(s.v_lg, 1)
                dve.wait_ge(s.v_lg, 3 * t + 3)

            dve.wait_ge(s.ld_wn, 32)
            dve.wait_ge(s.ld_rw, 32)
            for t in range(NT + 1):
                if t < NT:
                    dve.wait_ge(s.a_mxhi, t + 1)
                    nc.vector.tensor_tensor(mx_lo[:, t % 2, :, :], mixt[:, :, t * P:(t + 1) * P], mx_hi[:, t % 2, :, :].bitcast(F32),
                                            ALU.subtract).then_inc(s.v_mxlo, 1)
                if t >= 1:
                    x2_of(t - 1)
                    h2_of(t - 1)
                    route(t - 1)
            r = Steps(dve, s.v_route)
            r(nc.vector.tensor_tensor(gates, best[:, :, 0:TOP], best[:, :, 0:1].to_broadcast([P, NT, TOP]), ALU.subtract))
            r(nc.vector.tensor_copy(bestf, besti))
            r.done()
            for k in range(TOP):
                m_ = nc.vector.tensor_tensor(oneh[:, k], const("experts").unsqueeze(1).to_broadcast([P, NT, E]),
                                             bestf[:, :, k:k + 1].to_broadcast([P, NT, E]), ALU.is_equal)
                if k == TOP - 1:
                    r(m_)
                else:
                    m_.then_inc(s.v_dest, 1)
            d = Steps(dve, s.v_dest)
            d.n = TOP - 1
            r.done()
            r(nc.vector.tensor_tensor(chosen[:], oneh[:, 0], oneh[:, 1], ALU.add))
            d(nc.vector.tensor_tensor(prod[:], oneh[:, 2], oneh[:, 3], ALU.add))
            r.done()
            d.done()
            d(nc.vector.tensor_tensor(chosen[:], chosen[:], prod[:], ALU.add))
            d.done()
            dve.wait_ge(s.a_gexp, 1)
            d(nc.vector.tensor_reduce(gsum, gates, AX.X, ALU.add))
            d.done()
            d(nc.vector.reciprocal(gsum, gsum))
            d.done()
            d(nc.vector.tensor_tensor(gates, gates, gsum.unsqueeze(2).to_broadcast([P, NT, TOP]), ALU.mult))
            dve.wait_ge(s.p_rank, 1)
            d(nc.vector.tensor_copy(counts, ps[:, 0, 0:E]))
            d.done()
            d(nc.vector.tensor_tensor(stepc[:], counts.unsqueeze(2).to_broadcast([P, E, CAPT]),
                                      const("steps").unsqueeze(1).to_broadcast([P, E, CAPT]), ALU.is_gt))
            d.done()
            d(nc.vector.tensor_reduce(nblk, stepc[:], AX.X, ALU.add))
            d.done()
            d(nc.vector.tensor_tensor_scan(bend, const("ones", c1=E), nblk, 0.0, ALU.mult, ALU.add))
            d.done()
            d(nc.vector.tensor_tensor(bstart, bend, nblk, ALU.subtract))
            d(nc.vector.tensor_scalar(counts, bend, const("row"), None, ALU.is_le))
            d(nc.vector.tensor_copy(nbi, bend[:, E - 1:E]))
            d.done()
            d(nc.vector.tensor_reduce(bef, counts, AX.X, ALU.add))
            d(nc.vector.tensor_scalar(bstart, bstart, float(ROWS), None, ALU.mult))
            d.done()
            d(nc.vector.tensor_scalar(bei, bef, float(E - 1), None, ALU.min))
            d(nc.vector.tensor_tensor(place[:], ps[:, 7, 0:NT * E].rearrange("p (t e) -> p t e", t=NT),
                                      bstart.unsqueeze(1).to_broadcast([P, NT, E]), ALU.add))
            for k in range(TOP):
                d.done()
                d(nc.vector.tensor_tensor(prod[:], oneh[:, k], place[:], ALU.mult))
                d.done()
                d(nc.vector.tensor_reduce(destf[:, :, k], prod[:], AX.X, ALU.add))
            d.done()
            d(nc.vector.tensor_copy(desti, destf))
            assert d.n == DEST_STEPS, d.n
            d.done()

            nb = dve.value_load(nbi[0:1, 0:1], min_val=1, max_val=NBMAX)

            def x_lo(n):
                dve.wait_ge(s.e_xh, 2 * n)
                nc.vector.tensor_tensor(e_x[:, 0:6, 1, :].rearrange("p (b k) n -> p b k n", b=2),
                                        ps[:, 4:6, 0:3 * ROWS].rearrange("p b (k n) -> p b k n", k=3),
                                        e_x[:, 0:6, 0, :].rearrange("p (b k) n -> p b k n", b=2).bitcast(F32), ALU.subtract).then_inc(s.e_xl, 1)
                nc.vector.tensor_tensor(e_x[:, 6:8, 1, :], ps[:, 6, 0:2 * ROWS].rearrange("p (k n) -> p k n", k=2),
                                        e_x[:, 6:8, 0, :].bitcast(F32), ALU.subtract).then_inc(s.e_xl, 1)
                nc.vector.tensor_copy(bgu[:], ps[:, 6, 2 * ROWS:2 * ROWS + 16]).then_inc(s.e_bg, 1)

            def gather_rows(n):
                dve.wait_ge(s.ld_idx, n * 16)
                nc.vector.tensor_scalar(gidx[0:HALF, :], idx[0:HALF, :], TOP.bit_length() - 1, None, ALU.logical_shift_right).then_inc(s.e_gx, 1)

            def y_sums(i, m):
                dve.wait_ge(s.p_pc, i * PIECES + (m + 1))
                nc.vector.tensor_reduce(yt[:, 2 * m:2 * m + 2, :], sums_of(m), AX.X, ALU.add).then_inc(s.e_yd, 1)

            dve.wait_ge(s.ld_scur, 16)
            nc.vector.memset(bdn[:], 0.0).then_inc(s.e_bd, 1)
            dve.sem_inc(s.e_lo, 6)
            dve.sem_inc(s.e_al, 1)
            dve.sem_inc(s.e_ix, 1)
            dve.wait_ge(s.e_lo, 6)
            dve.wait_ge(s.e_al, 1)
            dve.wait_ge(s.e_ix, 1)
            gather_rows(1)
            x_lo(1)
            with dve.Fori(0, nb) as i:
                def split_lo(m):
                    dve.wait_ge(s.e_hi, i * PIECES + (m + 1))
                    ks = slice(0, KDVE)
                    nc.vector.tensor_tensor(piece(e_wlo, m)[:, ks], raw_piece(m)[:, ks], piece(e_whi, m)[:, ks].bitcast(F32),
                                            ALU.subtract).then_inc(s.e_lo, 1)

                def evacuate_gu(f):
                    dve.wait_ge(s.p_pc, i * PIECES + (f + 5))
                    nc.vector.tensor_reduce(esum[:, f % 2], sums_of(f), AX.X, ALU.add).then_inc(s.e_ev, 1)
                    dve.wait_ge(s.e_ev, i * 8 + (f + 1))
                    for g, dst in enumerate((gl, ul)):
                        nc.vector.tensor_scalar(dst[:, f // 2 % 2, f % 2, :], esum[:, f % 2, g, :], bgu[:, 8 * g + f:8 * g + f + 1],
                                                LIMIT, ALU.add, ALU.min).then_inc(s.e_mn, 1)

                def act_of(q):
                    dve.wait_ge(s.e_mn, i * 16 + 4 * (q + 1))
                    nc.vector.tensor_scalar(ul[:, q % 2], ul[:, q % 2], -LIMIT, 1.0, ALU.max, ALU.add).then_inc(s.e_cl, 1)
                    dve.wait_ge(s.e_cl, i * 4 + (q + 1))
                    nc.vector.tensor_tensor(tt[:, q % 2], ul[:, q % 2], gl[:, q % 2], ALU.mult).then_inc(s.e_t, 1)
                    dve.wait_ge(s.e_t, i * 4 + (q + 1))
                    dve.wait_ge(s.e_sg, i * 4 + (q + 1))
                    dve.wait_ge(s.e_al, i * 4 + max(q, 1))
                    nc.vector.tensor_tensor(af[:, q % 2], tt[:, q % 2], sg[:, q % 2], ALU.mult).then_inc(s.e_act, 1)

                def a_lo(q):
                    dve.wait_ge(s.e_ah, i * 4 + (q + 1))
                    nc.vector.tensor_tensor(e_a[:, 2 * q:2 * q + 2, 1, :], af[:, q % 2], e_a[:, 2 * q:2 * q + 2, 0, :].bitcast(F32),
                                            ALU.subtract).then_inc(s.e_al, 1)

                for m in range(4):
                    y_sums(i, m)
                    split_lo(m)
                dve.wait_ge(s.st_y, i * 32 + 32)
                dve.wait_ge(s.e_ix, i * 2 + 1)
                nc.vector.tensor_copy(slast[0:HALF, :], scur[0:HALF, :]).then_inc(s.e_ix, 1)
                dve.wait_ge(s.ld_idx, i * 16 + 16)
                dve.wait_ge(s.e_ix, i * 2 + 2)
                nc.vector.tensor_copy(scur[0:HALF, :], idx[0:HALF, :]).then_inc(s.e_ix, 1)
                dve.wait_ge(s.e_bg, i + 1)
                for q in range(4):
                    evacuate_gu(2 * q)
                    if q:
                        a_lo(q - 1)
                    split_lo(2 * q + 4)
                    evacuate_gu(2 * q + 1)
                    if q < 3:
                        split_lo(2 * q + 5)
                    act_of(q)
                    if q == 0:
                        dve.wait_ge(s.ld_xg, i * 32 + 32)
                        gather_rows(i + 2)
                a_lo(3)
                split_lo(11)
                x_lo(i + 2)
            for m in range(4):
                y_sums(nb, m)

            dve.wait_ge(s.ld_wn, 48)
            for t in range(NT):
                dve.wait_ge(ld_y[t % 2], 16 * (t // 2 + 1))
                dve.wait_ge(ld_x[t % 2], 16 * (NT + t // 2 + 1))
                for k in range(TOP):
                    if k:
                        dve.wait_ge(s.v_sum, 4 * t + k)
                    nc.vector.scalar_tensor_tensor(out=x3[:, t % 2, :], in0=yg[:, t % 2, k, :], scalar=gates[:, t, k:k + 1],
                                                   in1=x3[:, t % 2, :], op0=ALU.mult, op1=ALU.add).then_inc(s.v_sum, 1)
                dve.wait_ge(s.a_sq3, 2 * t + 2)
                nc.vector.reciprocal(rinv[:, t:t + 1], rstd[:, t:t + 1]).then_inc(s.v_rcp, 1)
                dve.wait_ge(s.v_rcp, 2 * NT + t + 1)
                nc.vector.scalar_tensor_tensor(out=ot[:, t % 2, :], in0=x3[:, t % 2, :], scalar=rinv[:, t:t + 1],
                                               in1=wn3[:], op0=ALU.mult, op1=ALU.mult).then_inc(s.v_o, 1)
        bctx.close()


_INS = ['x', 'mix_norm_w', 'w_in', 'conv_w', 'conv_b', 'igate_b', 'fgate_b', 'mlstm_norm_w', 'w_out', 'ffn_norm_w',
        'router_w', 'router_b', 'w_gate_up', 'b_gate_up', 'w_down', 'b_down', 'final_norm_w']


def kernel(**inputs):
    import numpy as _np
    import concourse.bacc as _bacc
    from concourse import mybir as _mybir
    from concourse.bass_utils import run_bass_kernel_spmd as _run

    nc = _bacc.Bacc("TRN2", target_bir_lowering=False, num_devices=1)
    held = {name: _np.ascontiguousarray(inputs[name]) for name in _INS}
    held["c_const"], held["c_carry"], held["c_slots"] = CONST_ARRAY, CARRY, unused_slots()
    held["c_rope_q"], held["c_rope_i"] = rope_tables(HD, HD // 4), rope_tables(ID, ID // 4)
    arrays = {f"in_{name}_dram": a for name, a in held.items()}
    I = {name: nc.dram_tensor(f"in_{name}_dram", a.shape, _mybir.dt.from_np(a.dtype), kind="ExternalInput").ap()
         for name, a in held.items()}
    out = nc.dram_tensor("out_0_dram", (1, T, D), F32, kind="ExternalOutput").ap()
    build(nc, I, out)
    r = _run(nc, [arrays], core_ids=[0])
    return r.results[0]["out_0_dram"]
```
